# Optimizing a Trainium2 kernel written in Bass

```python
import jax, jax.numpy as jnp
from jax import lax
import numpy as np

D_MODEL = 2048
BATCH = 1
SEQ = 256
DEPTH = 1

MIX_WIDTH = D_MODEL
FOURIER_WIDTH = MIX_WIDTH // 2
N_FOURIER_GROUPS = 4
FOURIER_GROUP_DIM = FOURIER_WIDTH // N_FOURIER_GROUPS
ATTN_WIDTH = MIX_WIDTH - FOURIER_WIDTH
HEAD_DIM = 128
N_HEADS = ATTN_WIDTH // HEAD_DIM
WINDOW_DILATIONS = ((128, 1), (512, 4), (2048, 16))
D_FF = 4 * D_MODEL
IN_WIDTH = FOURIER_WIDTH + 3 * ATTN_WIDTH
RMS_EPS = 1e-6


def _rmsnorm(x, g):
    xf = x.astype(jnp.float32)
    inv = lax.rsqrt(jnp.mean(xf * xf, axis=-1, keepdims=True) + RMS_EPS)
    return (xf * inv * g.astype(jnp.float32)).astype(x.dtype)

def _alibi_slopes(n_heads):
    return jnp.asarray(2.0 ** (-8.0 * (np.arange(n_heads) + 1) / n_heads), dtype=jnp.float32)

def _dilated_branch(q, k, v, slopes, dilation, radius):
    B, H, S, Dh = q.shape
    M = S // dilation
    blk = radius
    nb = -(-M // blk)
    Mp = nb * blk

    def to_classes(t):
        return t.reshape(B, H, M, dilation, Dh).transpose(0, 1, 3, 2, 4)

    pad0 = ((0, 0), (0, 0), (0, 0))
    qc = jnp.pad(to_classes(q), pad0 + ((0, Mp - M), (0, 0))).reshape(B, H, dilation, nb, blk, Dh)
    kc = jnp.pad(to_classes(k), pad0 + ((blk, Mp - M + blk), (0, 0))).reshape(B, H, dilation, nb + 2, blk, Dh)
    vc = jnp.pad(to_classes(v), pad0 + ((blk, Mp - M + blk), (0, 0))).reshape(B, H, dilation, nb + 2, blk, Dh)
    kw = jnp.concatenate([kc[:, :, :, :-2], kc[:, :, :, 1:-1], kc[:, :, :, 2:]], axis=4)
    vw = jnp.concatenate([vc[:, :, :, :-2], vc[:, :, :, 1:-1], vc[:, :, :, 2:]], axis=4)

    mq = jnp.arange(nb)[:, None, None] * blk + jnp.arange(blk)[None, :, None]
    mk = jnp.arange(nb)[:, None, None] * blk - blk + jnp.arange(3 * blk)[None, None, :]
    rel = mk - mq
    valid = (jnp.abs(rel) <= radius) & (mk >= 0) & (mk < M)
    dist = (dilation * jnp.abs(rel)).astype(jnp.float32)

    s = jnp.einsum('bhrnqd,bhrnkd->bhrnqk', qc, kw).astype(jnp.float32)
    s = s - slopes[None, :, None, None, None, None] * dist
    s = jnp.where(valid, s, -jnp.inf)
    mx = jnp.max(s, axis=-1, keepdims=True)
    p = jnp.exp(s - mx)
    den = jnp.sum(p, axis=-1)
    o = jnp.einsum('bhrnqk,bhrnkd->bhrnqd', p.astype(v.dtype), vw).astype(jnp.float32) / den[..., None]

    def from_classes(t):
        tail = t.shape[5:]
        t = t.reshape((B, H, dilation, Mp) + tail)[:, :, :, :M]
        t = jnp.moveaxis(t, 2, 3)
        return t.reshape((B, H, S) + tail)

    return from_classes(o), from_classes(mx[..., 0]), from_classes(den)

def _dilated_attention(q, k, v):
    slopes = _alibi_slopes(q.shape[1])
    outs, maxes, dens = [], [], []
    for window, dil in WINDOW_DILATIONS:
        o, m, d = _dilated_branch(q, k, v, slopes, dil, (window // 2) // dil)
        outs.append(o); maxes.append(m); dens.append(d)
    mx = jnp.stack(maxes)
    w = jnp.stack(dens) * jnp.exp(mx - jnp.max(mx, axis=0, keepdims=True))
    o = jnp.sum(w[..., None] * jnp.stack(outs), axis=0) / jnp.sum(w, axis=0)[..., None]
    return o

def _fourier_mix(u, w_f):
    B, S, _ = u.shape
    ug = u.reshape(B, S, N_FOURIER_GROUPS, FOURIER_GROUP_DIM).astype(jnp.float32)
    re = jnp.fft.fft2(ug, axes=(1, 3), norm="ortho").real.astype(u.dtype)
    y = jnp.einsum('bsgc,gce->bsge', re, w_f)
    return y.reshape(B, S, FOURIER_WIDTH)

def first_inputs(seed: int = 0) -> dict:
    key = jax.random.key(seed)
    ks = jax.random.split(key, 10)
    f32 = jnp.float32
    x = jax.random.normal(ks[0], (BATCH, SEQ, D_MODEL), f32)
    norm_mix_g = 1.0 + 0.02 * jax.random.normal(ks[1], (DEPTH, D_MODEL), f32)
    w_in = jax.random.normal(ks[2], (DEPTH, D_MODEL, IN_WIDTH), f32) * D_MODEL ** -0.5
    w_fourier = jax.random.normal(ks[3], (DEPTH, N_FOURIER_GROUPS, FOURIER_GROUP_DIM, FOURIER_GROUP_DIM), f32) * FOURIER_GROUP_DIM ** -0.5
    w_out = jax.random.normal(ks[4], (DEPTH, MIX_WIDTH, D_MODEL), f32) * MIX_WIDTH ** -0.5
    norm_mlp_g = 1.0 + 0.02 * jax.random.normal(ks[5], (DEPTH, D_MODEL), f32)
    w_up = jax.random.normal(ks[6], (DEPTH, D_MODEL, D_FF), f32) * D_MODEL ** -0.5
    w_down = jax.random.normal(ks[7], (DEPTH, D_FF, D_MODEL), f32) * D_FF ** -0.5
    norm_final_g = 1.0 + 0.02 * jax.random.normal(ks[8], (D_MODEL,), f32)
    return {"x": x, "norm_mix_g": norm_mix_g, "w_in": w_in, "w_fourier": w_fourier,
            "w_out": w_out, "norm_mlp_g": norm_mlp_g, "w_up": w_up, "w_down": w_down,
            "norm_final_g": norm_final_g}

def first_block(x, norm_mix_g, w_in, w_fourier, w_out, norm_mlp_g, w_up, w_down, norm_final_g):
    B, S, _ = x.shape
    h = x
    for layer in range(DEPTH):
        u = _rmsnorm(h, norm_mix_g[layer])
        proj = jnp.einsum('bsd,de->bse', u, w_in[layer])
        u_f = proj[..., :FOURIER_WIDTH]
        qkv = proj[..., FOURIER_WIDTH:].reshape(B, S, 3, N_HEADS, HEAD_DIM)
        q = jnp.transpose(qkv[:, :, 0], (0, 2, 1, 3)) * (HEAD_DIM ** -0.5)
        k = jnp.transpose(qkv[:, :, 1], (0, 2, 1, 3))
        v = jnp.transpose(qkv[:, :, 2], (0, 2, 1, 3))
        y_f = _fourier_mix(u_f, w_fourier[layer])
        y_a = _dilated_attention(q, k, v).astype(h.dtype)
        y_a = jnp.transpose(y_a, (0, 2, 1, 3)).reshape(B, S, ATTN_WIDTH)
        y = jnp.concatenate([y_f, y_a], axis=-1)
        h = h + jnp.einsum('bse,ed->bsd', y, w_out[layer])
        u = _rmsnorm(h, norm_mlp_g[layer])
        a = jnp.einsum('bsd,df->bsf', u, w_up[layer])
        a = jnp.square(jax.nn.relu(a))
        h = h + jnp.einsum('bsf,fd->bsd', a, w_down[layer])
    return _rmsnorm(h, norm_final_g)


CTX_LEN = 256
GRID_W = 64
D_MIX = D_MODEL
GLA_HEADS = 4
GLA_DK = 128
GLA_DV = 256
GLA_KW = GLA_HEADS * GLA_DK
GLA_VW = GLA_HEADS * GLA_DV
GATE_RANK = 16
GATE_NORM = 16.0
CHUNK = 64
CONV_W = D_MIX - GLA_VW
CONV_K = 3
FFN_HIDDEN = -(-8 * D_MODEL // (3 * 256)) * 256
IN_COLS = 2 * GLA_KW + 2 * GLA_VW + 2 * GATE_RANK + 3 * CONV_W
EPS = 1e-6


def rmsnorm(x, g):
    x32 = x.astype(jnp.float32)
    y = x32 * lax.rsqrt(jnp.mean(x32 * x32, axis=-1, keepdims=True) + EPS)
    return y.astype(x.dtype) * g

def modulate(h, shift, scale):
    return h * (1.0 + scale) + shift

def split_proj(p):
    sizes = [GLA_KW, GLA_KW, GLA_VW, GLA_VW, GATE_RANK, GATE_RANK, CONV_W, CONV_W, CONV_W]
    idx = np.cumsum(sizes)[:-1].tolist()
    return jnp.split(p, idx, axis=-1)

def gla_chunked(q, k, v, log_a, s0):
    b_, n, h, _ = q.shape
    dv = v.shape[-1]
    nc = n // CHUNK

    def blk(t):
        return t.reshape(b_, nc, CHUNK, h, t.shape[-1]).transpose(0, 3, 1, 2, 4)

    q, k, v, log_a = blk(q), blk(k), blk(v), blk(log_a)
    cum = jnp.cumsum(log_a, axis=3)
    last = cum[:, :, :, -1:, :]
    q_e = q * jnp.exp(cum)
    k_e = k * jnp.exp(-cum)
    tri = jnp.tril(jnp.ones((CHUNK, CHUNK), dtype=bool))
    scores = jnp.where(tri, jnp.einsum('bhnid,bhnjd->bhnij', q_e, k_e), 0.0)
    o_intra = jnp.einsum('bhnij,bhnjv->bhniv', scores, v)
    ds = jnp.einsum('bhnjd,bhnjv->bhndv', k * jnp.exp(last - cum), v)
    decay = jnp.exp(last[:, :, :, 0, :])

    def step(s, inp):
        d, u = inp
        return d[..., None] * s + u, s

    s_final, s_prev = lax.scan(step, s0, (jnp.moveaxis(decay, 2, 0), jnp.moveaxis(ds, 2, 0)))
    s_prev = jnp.moveaxis(s_prev, 0, 2)
    o = o_intra + jnp.einsum('bhnid,bhndv->bhniv', q_e, s_prev)
    return o.transpose(0, 2, 3, 1, 4).reshape(b_, n, h, dv), s_final

def gla_bidir(q, k, v, la_f, la_b, s0_f, s0_b):
    o_f, s_f = gla_chunked(q, k, v, la_f, s0_f)
    flip = lambda t: jnp.flip(t, axis=1)
    o_b, s_b = gla_chunked(flip(q), flip(k), flip(v), flip(la_b), s0_b)
    return o_f + flip(o_b), s_f, s_b

def gla_inputs(q, k, v, lf, lb, w_gf, b_gf, w_gb, b_gb):
    b_, n = q.shape[:2]
    heads = lambda t, d: t.reshape(b_, n, GLA_HEADS, d).astype(jnp.float32)
    qh = heads(q, GLA_DK) * (GLA_DK ** -0.5)
    kh = heads(k, GLA_DK)
    vh = heads(v, GLA_DV)
    la_f = heads(jax.nn.log_sigmoid((lf @ w_gf + b_gf).astype(jnp.float32)) / GATE_NORM, GLA_DK)
    la_b = heads(jax.nn.log_sigmoid((lb @ w_gb + b_gb).astype(jnp.float32)) / GATE_NORM, GLA_DK)
    return qh, kh, vh, la_f, la_b

def conv_grid(u, w):
    b_, n, ch = u.shape
    rows = n // GRID_W
    gp = jnp.pad(u.reshape(b_, rows, GRID_W, ch), ((0, 0), (0, 0), (CONV_K // 2, CONV_K // 2), (0, 0)))
    y = sum(w[j] * gp[:, :, j:j + GRID_W] for j in range(CONV_K))
    return y.reshape(b_, n, ch)

def conv_seq(u, w):
    n = u.shape[1]
    up = jnp.pad(u, ((0, 0), (CONV_K // 2, CONV_K // 2), (0, 0)))
    return sum(w[j] * up[:, j:j + n] for j in range(CONV_K))

def mix_output(o_gla, g, cb, cc, cx, conv_fn, conv_w, gla_g, w_out):
    b_, n = g.shape[:2]
    o32 = o_gla * lax.rsqrt(jnp.mean(o_gla * o_gla, axis=-1, keepdims=True) + EPS)
    o = (o32.astype(g.dtype) * gla_g).reshape(b_, n, GLA_VW) * jax.nn.silu(g)
    y_conv = cb * conv_fn(cc * cx, conv_w)
    return jnp.concatenate([o, y_conv], axis=-1) @ w_out

def swiglu(h, wg, wu, wd):
    return (jax.nn.silu(h @ wg) * (h @ wu)) @ wd

def second_inputs(seed: int = 0) -> dict:
    key = jax.random.key(seed)
    ks = jax.random.split(key, 24)
    nrm = lambda k, shape, s: jax.random.normal(k, shape, jnp.float32) * s
    D, L = D_MODEL, DEPTH
    return {
        "x": nrm(ks[0], (BATCH, SEQ, D), 1.0),
        "c": nrm(ks[1], (BATCH, D), 1.0),
        "ctx": nrm(ks[2], (BATCH, CTX_LEN, D), 1.0),
        "c_ctx": nrm(ks[3], (D,), 1.0),
        "w_mod": nrm(ks[4], (L, D, 6 * D), 0.5 * D ** -0.5),
        "b_mod": nrm(ks[5], (L, 6 * D), 0.01),
        "norm1_g": 1.0 + nrm(ks[6], (L, D), 0.05),
        "norm2_g": 1.0 + nrm(ks[7], (L, D), 0.05),
        "w_in": nrm(ks[8], (L, D, IN_COLS), D ** -0.5),
        "w_gate_f": nrm(ks[9], (L, GATE_RANK, GLA_KW), GATE_RANK ** -0.5),
        "b_gate_f": nrm(ks[10], (L, GLA_KW), 0.1),
        "w_gate_b": nrm(ks[11], (L, GATE_RANK, GLA_KW), GATE_RANK ** -0.5),
        "b_gate_b": nrm(ks[12], (L, GLA_KW), 0.1),
        "gla_norm_g": 1.0 + nrm(ks[13], (L, GLA_DV), 0.05),
        "conv_w": nrm(ks[14], (L, CONV_K, CONV_W), CONV_K ** -0.5),
        "w_out": nrm(ks[15], (L, D_MIX, D), D_MIX ** -0.5),
        "w_ffn_gate": nrm(ks[16], (L, D, FFN_HIDDEN), D ** -0.5),
        "w_ffn_up": nrm(ks[17], (L, D, FFN_HIDDEN), D ** -0.5),
        "w_ffn_down": nrm(ks[18], (L, FFN_HIDDEN, D), FFN_HIDDEN ** -0.5),
        "final_g": 1.0 + nrm(ks[19], (D,), 0.05),
    }

def second_block(x, c, ctx, c_ctx, w_mod, b_mod, norm1_g, norm2_g, w_in, w_gate_f, b_gate_f,
              w_gate_b, b_gate_b, gla_norm_g, conv_w, w_out, w_ffn_gate, w_ffn_up, w_ffn_down,
              final_g):
    b_ = x.shape[0]
    for i in range(DEPTH):
        mx = jax.nn.silu(c) @ w_mod[i] + b_mod[i]
        mc = jax.nn.silu(c_ctx) @ w_mod[i] + b_mod[i]
        sh1, sc1, gt1, sh2, sc2, gt2 = [t[:, None, :] for t in jnp.split(mx, 6, axis=-1)]
        sh1c, sc1c, gt1c, sh2c, sc2c, gt2c = jnp.split(mc, 6, axis=-1)

        hc = modulate(rmsnorm(ctx, norm1_g[i]), sh1c, sc1c)
        qc, kc, vc, gc, lfc, lbc, cbc, ccc, cxc = split_proj(hc @ w_in[i])
        qh, kh, vh, la_f, la_b = gla_inputs(qc, kc, vc, lfc, lbc, w_gate_f[i], b_gate_f[i],
                                             w_gate_b[i], b_gate_b[i])
        s0 = jnp.zeros((b_, GLA_HEADS, GLA_DK, GLA_DV), jnp.float32)
        o_c, s_f, s_b = gla_bidir(qh, kh, vh, la_f, la_b, s0, s0)

        hx = modulate(rmsnorm(x, norm1_g[i]), sh1, sc1)
        q, k, v, g, lf, lb, cb, cc, cx = split_proj(hx @ w_in[i])
        qh, kh, vh, la_f, la_b = gla_inputs(q, k, v, lf, lb, w_gate_f[i], b_gate_f[i],
                                             w_gate_b[i], b_gate_b[i])
        o_x, _, _ = gla_bidir(qh, kh, vh, la_f, la_b, s_f, s_b)
        mix = mix_output(o_x, g, cb, cc, cx, conv_grid, conv_w[i], gla_norm_g[i], w_out[i])
        x_next = x + gt1 * mix
        h2 = modulate(rmsnorm(x_next, norm2_g[i]), sh2, sc2)
        x_next = x_next + gt2 * swiglu(h2, w_ffn_gate[i], w_ffn_up[i], w_ffn_down[i])

        if i < DEPTH - 1:
            mix_c = mix_output(o_c, gc, cbc, ccc, cxc, conv_seq, conv_w[i], gla_norm_g[i], w_out[i])
            ctx = ctx + gt1c * mix_c
            h2c = modulate(rmsnorm(ctx, norm2_g[i]), sh2c, sc2c)
            ctx = ctx + gt2c * swiglu(h2c, w_ffn_gate[i], w_ffn_up[i], w_ffn_down[i])
        x = x_next
    return rmsnorm(x, final_g)


def setup_inputs(seed=0):
    out = dict(first_inputs(seed))
    for name, value in second_inputs(seed + 1).items():
        if name != "x":
            out[name + "_2"] = value
    return out


def reference(
    x, norm_mix_g, w_in, w_fourier, w_out, norm_mlp_g, w_up, w_down, norm_final_g, c_2, ctx_2,
    c_ctx_2, w_mod_2, b_mod_2, norm1_g_2, norm2_g_2, w_in_2, w_gate_f_2, b_gate_f_2, w_gate_b_2,
    b_gate_b_2, gla_norm_g_2, conv_w_2, w_out_2, w_ffn_gate_2, w_ffn_up_2, w_ffn_down_2,
    final_g_2,
):
    x = first_block(
        x, norm_mix_g, w_in, w_fourier, w_out, norm_mlp_g, w_up, w_down, norm_final_g,
    )
    return second_block(
        x, c_2, ctx_2, c_ctx_2, w_mod_2, b_mod_2, norm1_g_2, norm2_g_2, w_in_2, w_gate_f_2,
        b_gate_f_2, w_gate_b_2, b_gate_b_2, gla_norm_g_2, conv_w_2, w_out_2, w_ffn_gate_2,
        w_ffn_up_2, w_ffn_down_2, final_g_2,
    )


_drawn_inputs = setup_inputs


def setup_inputs(seed=0):
    import zlib

    import numpy as np

    out = dict(_drawn_inputs(seed))
    spreads = {}
    factors = {'norm_mix_g': 4.424,
     'norm_mlp_g': 2.937,
     'c_ctx_2': 3.682,
     'b_mod_2': 3.763,
     'norm2_g_2': 4.145,
     'w_gate_f_2': 3.295,
     'b_gate_f_2': 8.0,
     'b_gate_b_2': 8.0,
     'gla_norm_g_2': 7.705}
    for name, (base, spread) in spreads.items():
        noise = np.random.default_rng([zlib.crc32(name.encode()), seed]).standard_normal(out[name].shape)
        drawn = base * np.exp(spread * noise) if base else spread * noise
        out[name] = __import__('jax').numpy.asarray(drawn.astype(out[name].dtype))
    for name, factor in factors.items():
        out[name] = (out[name] * factor).astype(out[name].dtype)
    return out
```

```python
from contextlib import ExitStack, contextmanager

import numpy as np

import concourse.bass as bass
from concourse import mybir

P = 128
F32 = mybir.dt.float32
F32R = mybir.dt.float32r
U32 = mybir.dt.uint32
ACT = mybir.ActivationFunctionType
ALU = mybir.AluOpType
AX_X = mybir.AxisListType.X

D = 2048
S = 256
T = S // P
KT = D // P
NB = 512
KG = 4
EPS = 1e-6

FGROUPS, FDIM = 4, 256
HEADS, HD = 8, 128
MLP_CHUNKS = 4

GH, DK, DV = 4, 128, 256
CH = 64
NCH = S // CH
RANK2 = 32
OFF_Q, OFF_K, OFF_V, OFF_G, OFF_L, OFF_CB, OFF_CC, OFF_CX = 0, 512, 1024, 2048, 3072, 3104, 4128, 5152
FFN_BLOCKS = 11
GRID = 64

WSLOTS = 4
HSLOTS = 2
MSLOTS = 2
MSTEPS = 8
STATE_STEPS = (8, 6)
H0 = 2
SH1, SC1, GT1, SH2, SC2, GT2 = range(6)

V_MIXG, V_MLPG, V_N1G, V_N2G, V_C, V_CCTX = range(0, 96, 16)


class Counts:

    def __init__(self, **start):
        self.n = dict(start)
        self.i, self.per = None, {}

    def at(self, name, off=0):
        v = self.n.get(name, 0) + off
        if self.i is not None and self.per.get(name, 0):
            return self.i * self.per[name] + v
        return v

    def landed(self, name, slots):
        v = 16 * (self.n.get(name, 0) // slots + 1)
        if self.i is not None and self.per.get(name, 0):
            return self.i * (self.per[name] // slots * 16) + v
        return v

    def slot(self, name, slots):
        assert self.i is None or self.per.get(name, 0) % slots == 0, name
        return self.n.get(name, 0) % slots

    def add(self, name, k=1):
        self.n[name] = self.n.get(name, 0) + k

    @contextmanager
    def loop(self, eng, trips, **per):
        before = {k: self.n.get(k, 0) for k in per}
        with eng.Fori(0, trips) as i:
            self.i, self.per = i, per
            yield i
            self.i, self.per = None, {}
        for k, v in per.items():
            assert self.n.get(k, 0) - before[k] == v, (k, self.n.get(k, 0) - before[k], v)
            self.n[k] += v * (trips - 1)


def two_blocks(nc, x, ctx_in, w_in, w_fourier, w_out, w_up, w_down, w_mod, w_in2, w_out2, w_gate,
               w_up2, w_down2, vectors, gates_w, mid_g, final_g, tables, fourier_tables, attn_tables, out):
    ctx = ExitStack()
    with ctx:
        def sb(name, shape, dt=F32, scope=ctx):
            return scope.enter_context(nc.sbuf_tensor(name, shape, dt))

        def sem(name):
            return ctx.enter_context(nc.semaphore(name))

        wring = sb("wring", [P, WSLOTS, KG * NB])
        whi = sb("whi", [P, HSLOTS, KG * NB], F32R)
        wlo = sb("wlo", [P, HSLOTS, KG * NB], F32R)
        mring = sb("mring", [P, MSLOTS, 2, NB])
        macc = sb("macc", [P, 2, NB])
        h = sb("h", [P, T, D])
        xhi = sb("xhi", [P, KT, S], F32R)
        xlo = sb("xlo", [P, KT, S], F32R)
        tabs = sb("tabs", [P, 7, P])
        ident = tabs[:, 0, :]
        tri = [tabs[:, 1, :], tabs[:, 2, :]]
        after = [tabs[:, 3, :], tabs[:, 4, :]]
        keep = [tabs[:, 5, :].bitcast(U32), tabs[:, 6, :].bitcast(U32)]
        ones = sb("ones", [P, 1])
        vrows = sb("vrows", [P, 3, P])
        vecs = sb("vecs", [P, 3, P])
        csil = sb("csil", [P, 2, KT])
        modT = sb("modT", [P, 2, 6 * KT])
        gain1 = sb("gain1", [P, 2, KT])
        gain2 = sb("gain2", [P, KT])
        ssq = sb("ssq", [P, 7, T])
        rstd = sb("rstd", [P, 7, T])
        blk = sb("blk", [P, T, NB])
        blk2 = sb("blk2", [P, T, NB])
        tmpT = sb("tmpT", [P, 2, NB])

        with ExitStack() as ph:
            tab_f = sb("tab_f", [P, 2, 3 * S], scope=ph)
            tab_a = sb("tab_a", [P, 2, T * S], scope=ph)
            proj = sb("proj", [P, T, 8 * NB], scope=ph)
            wf = sb("wf", [P, FGROUPS, 2, FDIM], scope=ph)
            qkT = sb("qkT", [P, 2, 2, S], scope=ph)
            nmax = sb("nmax", [P, HEADS, T], scope=ph)
            aden = sb("aden", [P, HEADS, T], scope=ph)
            arden = sb("arden", [P, HEADS, T], scope=ph)
        u_mix = proj[:, :, 0:D]
        fpos = blk
        fre = tmpT[:, 0, :].rearrange("p (c s) -> p c s", c=2)
        probsT = tmpT[:, 1, :].rearrange("p (c s) -> p c s", c=2)
        sbias = blk2[:, 0, :]
        probs = blk2[:, 1, :]
        with ExitStack() as ph:
            ahi = sb("ahi", [P, KT, S], F32R, scope=ph)
            alo = sb("alo", [P, KT, S], F32R, scope=ph)
            u_mlp = sb("u_mlp", [P, T, D], scope=ph)
            mgain = sb("mgain", [P, D], scope=ph)
        with ExitStack() as ph:
            states = sb("states", [P, 2, GH, DV], scope=ph)
            wg = sb("wg", [P, 2, GH * DK], scope=ph)
            gk = sb("gk", [P, T, GH * DK], scope=ph)
            gv = sb("gv", [P, T, GH * DV], scope=ph)
            gq = sb("gq", [P, T, GH * DK], scope=ph)
            lrank = sb("lrank", [P, T, P], scope=ph)
            lrankT = sb("lrankT", [P, S], scope=ph)
            epos = sb("epos", [P, 2, S], scope=ph)
            gbig = sb("gbig", [P, 2 * D], scope=ph)
            silg = sb("silg", [P, T, GH * DV], scope=ph)
            oss = sb("oss", [P, T, GH], scope=ph)
            orstd = sb("orstd", [P, T, GH], scope=ph)
        u_g = gbig[:, :].rearrange("p (t d) -> p t d", t=T)
        la = gbig[:, 0:D].rearrange("p (t d c) -> p t d c", t=T, d=2)
        kdec = gbig[:, D:2 * D].rearrange("p (t d c) -> p t d c", t=T, d=2)
        convT = gbig[:, D:2 * D].rearrange("p (c s) -> p c s", c=8)
        gst = h[:, 0, :].rearrange("p (d c v) -> p d c v", d=2, c=NCH)
        o_all = h[:, 1, :].rearrange("p (t c) -> p t c", t=T)
        eneg = tmpT[:, 0, :].rearrange("p (d s) -> p d s", d=2)
        qe = blk[:, 0, :].rearrange("p (d s) -> p d s", d=2)
        ke = blk[:, 1, :].rearrange("p (d s) -> p d s", d=2)
        sc = blk2[:, 0, :].rearrange("p (d t s) -> p d t s", d=2, t=T)
        with ExitStack() as ph:
            with ExitStack() as sub:
                u_ffn = sb("u_ffn", [P, T, D], scope=sub)
            bhi = sb("bhi", [P, KT, S], F32R, scope=ph)
            blo = sb("blo", [P, KT, S], F32R, scope=ph)
            gates = sb("gates", [P, 2, D], scope=ph)
            fgain = sb("fgain", [P, D], scope=ph)

        acc = ctx.enter_context(nc.psum_tensor("acc", [P, 2 * T, NB], F32))
        tp = ctx.enter_context(nc.psum_tensor("tp", [P, 2, NB], F32))
        m0 = ctx.enter_context(nc.psum_tensor("m0", [P, NB], F32))
        m1 = ctx.enter_context(nc.psum_tensor("m1", [P, NB], F32))
        hspill = nc.dram_tensor("hspill", [T, P, D], F32).ap()

        group_landed = [sem(f"group_landed{i}") for i in range(WSLOTS)]
        hi_done = sem("hi_done")
        lo_done = sem("lo_done")
        group_multiplied = sem("group_multiplied")
        tp_ready = sem("tp_ready")
        tp_hi = sem("tp_hi")
        tp_tmp = sem("tp_tmp")
        tp_free = sem("tp_free")
        step_landed = [sem(f"step_landed{i}") for i in range(MSLOTS)]
        mod_acc = sem("mod_acc")
        mod_reduced = sem("mod_reduced")
        mod_set = sem("mod_set")
        start_in = sem("start_in")
        x_in = sem("x_in")
        misc_in = sem("misc_in")
        ctx_in_s = sem("ctx_in_s")
        wg_in = sem("wg_in")
        spill_s = sem("spill_s")
        reload_s = sem("reload_s")
        fg_in = sem("fg_in")
        mg_in = sem("mg_in")
        out_s = sem("out_s")
        pool_set = sem("pool_set")
        vec_turned = sem("vec_turned")
        vec_set = sem("vec_set")
        c_exp = sem("c_exp")
        c_sil = sem("c_sil")
        ssq_done = sem("ssq_done")
        mean_done = sem("mean_done")
        root_done = sem("root_done")
        rstd_done = sem("rstd_done")
        u_done = sem("u_done")
        blk_ready = sem("blk_ready")
        blk_half = sem("blk_half")
        h_added = sem("h_added")
        h_scaled = sem("h_scaled")
        proj_set = sem("proj_set")
        f1_done, f1_copied, f2_done, f2_copied, f3_done, f3_hi, f3_lo = (
            sem(n) for n in ("f1_done", "f1_copied", "f2_done", "f2_copied", "f3_done", "f3_hi", "f3_lo"))
        qk_turned, qk_copied, scores_done, scores_biased, max_set, exps_done = (
            sem(n) for n in ("qk_turned", "qk_copied", "scores_done", "scores_biased", "max_set", "exps_done"))
        probs_summed, den_inverted, probs_ready, probs_turned, probsT_copied, pv_done, pv_hi, pv_lo = (
            sem(n) for n in ("probs_summed", "den_inverted", "probs_ready", "probs_turned",
                             "probsT_copied", "pv_done", "pv_hi", "pv_lo"))
        gain_set = sem("gain_set")
        in_set = sem("in_set")
        lr_turned, lr_copied, z_done, la_step, la_ready, sfx_done, kdec_exp, kdec_ready = (
            sem(n) for n in ("lr_turned", "lr_copied", "z_done", "la_step", "la_ready", "sfx_done",
                             "kdec_exp", "kdec_ready"))
        cum_done, cum_exp, gqk_turned, qe_done, gsc_done, gsc_kept, ds_done, state_step, o_done, o_copied = (
            sem(n) for n in ("cum_done", "cum_exp", "gqk_turned", "qe_done", "gsc_done", "gsc_kept",
                             "ds_done", "state_step", "o_done", "o_copied"))
        sc_zeroed = sem("sc_zeroed")
        conv_step, conv_hi, conv_lo = sem("conv_step"), sem("conv_hi"), sem("conv_lo")
        o_mean, o_root, o_rstd, o_gated = sem("o_mean"), sem("o_root"), sem("o_rstd"), sem("o_gated")
        final_set = sem("final_set")

        C_IN = ("l", "k", "v0", "v1")
        X_IN = ("l", "k", "v0", "v1", "q", "cc0", "cx0", "cb0", "cc1", "cx1", "cb1", "g0", "g1")
        COLS = {"l": OFF_L, "k": OFF_K, "v0": OFF_V, "v1": OFF_V + NB, "q": OFF_Q,
                "cc0": OFF_CC, "cc1": OFF_CC + NB, "cx0": OFF_CX, "cx1": OFF_CX + NB,
                "cb0": OFF_CB, "cb1": OFF_CB + NB, "g0": OFF_G, "g1": OFF_G + NB}
        SPREAD = (2, 1, 1, 1, 1, 1, 1, 0)
        DENSE = (3, 3, 2, 0)
        CHUNKS = (4, 4, 3)
        IN_SET, stored = ({}, {}), 0
        for names, values in zip((C_IN, X_IN), IN_SET):
            for name in names:
                if name[:2] != "cx":
                    stored += 1
                    values[name] = stored
        T_O = 8 + 8 + 8 * MLP_CHUNKS + 8 + 8 + 8 + GH
        H_MLP = H0 + 4 + 4 * MLP_CHUNKS
        H_ALL = H_MLP + 4 + 4 * len(CHUNKS)
        block = ctx.enter_context(nc.Block())

        @block.sync
        def _(sp):
            c = Counts()

            def load(src, kts=KG, width=NB):
                sp.wait_ge(lo_done, c.at("g", 1))
                dst = wring[:, c.slot("g", WSLOTS), 0:kts * width].rearrange("p (k n) -> p k n", k=kts)
                sp.dma_start(dst, src).then_inc(group_landed[c.slot("g", WSLOTS)], 16)
                c.add("g")

            def block_of(w, col, kgroups=KT // KG, kg0=0):
                v = w.rearrange("(g k p) n -> g p k n", k=KG, p=P)
                for kg in range(kgroups):
                    if isinstance(kg0, int):
                        load(v[kg0 + kg, :, :, bass.ds(col, NB)])
                    else:
                        load(v[bass.ds(kg0 + kg, 1), :, :, bass.ds(col, NB)].rearrange("a p k n -> (a p) k n"))

            with c.loop(sp, 4, g=8) as i:
                for j in range(2):
                    block_of(w_in, i * (2 * NB) + j * NB)
            with c.loop(sp, 2, g=8) as i:
                for j in range(2):
                    block_of(w_out, i * (2 * NB) + j * NB)
            with c.loop(sp, MLP_CHUNKS, g=32) as i:
                for j in range(4):
                    block_of(w_up, i * D + j * NB)
                for n in range(4):
                    block_of(w_down, n * NB, kg0=i * 4)
            for names in (C_IN, X_IN):
                for name in names:
                    if name == "l":
                        v = w_in2.rearrange("(g k p) n -> g p k n", k=8, p=P)
                        for half in range(2):
                            load(v[half, :, :, OFF_L:OFF_L + RANK2], 8, RANK2)
                    else:
                        block_of(w_in2, COLS[name])
            with c.loop(sp, 2, g=8) as i:
                for j in range(2):
                    block_of(w_out2, i * (2 * NB) + j * NB)

            def ffn(i, blocks):
                for j in range(blocks):
                    block_of(w_gate, i * D + j * NB)
                    block_of(w_up2, i * D + j * NB)
                for n in range(4):
                    block_of(w_down2, n * NB, kgroups=blocks, kg0=i * 4)

            with c.loop(sp, 2, g=48) as i:
                ffn(i, 4)
            ffn(2, 3)

        @block.gpsimd
        def _(pool):
            c = Counts()
            pool.memset(ones[:, :], 1.0).then_inc(pool_set, 1)
            pool.dma_start(tab_f[:, :, :], fourier_tables).then_inc(misc_in, 16)
            pool.dma_start(tab_a[:, :, :], attn_tables).then_inc(misc_in, 16)
            for g in range(FGROUPS):
                pool.dma_start(wf[:, g, :, :], w_fourier[g].rearrange("(c p) e -> p c e", p=P)).then_inc(misc_in, 16)
            w_mod_v = w_mod.rearrange("(s k p) n -> s p k n", k=2, p=P)

            def mod_block(kind, i, per_step, last_step):
                for s in range(MSTEPS):
                    pool.wait_ge(mod_acc, c.at("ma", 8 - (last_step if s == 0 else per_step)))
                    pool.dma_start(mring[:, c.slot("m", MSLOTS), :, :],
                                   w_mod_v[s, :, :, bass.ds(i * NB + kind * D, NB)])\
                        .then_inc(step_landed[c.slot("m", MSLOTS)], 16)
                    c.add("m")
                    c.add("ma", per_step)

            with c.loop(pool, 4, m=8, ma=32) as i:
                mod_block(SH1, i, 4, 4)
            pool.wait_ge(tp_free, 2 + 16)
            pool.dma_start(u_g[:, :, :], ctx_in.rearrange("(t p) d -> p t d", p=P)).then_inc(ctx_in_s, 16)
            pool.dma_start(mgain[:, :], mid_g.rearrange("(a n) -> a n", a=1).partition_broadcast(P)).then_inc(mg_in, 16)
            with c.loop(pool, MLP_CHUNKS, m=24, ma=64) as i:
                mod_block(SC1, i, 4, 2)
                mod_block(GT1, i, 2, 4)
                mod_block(SH2, i, 2, 2)
            pool.wait_ge(h_added, H_MLP)
            pool.dma_start(wg[:, :, :], gates_w).then_inc(wg_in, 16)
            pool.memset(lrank[:, :, :], 0.0).then_inc(pool_set, 1)
            pool.wait_ge(pool_set, 2)
            pool.memset(lrank[:, :, RANK2:RANK2 + 1], 1.0).then_inc(pool_set, 1)
            pool.wait_ge(u_done, 4 * T)
            pool.dma_start(hspill.rearrange("t p d -> p t d"), h[:, :, :]).then_inc(spill_s, 16)
            with c.loop(pool, 4, m=8, ma=16) as i:
                mod_block(SC2, i, 2, 2)
            with c.loop(pool, 4, m=8, ma=16) as i:
                mod_block(GT2, i, 2, 2)
            pool.wait_ge(tp_ready, T_O)
            pool.wait_ge(spill_s, 16)
            pool.dma_start(h[:, :, :], hspill.rearrange("t p d -> p t d")).then_inc(reload_s, 16)
            pool.dma_start(fgain[:, :], final_g.rearrange("(a n) -> a n", a=1).partition_broadcast(P))\
                .then_inc(fg_in, 16)

        @block.scalar
        def _(act):
            c = Counts()

            def round_groups(n, size=KG * NB):
                for _ in range(n):
                    g4, g2 = c.slot("g", WSLOTS), c.slot("g", HSLOTS)
                    act.wait_ge(group_landed[g4], c.landed("g", WSLOTS))
                    act.wait_ge(group_multiplied, c.at("g", 1))
                    act.activation(whi[:, g2, 0:size], wring[:, g4, 0:size], ACT.Copy).then_inc(hi_done, 1)
                    c.add("g")

            def wait_block(back):
                act.wait_ge(group_multiplied, c.at("g", HSLOTS - back))

            def round_banks(dst, tile, banks, gain=None):
                for b in range(banks):
                    src = tp[:, c.slot("q", 2), :].rearrange("p (j s) -> p j s", j=2)
                    act.wait_ge(tp_ready, c.at("q", 1))
                    t0 = tile + 2 * b
                    if gain is None:
                        act.activation(dst[:, t0:t0 + 2, :], src, ACT.Copy).then_inc(tp_hi, 1)
                    else:
                        act.activation(dst[:, t0, :], src[:, 0, :], ACT.Copy, scale=gain(t0)).then_inc(tp_hi, 1)
                        act.activation(dst[:, t0 + 1, :], src[:, 1, :], ACT.Copy, scale=gain(t0 + 1)).then_inc(tp_hi, 1)
                    c.add("q")

            def round_modulated(dst):
                for b in range(KT // 2):
                    act.wait_ge(tp_tmp, c.at("tmp", 1))
                    act.activation(dst[:, 2 * b:2 * b + 2, :],
                                   tmpT[:, b % 2, :].rearrange("p (j s) -> p j s", j=2), ACT.Copy).then_inc(tp_hi, 1)
                    c.add("tmp")
                    c.add("q")

            def norm_stats(n, src, junk=None):
                for t in range(T):
                    if t:
                        act.wait_ge(ssq_done, c.at("ssq"))
                    act.activation(acc[:, :, :].rearrange("p a n -> p (a n)") if junk is None else junk, src[:, t, :], ACT.Square,
                                   accum_out=ssq[:, n, t:t + 1]).then_inc(ssq_done, 1)
                    c.add("ssq")
                act.wait_ge(mean_done, n + 1)
                act.activation(ssq[:, n, :], ssq[:, n, :], ACT.Sqrt).then_inc(root_done, 1)

            act.dma_start(h[:, 0, :], x[0:P, :]).then_inc(x_in, 16)
            act.dma_start(h[:, 1, :], x[P:2 * P, :]).then_inc(x_in, 16)
            act.dma_start(vrows[:, :, :], vectors).then_inc(start_in, 16)
            act.dma_start(tabs[:, :, :], tables).then_inc(start_in, 16)
            act.sem_inc(proj_set, 2)
            act.wait_ge(x_in, 32)
            norm_stats(0, h)
            act.wait_ge(vec_set, 1)
            act.activation(csil[:, :, :].rearrange("p w k -> p (w k)"), vecs[:, 0, V_C:V_C + 2 * KT],
                           ACT.Exp, scale=-1.0).then_inc(c_exp, 1)
            round_banks(xhi, 0, 8, lambda k: vecs[:, 0, V_MIXG + k:V_MIXG + k + 1])

            with c.loop(act, 4, g=8) as i:
                for j in range(2):
                    round_groups(2)
                    if j:
                        wait_block(2)
                        act.activation(proj[:, :, bass.ds(i * (2 * NB), NB)], acc[:, 0:2, :], ACT.Copy).then_inc(proj_set, 1)
                    round_groups(2)
                wait_block(0)
                act.activation(proj[:, :, bass.ds(i * (2 * NB) + NB, NB)], acc[:, 2:4, :], ACT.Copy).then_inc(proj_set, 1)

            act.wait_ge(misc_in, 16 * 6)
            for s in range(HEADS + 1):
                g = s // 2
                if s < HEADS:
                    act.wait_ge(qk_turned, s + 1)
                    if s >= 2:
                        act.wait_ge(scores_done, s - 1)
                    act.activation(qkT[:, s % 2, 0, :], tp[:, 0, 0:S], ACT.Copy, scale=HD ** -0.5).then_inc(qk_copied, 1)
                    act.activation(qkT[:, s % 2, 1, :], tp[:, 0, S:2 * S], ACT.Copy).then_inc(qk_copied, 1)
                if s < HEADS and s % 2 == 0:
                    act.wait_ge(f1_done, g + 1)
                    if g:
                        act.wait_ge(f2_done, g)
                    act.activation(fpos[:, :, :], acc[:, 0:2, :], ACT.Copy).then_inc(f1_copied, 1)
                if s % 2:
                    act.wait_ge(f2_done, g + 1)
                    if g:
                        act.wait_ge(f3_done, g)
                    act.activation(fre, m0[:, :].rearrange("p (c s) -> p c s", c=2), ACT.Copy).then_inc(f2_copied, 1)
                if s:
                    act.wait_ge(probs_turned, s)
                    if s >= 2:
                        act.wait_ge(pv_done, s - 1)
                    act.activation(probsT, tp[:, 1, :].rearrange("p (c s) -> p c s", c=2), ACT.Copy).then_inc(probsT_copied, 1)
                if s < HEADS:
                    act.wait_ge(max_set, s + 1)
                    for t in range(T):
                        act.activation(probs[:, t * S:(t + 1) * S], sbias[:, t * S:(t + 1) * S], ACT.Exp,
                                       bias=nmax[:, s, t:t + 1]).then_inc(exps_done, 1)
                if s % 2:
                    act.wait_ge(f3_done, g + 1)
                    act.activation(xhi[:, 2 * g:2 * g + 2, :], m1[:, :].rearrange("p (c s) -> p c s", c=2),
                                   ACT.Copy).then_inc(f3_hi, 1)
                if s:
                    act.wait_ge(pv_done, s)
                    act.activation(xhi[:, 7 + s, :], acc[:, 3, 0:S], ACT.Copy).then_inc(pv_hi, 1)

            with c.loop(act, 2, g=8):
                round_groups(8)
            act.wait_ge(h_added, H0 + 4)
            norm_stats(1, h)
            round_banks(xhi, 0, 8, lambda k: vecs[:, 0, V_MLPG + k:V_MLPG + k + 1])

            def relu_square(j):
                act.activation(blk2[:, :, :], acc[:, 2 * (j % 2):2 * (j % 2) + 2, :], ACT.Relu).then_inc(blk_half, 1)
                c.add("half")
                act.wait_ge(blk_half, c.at("half"))
                act.activation(blk[:, :, :], blk2[:, :, :], ACT.Square).then_inc(blk_ready, 1)
                c.add("blk")

            with c.loop(act, MLP_CHUNKS, g=32, q=8, half=4, blk=4):
                for j in range(8):
                    round_groups(2)
                    if 1 <= j <= 4:
                        wait_block(2)
                        relu_square(j - 1)
                    round_groups(2)
                    if 1 <= j <= 4:
                        round_banks(ahi, 4 * (j - 1), 2)

            def store_block(name, pair, x_pass):
                src = acc[:, 2 * pair:2 * pair + 2, :]
                if name == "l":
                    act.wait_ge(pool_set, 3)
                    act.activation(lrank[:, :, 0:RANK2], src[:, :, 0:RANK2], ACT.Copy).then_inc(in_set, 1)
                elif name == "k":
                    act.activation(gk[:, :, :], src, ACT.Copy).then_inc(in_set, 1)
                elif name in ("v0", "v1"):
                    o = NB * int(name[1])
                    act.activation(gv[:, :, o:o + NB], src, ACT.Copy).then_inc(in_set, 1)
                elif name == "q":
                    act.activation(gq[:, :, :], src, ACT.Copy).then_inc(in_set, 1)
                elif name in ("cc0", "cc1"):
                    if name == "cc1":
                        act.wait_ge(tp_ready, 8 + 8 + 8 * MLP_CHUNKS + 8 + 8 + 4)
                    act.activation(blk[:, :, :], src, ACT.Copy).then_inc(in_set, 1)
                elif name in ("cb0", "cb1"):
                    act.activation(blk2[:, :, :], src, ACT.Copy).then_inc(in_set, 1)
                elif name in ("g0", "g1"):
                    o = NB * int(name[1])
                    act.activation(silg[:, :, o:o + NB], src, ACT.Silu).then_inc(in_set, 1)

            def in_blocks(names, b0, x_pass):
                for n, name in enumerate(names):
                    wide = name != "l"
                    parts = (2, 2) if wide else (2, 0)
                    round_groups(parts[0], KG * NB if wide else 8 * RANK2)
                    if n:
                        wait_block(2)
                        store_block(names[n - 1], (b0 + n - 1) % 2, x_pass)
                    if not x_pass and name == "k":
                        norm_stats(3, h, u_g[:, 1, :])
                    round_groups(parts[1])
                wait_block(0)
                store_block(names[-1], (b0 + len(names) - 1) % 2, x_pass)

            def gla(p):
                act.wait_ge(lr_turned, p + 1)
                act.activation(lrankT[:, :], m0[:, 0:S], ACT.Copy).then_inc(lr_copied, 1)
                n0 = 6 * p
                for t in range(T):
                    act.wait_ge(z_done, T * p + t + 1)
                    act.activation(la[:, t], acc[:, 2 * t:2 * t + 2, :], ACT.Abs).then_inc(la_step, 1)
                for t in range(T):
                    act.wait_ge(la_step, n0 + t + 1)
                    act.activation(la[:, t], la[:, t], ACT.Exp, scale=-1.0).then_inc(la_step, 1)
                for t in range(T):
                    act.wait_ge(la_step, n0 + 2 + t + 1)
                    act.activation(la[:, t], la[:, t], ACT.Ln, bias=1.0).then_inc(la_step, 1)
                if p:
                    act.wait_ge(conv_lo, 1)
                for t in range(T):
                    act.wait_ge(sfx_done, T * p + t + 1)
                    act.activation(kdec[:, t], acc[:, 2 * t:2 * t + 2, :], ACT.Exp).then_inc(kdec_exp, 1)
                for hd in range(GH):
                    n = GH * p + hd
                    act.wait_ge(cum_done, n + 1)
                    if hd:
                        act.wait_ge(state_step, STATE_STEPS[p] * hd + (STATE_STEPS[0] * GH if p else 0))
                    act.activation(epos[:, :, :], m0[:, :].rearrange("p (d s) -> p d s", d=2), ACT.Exp).then_inc(cum_exp, 1)
                    if p:
                        if hd:
                            act.wait_ge(qe_done, 4 * hd)
                        act.activation(eneg, m0[:, :].rearrange("p (d s) -> p d s", d=2), ACT.Exp, scale=-1.0).then_inc(cum_exp, 1)
                        act.wait_ge(o_done, hd + 1)
                        for t in range(T):
                            act.activation(o_all[:, t, hd * DV:(hd + 1) * DV], tp[:, 1, t * DV:(t + 1) * DV], ACT.Copy).then_inc(o_copied, 1)
                            act.activation(tmpT[:, 1, t * DV:(t + 1) * DV], tp[:, 1, t * DV:(t + 1) * DV], ACT.Square,
                                           accum_out=oss[:, t, hd:hd + 1]).then_inc(o_copied, 1)

            act.wait_ge(ctx_in_s, 16)
            act.wait_ge(h_added, H_MLP)
            norm_stats(2, u_g)
            round_modulated(xhi)
            in_blocks(C_IN, 44, False)
            gla(0)
            act.wait_ge(state_step, STATE_STEPS[0] * GH)
            norm_stats(4, h)
            round_modulated(xhi)
            in_blocks(X_IN, 48, True)
            c.add("q", 8)
            act.wait_ge(conv_step, 8 * 4)
            act.activation(xhi[:, 8:16, :], convT, ACT.Copy).then_inc(conv_hi, 1)
            act.wait_ge(spill_s, 16)
            gla(1)
            act.wait_ge(o_mean, 1)
            act.activation(oss[:, :, :], oss[:, :, :], ACT.Sqrt).then_inc(o_root, 1)
            round_banks(xhi, 0, 4, lambda k: vecs[:, 2, 24 + k % 2:25 + k % 2])

            c.add("q", 8)
            with c.loop(act, 2, g=8):
                round_groups(8)
            act.wait_ge(h_added, H_MLP + 4)
            norm_stats(5, h)
            round_modulated(xhi)

            def silu_gate(pair):
                act.wait_ge(blk_ready, c.at("blk"))
                act.wait_ge(h_added, c.at("ha"))
                act.activation(blk2[:, :, :], acc[:, 2 * pair:2 * pair + 2, :], ACT.Silu).then_inc(blk_half, 1)
                c.add("half")

            def ffn(blocks):
                for j in range(blocks):
                    round_groups(2)
                    if j:
                        c.add("blk")
                    round_groups(2)
                    if j:
                        round_banks(bhi, 4 * (j - 1), 2)
                    round_groups(2)
                    wait_block(2)
                    silu_gate(0)
                    round_groups(2)
                c.add("blk")
                for n in range(4):
                    round_groups(2)
                    round_groups(blocks - 2)
                    if n == 0:
                        round_banks(bhi, 4 * (blocks - 1), 2)
                c.add("ha", 4)

            c.n["ha"], c.n["blk"] = H_MLP + 4, 4 * MLP_CHUNKS + 2
            with c.loop(act, 2, g=48, q=8, half=4, blk=4, ha=4):
                ffn(4)
            ffn(3)
            act.wait_ge(h_added, H_ALL)
            norm_stats(6, h)
            act.wait_ge(fg_in, 16)
            for t in range(T):
                act.wait_ge(final_set, t + 1)
                act.dma_start(out[t * P:(t + 1) * P, :], u_ffn[:, t, :]).then_inc(out_s, 16)
            act.wait_ge(out_s, 32)

        @block.vector
        def _(dve):
            c = Counts()

            def remainders(n, size=KG * NB):
                for _ in range(n):
                    g4, g2 = c.slot("g", WSLOTS), c.slot("g", HSLOTS)
                    dve.wait_ge(hi_done, c.at("g", 1))
                    dve.tensor_tensor(wlo[:, g2, 0:size], wring[:, g4, 0:size], whi[:, g2, 0:size].bitcast(F32),
                                      ALU.subtract).then_inc(lo_done, 1)
                    c.add("g")

            def wait_block(back):
                dve.wait_ge(group_multiplied, c.at("g", HSLOTS - back))

            def mod_steps(n, s0, dual):
                for s in range(s0, s0 + n):
                    m2 = c.slot("m", MSLOTS)
                    dve.wait_ge(step_landed[m2], c.landed("m", MSLOTS))
                    for kt in range(2):
                        k = 2 * s + kt
                        for who in range(2 if dual else 1):
                            if k == 0:
                                dve.tensor_scalar(macc[:, who, :], mring[:, m2, kt, :], csil[:, who, k:k + 1], None,
                                                  ALU.mult).then_inc(mod_acc, 1)
                            else:
                                dve.wait_ge(mod_acc, c.at("ma", 8 - (1 if dual else 0)))
                                dve.scalar_tensor_tensor(macc[:, who, :], mring[:, m2, kt, :], csil[:, who, k:k + 1],
                                                         macc[:, who, :], ALU.mult, ALU.add).then_inc(mod_acc, 1)
                            c.add("ma")
                    c.add("m")

            def set_mod(kind, i, dual):
                dve.wait_ge(mod_reduced, c.at("mb", 1))
                for who in range(2 if dual else 1):
                    dve.tensor_tensor(modT[:, who, bass.ds(i * 4 + kind * KT, 4)], m1[:, 4 * who:4 * who + 4],
                                      vecs[:, 1, bass.ds(i * 4 + kind * KT, 4)], ALU.add).then_inc(mod_set, 1)
                c.add("mb")

            def groups_with_mod(pattern, s0, dual):
                s = s0
                for n in pattern:
                    remainders(1)
                    mod_steps(n, s, dual)
                    s += n

            def remain_banks(hi, lo, tile, banks, gain=None):
                for b in range(banks):
                    src = tp[:, c.slot("q", 2), :].rearrange("p (j s) -> p j s", j=2)
                    t0 = tile + 2 * b
                    dve.wait_ge(tp_hi, c.at("hi", 1 if gain is None else 2))
                    c.add("hi", 1 if gain is None else 2)
                    if gain is None:
                        dve.tensor_tensor(lo[:, t0:t0 + 2, :], src, hi[:, t0:t0 + 2, :].bitcast(F32), ALU.subtract).then_inc(tp_free, 1)
                    else:
                        dve.scalar_tensor_tensor(lo[:, t0, :], src[:, 0, :], gain(t0), hi[:, t0, :].bitcast(F32),
                                                 ALU.mult, ALU.subtract)
                        dve.scalar_tensor_tensor(lo[:, t0 + 1, :], src[:, 1, :], gain(t0 + 1), hi[:, t0 + 1, :].bitcast(F32),
                                                 ALU.mult, ALU.subtract).then_inc(tp_free, 1)
                    c.add("q")

            def modulate(hi, lo, gain, shift):
                def remainder(b):
                    dve.wait_ge(tp_hi, c.at("hi", 1))
                    dve.tensor_tensor(lo[:, 2 * b:2 * b + 2, :], tmpT[:, b % 2, :].rearrange("p (j s) -> p j s", j=2),
                                      hi[:, 2 * b:2 * b + 2, :].bitcast(F32), ALU.subtract).then_inc(tp_free, 1)
                    c.add("hi")

                for b in range(KT // 2):
                    q = c.slot("q", 2)
                    dve.wait_ge(tp_ready, c.at("q", 1))
                    dve.tensor_scalar(tmpT[:, b % 2, 0:S], tp[:, q, 0:S], gain(2 * b), shift(2 * b), ALU.mult, ALU.add)
                    dve.tensor_scalar(tmpT[:, b % 2, S:2 * S], tp[:, q, S:2 * S], gain(2 * b + 1), shift(2 * b + 1),
                                      ALU.mult, ALU.add).then_inc(tp_tmp, 1)
                    c.add("q")
                    if b:
                        remainder(b - 1)
                remainder(KT // 2 - 1)

            def norm_scale(n, src, dst, gain=None):
                dve.wait_ge(ssq_done, T * (n + 1))
                dve.tensor_scalar(ssq[:, n, :], ssq[:, n, :], 1.0 / D, EPS, ALU.mult, ALU.add).then_inc(mean_done, 1)
                dve.wait_ge(root_done, n + 1)
                dve.reciprocal(rstd[:, n, :], ssq[:, n, :]).then_inc(rstd_done, 1)
                dve.wait_ge(rstd_done, n + 1)
                for t in range(T if dst is not None else 0):
                    if gain is not None:
                        dve.scalar_tensor_tensor(dst[:, t, :], src[:, t, :], rstd[:, n, t:t + 1], gain,
                                                 ALU.mult, ALU.mult).then_inc(u_done, 1)
                    else:
                        dve.tensor_scalar(dst[:, t, :], src[:, t, :], rstd[:, n, t:t + 1], None, ALU.mult).then_inc(u_done, 1)

            dve.sem_inc(mod_acc, 8)
            dve.sem_inc(lo_done, WSLOTS)
            dve.sem_inc(h_added, H0)
            dve.sem_inc(tp_free, 2)
            dve.wait_ge(x_in, 32)
            norm_scale(0, h, u_mix)
            dve.wait_ge(vec_turned, 3)
            dve.tensor_copy(vecs[:, :, :], m0[:, 0:3 * P].rearrange("p (a b) -> p a b", a=3)).then_inc(vec_set, 1)
            dve.wait_ge(c_exp, 1)
            csil_flat = csil[:, :, :].rearrange("p w k -> p (w k)")
            dve.tensor_scalar(csil_flat, csil_flat, 1.0, None, ALU.add).then_inc(c_sil, 1)
            dve.wait_ge(c_sil, 1)
            dve.reciprocal(csil_flat, csil_flat).then_inc(c_sil, 1)
            dve.wait_ge(c_sil, 2)
            dve.tensor_tensor(csil_flat, csil_flat, vecs[:, 0, V_C:V_C + 2 * KT], ALU.mult).then_inc(c_sil, 1)
            remain_banks(xhi, xlo, 0, 8, lambda k: vecs[:, 0, V_MIXG + k:V_MIXG + k + 1])
            dve.wait_ge(c_sil, 3)

            with c.loop(dve, 4, g=8, m=8, ma=32, mb=1) as i:
                groups_with_mod(SPREAD, 0, True)
                set_mod(SH1, i, True)

            dve.wait_ge(misc_in, 16 * 6)
            for s in range(HEADS + 1):
                g = s // 2
                if s < HEADS:
                    dve.wait_ge(scores_done, s + 1)
                    if s:
                        dve.wait_ge(exps_done, T * s)
                    dve.scalar_tensor_tensor(sbias, tab_a[:, 0, :], 2.0 ** (-8.0 * (s + 1) / HEADS), acc[:, 2, :],
                                             ALU.mult, ALU.add).then_inc(scores_biased, 1)
                    dve.wait_ge(scores_biased, s + 1)
                    dve.reduce_max(nmax[:, s, :], sbias.rearrange("p (t k) -> p t k", t=T), AX_X, negate=True).then_inc(max_set, 1)
                if s % 2:
                    dve.wait_ge(f3_hi, g + 1)
                    dve.tensor_tensor(xlo[:, 2 * g:2 * g + 2, :], m1[:, :].rearrange("p (c s) -> p c s", c=2),
                                      xhi[:, 2 * g:2 * g + 2, :].bitcast(F32), ALU.subtract).then_inc(f3_lo, 1)
                if s:
                    dve.wait_ge(pv_hi, s)
                    dve.tensor_tensor(xlo[:, 7 + s, :], acc[:, 3, 0:S], xhi[:, 7 + s, :].bitcast(F32),
                                      ALU.subtract).then_inc(pv_lo, 1)
                if s < HEADS:
                    for t in range(T):
                        dve.wait_ge(exps_done, T * s + t + 1)
                        dve.scalar_tensor_tensor(probs[:, t * S:(t + 1) * S], probs[:, t * S:(t + 1) * S], 1.0,
                                                 tab_a[:, 1, t * S:(t + 1) * S], ALU.mult, ALU.mult,
                                                 accum_out=aden[:, s, t:t + 1]).then_inc(probs_summed, 1)
                    dve.wait_ge(probs_summed, T * (s + 1))
                    dve.reciprocal(arden[:, s, :], aden[:, s, :]).then_inc(den_inverted, 1)
                    dve.wait_ge(den_inverted, s + 1)
                    for t in range(T):
                        dve.tensor_scalar(probs[:, t * S:(t + 1) * S], probs[:, t * S:(t + 1) * S],
                                          arden[:, s, t:t + 1], None, ALU.mult).then_inc(probs_ready, 1)

            def add_block(n, pair):
                dve.tensor_tensor(h[:, :, bass.ds(n, NB)], acc[:, 2 * pair:2 * pair + 2, :], h[:, :, bass.ds(n, NB)],
                                  ALU.add).then_inc(h_added, 1)

            with c.loop(dve, 2, g=8) as i:
                remainders(6)
                wait_block(2)
                add_block(i * (2 * NB), 0)
                remainders(2)
                wait_block(0)
                add_block(i * (2 * NB) + NB, 1)
            dve.wait_ge(h_added, H0 + 4)
            norm_scale(1, h, u_mlp)
            remain_banks(xhi, xlo, 0, 8, lambda k: vecs[:, 0, V_MLPG + k:V_MLPG + k + 1])

            with c.loop(dve, MLP_CHUNKS, g=32, q=8, hi=8, m=24, ma=64, mb=3) as i:
                kinds = ((SC1, True), (GT1, False), (SH2, False), None)
                for t in range(4):
                    s = 0
                    for g in range(8):
                        j = 2 * t + g // 4
                        remainders(1)
                        if t < 3:
                            mod_steps(SPREAD[g], s, kinds[t][1])
                            s += SPREAD[g]
                        if g % 4 == 1 and j >= 5:
                            wait_block(2)
                            add_block((j - 5) * NB, (j - 1) % 2)
                        if g % 4 == 3 and 1 <= j <= 4:
                            remain_banks(ahi, alo, 4 * (j - 1), 2)
                    if t < 3:
                        set_mod(kinds[t][0], i, kinds[t][1])
                wait_block(0)
                add_block(3 * NB, 1)

            def store_block(name, pair):
                src = acc[:, 2 * pair:2 * pair + 2, :]
                if name in ("cx0", "cx1"):
                    dve.wait_ge(in_set, IN_SET[1]["cc" + name[2]])
                    dve.tensor_tensor(blk[:, :, :], blk[:, :, :], src, ALU.mult).then_inc(blk_ready, 1)

            def conv(half, pr):
                qu, qb = c.slot("q", 2), (c.slot("q", 2) + 1) % 2
                dve.wait_ge(tp_ready, c.at("q", 2))
                for j in range(2):
                    ch = 4 * half + 2 * pr + j
                    n = 4 * ch
                    y = convT[:, ch, :]
                    yr = y.rearrange("p (r w) -> p r w", w=GRID)
                    u = tp[:, qu, j * S:(j + 1) * S]
                    ur = u.rearrange("p (r w) -> p r w", w=GRID)
                    tap = [vecs[:, 2, 8 * k + ch:8 * k + ch + 1] for k in range(3)]
                    dve.tensor_scalar(y, u, tap[1], None, ALU.mult).then_inc(conv_step, 1)
                    dve.wait_ge(conv_step, n + 1)
                    dve.scalar_tensor_tensor(yr[:, :, 1:GRID], ur[:, :, 0:GRID - 1], tap[0], yr[:, :, 1:GRID],
                                             ALU.mult, ALU.add).then_inc(conv_step, 1)
                    dve.wait_ge(conv_step, n + 2)
                    dve.scalar_tensor_tensor(yr[:, :, 0:GRID - 1], ur[:, :, 1:GRID], tap[2], yr[:, :, 0:GRID - 1],
                                             ALU.mult, ALU.add).then_inc(conv_step, 1)
                    dve.wait_ge(conv_step, n + 3)
                    dve.tensor_tensor(y, y, tp[:, qb, j * S:(j + 1) * S], ALU.mult).then_inc(conv_step, 1)
                dve.wait_ge(conv_step, n + 4)
                dve.sem_inc(tp_free, 2)
                c.add("q", 2)

            def gla(p):
                for t in range(T):
                    dve.wait_ge(la_step, 6 * p + 4 + t + 1)
                    dve.scalar_tensor_tensor(la[:, t], acc[:, 2 * t:2 * t + 2, :], 0.0, la[:, t], ALU.min,
                                             ALU.subtract).then_inc(la_ready, 1)
                if p:
                    dve.wait_ge(conv_hi, 1)
                    dve.tensor_tensor(xlo[:, 8:16, :], convT, xhi[:, 8:16, :].bitcast(F32), ALU.subtract).then_inc(conv_lo, 1)
                for t in range(T):
                    dve.wait_ge(kdec_exp, T * p + t + 1)
                    for d in range(2):
                        dve.tensor_tensor(kdec[:, t, d], kdec[:, t, d], gk[:, t, :], ALU.mult).then_inc(kdec_ready, 1)
                for hd in range(GH):
                    n = GH * p + hd
                    dve.wait_ge(cum_exp, hd + 1 if p == 0 else GH + 2 * (hd + 1))
                    if p:
                        dve.wait_ge(gqk_turned, hd + 1)
                        if hd:
                            dve.wait_ge(o_done, hd)
                        else:
                            dve.memset(sc, 0.0).then_inc(sc_zeroed, 1)
                            dve.wait_ge(sc_zeroed, 1)
                        for d in range(2):
                            dve.scalar_tensor_tensor(qe[:, d, :], tp[:, 0, 0:S], DK ** -0.5, epos[:, d, :],
                                                     ALU.mult, ALU.mult).then_inc(qe_done, 1)
                            dve.tensor_tensor(ke[:, d, :], tp[:, 0, S:2 * S], eneg[:, d, :], ALU.mult).then_inc(qe_done, 1)
                        dve.wait_ge(gsc_done, hd + 1)
                        for d in range(2):
                            for t in range(T):
                                dve.copy_predicated(sc[:, d, t, :], keep[d], m1[:, (2 * d + t) * P:(2 * d + t + 1) * P]).then_inc(gsc_kept, 1)
                    dve.wait_ge(ds_done, n + 1)
                    base = STATE_STEPS[0] * GH * p + STATE_STEPS[p] * hd
                    done = 0
                    order = ((0, 1, 2, 3), (3, 2, 1, 0))
                    for step in range(NCH):
                        for d in range(2):
                            ck = order[d][step]
                            decay = epos[:, d, CH * ck + CH - 1:CH * ck + CH] if d == 0 else epos[:, d, CH * ck:CH * ck + 1]
                            ds = acc[:, 2 * d + ck % 2, (ck // 2) * DV:(ck // 2 + 1) * DV]
                            if p == 0 and step == 0:
                                dve.tensor_copy(states[:, d, hd, :], ds).then_inc(state_step, 1)
                                done += 1
                            elif p == 0:
                                dve.wait_ge(state_step, base + done - 1)
                                dve.scalar_tensor_tensor(states[:, d, hd, :], states[:, d, hd, :], decay, ds,
                                                         ALU.mult, ALU.add).then_inc(state_step, 1)
                                done += 1
                            elif step < NCH - 1:
                                src = states[:, d, hd, :] if step == 0 else gst[:, d, ck, :]
                                if step:
                                    dve.wait_ge(state_step, base + done - 1)
                                elif hd == 0 and d == 0:
                                    dve.wait_ge(spill_s, 16)
                                dve.scalar_tensor_tensor(gst[:, d, order[d][step + 1], :], src, decay, ds,
                                                         ALU.mult, ALU.add).then_inc(state_step, 1)
                                done += 1
                    assert done == STATE_STEPS[p]

            dve.wait_ge(mod_set, 8 + MLP_CHUNKS * 4)
            for who in range(2):
                dve.scalar_tensor_tensor(gain1[:, who, :], modT[:, who, SC1 * KT:(SC1 + 1) * KT], 1.0,
                                         vecs[:, 0, V_N1G:V_N1G + KT], ALU.add, ALU.mult).then_inc(gain_set, 1)
            dve.wait_ge(ctx_in_s, 16)
            norm_scale(2, u_g, u_g)
            dve.wait_ge(gain_set, 2)
            modulate(xhi, xlo, lambda k: gain1[:, 1, k:k + 1], lambda k: modT[:, 1, SH1 * KT + k:SH1 * KT + k + 1])
            remainders(2, 8 * RANK2)
            remainders(2)
            dve.wait_ge(mg_in, 16)
            norm_scale(3, h, h, mgain[:, :])
            remainders(10)
            gla(0)
            dve.wait_ge(u_done, 4 * T)
            norm_scale(4, h, u_g)
            modulate(xhi, xlo, lambda k: gain1[:, 0, k:k + 1], lambda k: modT[:, 0, SH1 * KT + k:SH1 * KT + k + 1])
            for n, name in enumerate(X_IN):
                if name == "l":
                    remainders(2, 8 * RANK2)
                    continue
                pattern = DENSE if n < 5 else (SPREAD[0:4] if n % 2 else SPREAD[4:8])
                s = 0 if n < 5 or n % 2 else sum(SPREAD[0:4])
                for kg in range(4):
                    remainders(1)
                    mod_steps(pattern[kg], s, False)
                    s += pattern[kg]
                    if kg == 1:
                        wait_block(2)
                        store_block(X_IN[n - 1], (48 + n - 1) % 2)
                    if kg >= 2 and name in ("cc1", "g0"):
                        conv(0 if name == "cc1" else 1, kg - 2)
                if n < 5:
                    set_mod(SC2, n - 1, False)
                elif n % 2 == 0:
                    set_mod(GT2, (n - 6) // 2, False)
            gla(1)
            dve.wait_ge(o_copied, 4 * GH)
            dve.tensor_scalar(oss[:, :, :], oss[:, :, :], 1.0 / DV, EPS, ALU.mult, ALU.add).then_inc(o_mean, 1)
            dve.wait_ge(o_root, 1)
            dve.reciprocal(orstd[:, :, :], oss[:, :, :]).then_inc(o_rstd, 1)
            dve.wait_ge(o_rstd, 1)
            for hd in range(GH):
                for t in range(T):
                    o = o_all[:, t, hd * DV:(hd + 1) * DV]
                    dve.scalar_tensor_tensor(o, o, orstd[:, t, hd:hd + 1], silg[:, t, hd * DV:(hd + 1) * DV],
                                             ALU.mult, ALU.mult).then_inc(o_gated, 1)
            remain_banks(xhi, xlo, 0, 4, lambda k: vecs[:, 2, 24 + k % 2:25 + k % 2])
            for b in range(8):
                dve.wait_ge(tp_ready, c.at("q", 1))
                dve.tensor_copy(gates[:, b // 4, (b % 4) * NB:(b % 4 + 1) * NB], tp[:, c.slot("q", 2), :]).then_inc(tp_free, 1)
                c.add("q")
            dve.wait_ge(tp_free, c.at("q", 2))

            def gated_add(which, n, pair):
                gate = gates[:, which, bass.ds(n, NB)].unsqueeze(1).broadcast_to([P, T, NB])
                dve.tensor_tensor(blk2[:, :, :], acc[:, 2 * pair:2 * pair + 2, :], gate, ALU.mult).then_inc(h_scaled, 1)
                c.add("hs")
                dve.wait_ge(h_scaled, c.at("hs"))
                dve.tensor_tensor(h[:, :, bass.ds(n, NB)], blk2[:, :, :], h[:, :, bass.ds(n, NB)], ALU.add).then_inc(h_added, 1)
                c.add("ha")

            dve.wait_ge(reload_s, 16)
            with c.loop(dve, 2, g=8, hs=2, ha=2) as i:
                remainders(6)
                wait_block(2)
                gated_add(0, i * (2 * NB), 0)
                remainders(2)
                wait_block(0)
                gated_add(0, i * (2 * NB) + NB, 1)
            dve.wait_ge(h_added, H_MLP + 4)
            norm_scale(5, h, u_ffn)
            dve.scalar_tensor_tensor(gain2[:, :], modT[:, 0, SC2 * KT:(SC2 + 1) * KT], 1.0,
                                     vecs[:, 0, V_N2G:V_N2G + KT], ALU.add, ALU.mult).then_inc(gain_set, 1)
            dve.wait_ge(gain_set, 3)
            modulate(xhi, xlo, lambda k: gain2[:, k:k + 1], lambda k: modT[:, 0, SH2 * KT + k:SH2 * KT + k + 1])

            def gate_up():
                dve.wait_ge(blk_half, c.at("half", 1))
                dve.tensor_tensor(blk[:, :, :], blk2[:, :, :], acc[:, 2:4, :], ALU.mult).then_inc(blk_ready, 1)
                c.add("half")

            def ffn(blocks):
                for j in range(blocks):
                    remainders(2)
                    if j:
                        wait_block(2)
                        gate_up()
                    remainders(2)
                    if j:
                        remain_banks(bhi, blo, 4 * (j - 1), 2)
                    remainders(4)
                for n in range(4):
                    remainders(2)
                    wait_block(2)
                    if n == 0:
                        gate_up()
                    else:
                        gated_add(1, (n - 1) * NB, (n - 1) % 2)
                    remainders(blocks - 2)
                    if n == 0:
                        remain_banks(bhi, blo, 4 * (blocks - 1), 2)
                wait_block(0)
                gated_add(1, 3 * NB, 1)

            c.n["half"] = 4 * MLP_CHUNKS
            with c.loop(dve, 2, g=48, q=8, hi=8, half=4, hs=4, ha=4):
                ffn(4)
            ffn(3)
            dve.wait_ge(h_added, H_ALL)
            norm_scale(6, h, None)
            dve.wait_ge(fg_in, 16)
            for t in range(T):
                dve.scalar_tensor_tensor(u_ffn[:, t, :], h[:, t, :], rstd[:, 6, t:t + 1], fgain[:, :],
                                         ALU.mult, ALU.mult).then_inc(final_set, 1)

        @block.tensor
        def _(pe):
            c = Counts()

            def multiply(hi, lo, kgs, kgroups, pair, half=None):
                kts, width = (KG, NB) if half is None else (8, RANK2)
                for kg in kgs:
                    g2 = c.slot("g", HSLOTS)
                    pe.wait_ge(lo_done, c.at("g", WSLOTS + 1))
                    for k in range(kts):
                        tile = kg * kts + k
                        w = slice(k * width, (k + 1) * width)
                        for t in range(T):
                            dst = acc[:, 2 * pair + t, 0:width]
                            rows = slice(t * P, (t + 1) * P)
                            pe.matmul(dst, hi[:, tile, rows], whi[:, g2, w], start=(tile == 0), stop=False)
                            pe.matmul(dst, hi[:, tile, rows], wlo[:, g2, w], start=False, stop=False)
                            last = pe.matmul(dst, lo[:, tile, rows], whi[:, g2, w], start=False,
                                             stop=(tile == kgroups * kts - 1))
                    last.then_inc(group_multiplied, 1)
                    c.add("g")

            def turn_rows(src, banks):
                for b in range(banks):
                    q = c.slot("q", 2)
                    pe.wait_ge(tp_free, c.at("q", 1))
                    for j in range(2):
                        for t in range(T):
                            f = (2 * b + j) * P
                            last = pe.transpose(tp[:, q, j * S + t * P:j * S + (t + 1) * P], src[:, t, f:f + P], ident)
                    last.then_inc(tp_ready, 1)
                    c.add("q")

            def reduce_mod(per_nb, dual):
                c.add("ma", per_nb)
                pe.wait_ge(mod_acc, c.at("ma", 8))
                for who in range(2 if dual else 1):
                    for j in range(4):
                        last = pe.matmul(m1[:, 4 * who + j:4 * who + j + 1], macc[:, who, j * P:(j + 1) * P],
                                         ones[:, 0:1], start=True, stop=True)
                last.then_inc(mod_reduced, 1)

            pe.sem_inc(group_multiplied, HSLOTS)
            pe.wait_ge(start_in, 32)
            for a in range(3):
                pe.transpose(m0[:, a * P:(a + 1) * P], vrows[:, a, :], ident).then_inc(vec_turned, 1)
            pe.wait_ge(u_done, T)
            turn_rows(u_mix, 8)
            pe.wait_ge(tp_free, c.at("q", 2))
            pe.wait_ge(pool_set, 1)

            with c.loop(pe, 4, g=8, ma=32, ps=2):
                pe.wait_ge(proj_set, c.at("ps", 1))
                multiply(xhi, xlo, range(4), 4, 0)
                c.add("ps")
                pe.wait_ge(proj_set, c.at("ps", 1))
                multiply(xhi, xlo, range(3), 4, 1)
                c.add("ps")
                reduce_mod(32, True)
                multiply(xhi, xlo, (3,), 4, 1)

            pe.wait_ge(proj_set, 2 + 8)
            pe.wait_ge(misc_in, 16 * 6)
            for s in range(HEADS + 1):
                g = s // 2
                if s < HEADS:
                    if s:
                        pe.wait_ge(qk_copied, 2 * s)
                    for w, col in ((0, 2 * NB), (1, 4 * NB)):
                        for t in range(T):
                            last = pe.transpose(tp[:, 0, w * S + t * P:w * S + (t + 1) * P],
                                                proj[:, t, col + s * HD:col + (s + 1) * HD], ident)
                    last.then_inc(qk_turned, 1)
                if s < HEADS and s % 2 == 0:
                    if g:
                        pe.wait_ge(f1_copied, g)
                    for ct in range(2):
                        for t in range(T):
                            last = pe.matmul(acc[:, ct, :], proj[:, t, g * FDIM + ct * P:g * FDIM + (ct + 1) * P],
                                             tab_f[:, t, 0:2 * S], start=(t == 0), stop=(t == T - 1))
                    last.then_inc(f1_done, 1)
                if s % 2:
                    pe.wait_ge(f1_copied, g + 1)
                    if g:
                        pe.wait_ge(f2_copied, g)
                    for cc in range(2):
                        for n, (part, ct) in enumerate(((0, 0), (0, 1), (1, 0), (1, 1))):
                            last = pe.matmul(m0[:, cc * S:(cc + 1) * S],
                                             tab_f[:, ct, part * 2 * S + cc * P:part * 2 * S + (cc + 1) * P],
                                             fpos[:, ct, part * S:(part + 1) * S], start=(n == 0), stop=(n == 3))
                    last.then_inc(f2_done, 1)
                if s < HEADS:
                    pe.wait_ge(qk_copied, 2 * (s + 1))
                    if s:
                        pe.wait_ge(scores_biased, s)
                    for t in range(T):
                        last = pe.matmul(acc[:, 2, t * S:(t + 1) * S], qkT[:, s % 2, 0, t * P:(t + 1) * P],
                                         qkT[:, s % 2, 1, :], start=True, stop=True)
                    last.then_inc(scores_done, 1)
                if s:
                    pe.wait_ge(probs_ready, T * s)
                    if s >= 2:
                        pe.wait_ge(probsT_copied, s - 1)
                    for kt in range(2):
                        for t in range(T):
                            last = pe.transpose(tp[:, 1, kt * S + t * P:kt * S + (t + 1) * P],
                                                probs[:, t * S + kt * P:t * S + (kt + 1) * P], ident)
                    last.then_inc(probs_turned, 1)
                if s % 2:
                    pe.wait_ge(f2_copied, g + 1)
                    if g:
                        pe.wait_ge(f3_lo, g)
                    for e in range(2):
                        for cc in range(2):
                            last = pe.matmul(m1[:, e * S:(e + 1) * S], wf[:, g, cc, e * P:(e + 1) * P], fre[:, cc, :],
                                             start=(cc == 0), stop=(cc == 1))
                    last.then_inc(f3_done, 1)
                if s:
                    pe.wait_ge(probsT_copied, s)
                    if s >= 2:
                        pe.wait_ge(pv_lo, s - 1)
                    v = 6 * NB + (s - 1) * HD
                    for kt in range(2):
                        last = pe.matmul(acc[:, 3, 0:S], proj[:, kt, v:v + HD], probsT[:, kt, :],
                                         start=(kt == 0), stop=(kt == 1))
                    last.then_inc(pv_done, 1)
            pe.wait_ge(f3_lo, FGROUPS)
            pe.wait_ge(pv_lo, HEADS)

            with c.loop(pe, 2, g=8, ha=2):
                for pair in range(2):
                    pe.wait_ge(h_added, c.at("ha", 1))
                    multiply(xhi, xlo, range(4), 4, pair)
                    c.add("ha")
            pe.wait_ge(u_done, 2 * T)
            turn_rows(u_mlp, 8)
            pe.wait_ge(tp_free, c.at("q", 2))

            with c.loop(pe, MLP_CHUNKS, g=32, q=8, ma=64, ha=4, half=4, blk=4):
                for j in range(8):
                    pair = j % 2
                    if j < 2:
                        pe.wait_ge(h_added, c.at("ha", 1 + j))
                    elif j < 6:
                        pe.wait_ge(blk_half, c.at("half", j - 1))
                    else:
                        pe.wait_ge(h_added, c.at("ha", 2 + j - 5))
                    hi, lo = (xhi, xlo) if j < 4 else (ahi, alo)
                    multiply(hi, lo, range(2), 4, pair)
                    if 1 <= j <= 4:
                        pe.wait_ge(blk_ready, c.at("blk", j))
                        turn_rows(blk, 2)
                    multiply(hi, lo, (2,), 4, pair)
                    if j % 2 and j < 6:
                        reduce_mod(32 if j == 1 else 16, j == 1)
                    if j == 4:
                        pe.wait_ge(tp_free, c.at("q", 2))
                    multiply(hi, lo, (3,), 4, pair)
                c.add("ha", 4)
                c.add("half", 4)
                c.add("blk", 4)

            def evacuated(name, p):
                if p and name in ("cx0", "cx1"):
                    pe.wait_ge(blk_ready, 4 * MLP_CHUNKS + 1 + int(name[2]))
                else:
                    pe.wait_ge(in_set, IN_SET[p][name])

            def in_blocks(names, b0, p):
                for n, name in enumerate(names):
                    pair = (b0 + n) % 2
                    if n >= 2:
                        evacuated(names[n - 2], p)
                    if name == "l":
                        multiply(xhi, xlo, range(2), 2, pair, half=True)
                        continue
                    multiply(xhi, xlo, range(2), 4, pair)
                    if p and name in ("cc1", "g0"):
                        turn_conv(0 if name == "cc1" else 1, 0)
                    multiply(xhi, xlo, (2,), 4, pair)
                    if p and name in ("cc1", "g0"):
                        turn_conv(0 if name == "cc1" else 1, 1)
                    if p and (n < 5 or n % 2 == 0):
                        reduce_mod(16, False)
                    multiply(xhi, xlo, (3,), 4, pair)

            def turn_conv(half, pr):
                pe.wait_ge(blk_ready, 4 * MLP_CHUNKS + 1 + half)
                pe.wait_ge(in_set, IN_SET[1]["cb1" if half else "cb0"])
                for src in (blk, blk2):
                    q = c.slot("q", 2)
                    pe.wait_ge(tp_free, c.at("q", 1))
                    for j in range(2):
                        for t in range(T):
                            f = (2 * pr + j) * P
                            last = pe.transpose(tp[:, q, j * S + t * P:j * S + (t + 1) * P], src[:, t, f:f + P], ident)
                    last.then_inc(tp_ready, 1)
                    c.add("q")

            def gla(p):
                pe.wait_ge(in_set, IN_SET[p]["g1" if p else "v1"])
                if p:
                    pe.wait_ge(cum_exp, GH)
                for t in range(T):
                    last = pe.transpose(m0[:, t * P:(t + 1) * P], lrank[:, t, :], ident)
                last.then_inc(lr_turned, 1)
                pe.wait_ge(lr_copied, p + 1)
                pe.wait_ge(wg_in, 16)
                for t in range(T):
                    for d in range(2):
                        last = pe.matmul(acc[:, 2 * t + d, :], lrankT[:, t * P:(t + 1) * P], wg[:, d, :], start=True, stop=True)
                    last.then_inc(z_done, 1)
                for t in range(T):
                    pe.wait_ge(la_ready, T * p + t + 1)
                    for d in range(2):
                        last = pe.matmul(acc[:, 2 * t + d, :], after[d], la[:, t, d], start=True, stop=True)
                    last.then_inc(sfx_done, 1)
                for hd in range(GH):
                    n = GH * p + hd
                    base = STATE_STEPS[0] * GH * p + STATE_STEPS[p] * hd
                    if hd:
                        pe.wait_ge(cum_exp, hd if p == 0 else GH + 2 * hd)
                    for d in range(2):
                        for t in range(T):
                            last = pe.matmul(m0[:, d * S + t * P:d * S + (t + 1) * P], la[:, t, d, hd * DK:(hd + 1) * DK],
                                             tri[d], start=True, stop=True)
                    last.then_inc(cum_done, 1)
                    if p:
                        if hd:
                            pe.wait_ge(qe_done, 4 * hd)
                        for w, src in ((0, gq), (1, gk)):
                            for t in range(T):
                                last = pe.transpose(tp[:, 0, w * S + t * P:w * S + (t + 1) * P],
                                                    src[:, t, hd * DK:(hd + 1) * DK], ident)
                        last.then_inc(gqk_turned, 1)
                    if hd:
                        pe.wait_ge(state_step, base)
                    else:
                        pe.wait_ge(kdec_ready, 4 * (p + 1))
                    for d in range(2):
                        for ck in range(NCH):
                            rows = slice((ck % 2) * CH, (ck % 2 + 1) * CH)
                            last = pe.matmul(acc[:, 2 * d + ck % 2, (ck // 2) * DV:(ck // 2 + 1) * DV],
                                             kdec[rows, ck // 2, d, hd * DK:(hd + 1) * DK],
                                             gv[rows, ck // 2, hd * DV:(hd + 1) * DV], start=True, stop=True)
                    last.then_inc(ds_done, 1)
                    if not p:
                        continue
                    pe.wait_ge(qe_done, 4 * (hd + 1))
                    for d in range(2):
                        for t in range(T):
                            last = pe.matmul(m1[:, (2 * d + t) * P:(2 * d + t + 1) * P], ke[:, d, t * P:(t + 1) * P],
                                             qe[:, d, t * P:(t + 1) * P], start=True, stop=True)
                    last.then_inc(gsc_done, 1)
                    pe.wait_ge(gsc_kept, 4 * (hd + 1))
                    pe.wait_ge(state_step, base + STATE_STEPS[1])
                    if hd:
                        pe.wait_ge(o_copied, 4 * hd)
                    for t in range(T):
                        for d in range(2):
                            pe.matmul(tp[:, 1, t * DV:(t + 1) * DV], sc[:, d, t, :], gv[:, t, hd * DV:(hd + 1) * DV],
                                      start=(d == 0), stop=False)
                        for d in range(2):
                            for half in range(2):
                                ck = 2 * t + half
                                first = ck == (0 if d == 0 else NCH - 1)
                                state = states[:, d, hd, :] if first else gst[:, d, ck, :]
                                last = pe.matmul(tp[half * CH:(half + 1) * CH, 1, t * DV:(t + 1) * DV],
                                                 qe[:, d, ck * CH:(ck + 1) * CH], state, start=False, stop=(d == 1))
                    last.then_inc(o_done, 1)

            pe.wait_ge(u_done, 3 * T)
            turn_rows(u_g, 8)
            pe.wait_ge(tp_free, c.at("q", 2))
            in_blocks(C_IN, 44, 0)
            gla(0)
            pe.wait_ge(u_done, 5 * T)
            turn_rows(u_g, 8)
            pe.wait_ge(tp_free, c.at("q", 2))
            in_blocks(X_IN, 48, 1)
            gla(1)
            pe.wait_ge(o_gated, T * GH)
            turn_rows(o_all, 4)
            pe.wait_ge(mod_set, 32)
            for b in range(8):
                q = c.slot("q", 2)
                pe.wait_ge(tp_free, c.at("q", 1))
                for j in range(4):
                    col = (GT1 if b < 4 else GT2) * KT + 4 * (b % 4) + j
                    last = pe.matmul(tp[:, q, j * P:(j + 1) * P], modT[:, 0, col:col + 1].broadcast_to([P, P]), ident,
                                     start=True, stop=True)
                last.then_inc(tp_ready, 1)
                c.add("q")
            pe.wait_ge(tp_free, c.at("q", 2))

            with c.loop(pe, 2, g=8, ha=2):
                for pair in range(2):
                    pe.wait_ge(h_added, c.at("ha", 1))
                    multiply(xhi, xlo, range(4), 4, pair)
                    c.add("ha")
            pe.wait_ge(u_done, 6 * T)
            turn_rows(u_ffn, 8)
            pe.wait_ge(tp_free, c.at("q", 2))
            c.n["half"] = 4 * MLP_CHUNKS
            c.n["blk"] = 4 * MLP_CHUNKS + 2

            def ffn(blocks):
                for j in range(blocks):
                    if j:
                        pe.wait_ge(blk_half, c.at("half", j))
                    else:
                        pe.wait_ge(h_scaled, c.at("hs", -1))
                    multiply(xhi, xlo, range(2), 4, 0)
                    if j:
                        pe.wait_ge(blk_ready, c.at("blk", j))
                        turn_rows(blk, 2)
                    multiply(xhi, xlo, (2, 3), 4, 0)
                    if not j:
                        pe.wait_ge(h_scaled, c.at("hs"))
                    multiply(xhi, xlo, range(4), 4, 1)
                for n in range(4):
                    if n == 0:
                        pe.wait_ge(blk_half, c.at("half", blocks))
                    elif n >= 2:
                        pe.wait_ge(h_scaled, c.at("hs", n - 1))
                    multiply(bhi, blo, range(2), blocks, n % 2)
                    if n == 0:
                        pe.wait_ge(blk_ready, c.at("blk", blocks))
                        turn_rows(blk, 2)
                    for kg in range(2, blocks):
                        if n == 0 and kg == blocks - 1:
                            pe.wait_ge(tp_free, c.at("q", 2))
                        multiply(bhi, blo, (kg,), blocks, n % 2)
                c.add("half", blocks)
                c.add("blk", blocks)
                c.add("hs", 4)

            c.n["hs"] = 4
            with c.loop(pe, 2, g=48, q=8, half=4, blk=4, hs=4):
                ffn(4)
            ffn(3)


def kernel(**inputs):
    import concourse.bacc as bacc
    from concourse.bass_utils import run_bass_kernel_spmd

    nc = bacc.Bacc("TRN2", target_bir_lowering=False, num_devices=1)
    a = {k: np.asarray(v) for k, v in inputs.items()}

    vectors = np.zeros((P, 3, P), np.float32)
    rows = [a["norm_mix_g"], a["norm_mlp_g"], a["norm1_g_2"], a["norm2_g_2"], a["c_2"], a["c_ctx_2"]]
    vectors[0:96, 0] = np.concatenate([r.reshape(KT, P) for r in rows])
    vectors[0:96, 1] = a["b_mod_2"].reshape(6 * KT, P)
    vectors[0:24, 2] = a["conv_w_2"].reshape(24, P)
    vectors[24:26, 2] = a["gla_norm_g_2"].reshape(2, P)
    gates_w = np.zeros((P, 2, GH * DK), np.float32)
    for d, n in enumerate(("f", "b")):
        gates_w[16 * d:16 * d + 16, d] = a[f"w_gate_{n}_2"][0]
        gates_w[RANK2, d] = a[f"b_gate_{n}_2"][0]

    j, i = np.mgrid[0:P, 0:P]
    same = j // CH == i // CH
    tables = np.stack([np.eye(P), (same & (j <= i)) / 16.0, (same & (j >= i)) / 16.0,
                       (same & (j > i)) / 16.0, (same & (j < i)) / 16.0,
                       same & (j <= i), same & (j >= i)], axis=1).astype(np.float32)
    ang = 2 * np.pi * (np.outer(np.arange(S), np.arange(S)) % S) / S
    dft = np.concatenate([np.cos(ang), np.sin(ang), -np.sin(ang)], axis=1) / np.sqrt(S)
    fourier_tables = np.ascontiguousarray(dft.reshape(2, P, 3 * S).transpose(1, 0, 2)).astype(np.float32)
    dist = np.abs(np.arange(S)[:, None] - np.arange(S)[None, :])
    seen = sum(((dist % dil == 0) & (dist // dil <= (window // 2) // dil)).astype(int)
               for window, dil in ((128, 1), (512, 4), (2048, 16)))
    attn = np.stack([np.where(seen > 0, -dist, -1e30), seen])
    attn_tables = np.ascontiguousarray(attn.reshape(2, T, P, S).transpose(2, 0, 1, 3).reshape(P, 2, T * S)).astype(np.float32)

    arrays = {
        "x": a["x"][0], "ctx_in": a["ctx_2"][0], "w_in": a["w_in"][0], "w_fourier": a["w_fourier"][0],
        "w_out": a["w_out"][0], "w_up": a["w_up"][0], "w_down": a["w_down"][0], "w_mod": a["w_mod_2"][0],
        "w_in2": a["w_in_2"][0], "w_out2": a["w_out_2"][0], "w_gate": a["w_ffn_gate_2"][0],
        "w_up2": a["w_ffn_up_2"][0], "w_down2": a["w_ffn_down_2"][0], "vectors": vectors,
        "gates_w": gates_w, "mid_g": a["norm_final_g"], "final_g": a["final_g_2"], "tables": tables,
        "fourier_tables": fourier_tables, "attn_tables": attn_tables,
    }
    args = {}
    for name, v in arrays.items():
        arrays[name] = np.ascontiguousarray(v)
        args[name] = nc.dram_tensor(name, arrays[name].shape, mybir.dt.from_np(arrays[name].dtype), kind="ExternalInput").ap()
    args["out"] = nc.dram_tensor("out", [S, D], F32, kind="ExternalOutput").ap()
    two_blocks(nc, **args)
    r = run_bass_kernel_spmd(nc, [arrays], core_ids=[0])
    return r.results[0]["out"].reshape(1, S, D)
```

```python
from contextlib import ExitStack, contextmanager

import numpy as np

import concourse.bass as bass
from concourse import mybir

P = 128
F32 = mybir.dt.float32
F32R = mybir.dt.float32r
U32 = mybir.dt.uint32
ACT = mybir.ActivationFunctionType
ALU = mybir.AluOpType
AX_X = mybir.AxisListType.X

D = 2048
S = 256
T = S // P
KT = D // P
NB = 512
KG = 4
EPS = 1e-6

FGROUPS, FDIM = 4, 256
HEADS, HD = 8, 128
MLP_CHUNKS = 4

GH, DK, DV = 4, 128, 256
CH = 64
NCH = S // CH
RANK2 = 32
OFF_Q, OFF_K, OFF_V, OFF_G, OFF_L, OFF_CB, OFF_CC, OFF_CX = 0, 512, 1024, 2048, 3072, 3104, 4128, 5152
FFN_BLOCKS = 11
GRID = 64

WSLOTS = 4
HSLOTS = 2
MSLOTS = 2
MSTEPS = 8
STATE_STEPS = (8, 6)
H0 = 2
SH1, SC1, GT1, SH2, SC2, GT2 = range(6)

V_MIXG, V_MLPG, V_N1G, V_N2G, V_C, V_CCTX = range(0, 96, 16)


class Counts:

    def __init__(self, **start):
        self.n = dict(start)
        self.i, self.start, self.per = None, 0, {}

    def at(self, name, off=0):
        v = self.n.get(name, 0) + off
        if self.i is not None and self.per.get(name, 0):
            return self.i * self.per[name] + (v - self.start * self.per[name])
        return v

    def landed(self, name, slots):
        v = 16 * (self.n.get(name, 0) // slots + 1)
        if self.i is not None and self.per.get(name, 0):
            per = self.per[name] // slots * 16
            return self.i * per + (v - self.start * per)
        return v

    def slot(self, name, slots):
        assert self.i is None or self.per.get(name, 0) % slots == 0, name
        return self.n.get(name, 0) % slots

    def add(self, name, k=1):
        self.n[name] = self.n.get(name, 0) + k

    @contextmanager
    def loop(self, eng, trips, start=0, **per):
        before = {k: self.n.get(k, 0) for k in per}
        with eng.Fori(start, trips) as i:
            self.i, self.start, self.per = i, start, per
            yield i
            self.i, self.per = None, {}
        for k, v in per.items():
            assert self.n.get(k, 0) - before[k] == v, (k, self.n.get(k, 0) - before[k], v)
            self.n[k] += v * (trips - start - 1)


def two_blocks(nc, x, ctx_in, w_in, w_fourier, w_out, w_up, w_down, w_mod, w_in2, w_out2, w_gate,
               w_up2, w_down2, vectors, gates_w, mid_g, final_g, tables, fourier_tables, attn_tables, out):
    ctx = ExitStack()
    with ctx:
        def sb(name, shape, dt=F32, scope=ctx):
            return scope.enter_context(nc.sbuf_tensor(name, shape, dt))

        def sem(name):
            return ctx.enter_context(nc.semaphore(name))

        wring = sb("wring", [P, WSLOTS, KG * NB])
        whi = sb("whi", [P, HSLOTS, KG * NB], F32R)
        wlo = sb("wlo", [P, HSLOTS, KG * NB], F32R)
        mring = sb("mring", [P, MSLOTS, 2, NB])
        macc = sb("macc", [P, 2, NB])
        h = sb("h", [P, T, D])
        xhi = sb("xhi", [P, KT, S], F32R)
        xlo = sb("xlo", [P, KT, S], F32R)
        tabs = sb("tabs", [P, 7, P])
        ident = tabs[:, 0, :]
        tri = [tabs[:, 1, :], tabs[:, 2, :]]
        after = [tabs[:, 3, :], tabs[:, 4, :]]
        keep = [tabs[:, 5, :].bitcast(U32), tabs[:, 6, :].bitcast(U32)]
        ones = sb("ones", [P, 1])
        vrows = sb("vrows", [P, 3, P])
        vecs = sb("vecs", [P, 3, P])
        csil = sb("csil", [P, 2, KT])
        modT = sb("modT", [P, 2, 6 * KT])
        gain1 = sb("gain1", [P, 2, KT])
        gain2 = sb("gain2", [P, KT])
        squares = sb("squares", [P, T, KG])
        ssq = sb("ssq", [P, 7, T])
        rstd = sb("rstd", [P, 7, T])
        blk = sb("blk", [P, T, NB])
        blk2 = sb("blk2", [P, T, NB])
        tmpT = sb("tmpT", [P, 2, NB])

        with ExitStack() as ph:
            tab_f = sb("tab_f", [P, 2, 3 * S], scope=ph)
            tab_a = sb("tab_a", [P, 2, T * S], scope=ph)
            proj = sb("proj", [P, T, 8 * NB], scope=ph)
            wf = sb("wf", [P, FGROUPS, 2, FDIM], scope=ph)
            qkT = sb("qkT", [P, 2, 2, S], scope=ph)
            nmax = sb("nmax", [P, HEADS, T], scope=ph)
            aden = sb("aden", [P, HEADS, T], scope=ph)
            arden = sb("arden", [P, HEADS, T], scope=ph)
        u_mix = proj[:, :, 0:D]
        fpos = blk
        fre = tmpT[:, 0, :].rearrange("p (c s) -> p c s", c=2)
        probsT = tmpT[:, 1, :].rearrange("p (c s) -> p c s", c=2)
        sbias = blk2[:, 0, :]
        probs = blk2[:, 1, :]
        with ExitStack() as ph:
            ahi = sb("ahi", [P, KT, S], F32R, scope=ph)
            alo = sb("alo", [P, KT, S], F32R, scope=ph)
            u_mlp = sb("u_mlp", [P, T, D], scope=ph)
            mgain = sb("mgain", [P, D], scope=ph)
        with ExitStack() as ph:
            states = sb("states", [P, 2, GH, DV], scope=ph)
            wg = sb("wg", [P, 2, GH * DK], scope=ph)
            gk = sb("gk", [P, T, GH * DK], scope=ph)
            gv = sb("gv", [P, T, GH * DV], scope=ph)
            gq = sb("gq", [P, T, GH * DK], scope=ph)
            lrank = sb("lrank", [P, T, P], scope=ph)
            lrankT = sb("lrankT", [P, S], scope=ph)
            epos = sb("epos", [P, 2, S], scope=ph)
            gbig = sb("gbig", [P, 2 * D], scope=ph)
            silg = sb("silg", [P, T, GH * DV], scope=ph)
            convT = sb("convT", [P, 8, S], scope=ph)
            oss = sb("oss", [P, T, GH], scope=ph)
            orstd = sb("orstd", [P, T, GH], scope=ph)
        u_g = gbig[:, :].rearrange("p (t d) -> p t d", t=T)
        la = gbig[:, 0:D].rearrange("p (t d c) -> p t d c", t=T, d=2)
        kdec = gbig[:, D:2 * D].rearrange("p (t d c) -> p t d c", t=T, d=2)
        gst = h[:, 0, :].rearrange("p (d c v) -> p d c v", d=2, c=NCH)
        o_all = h[:, 1, :].rearrange("p (t c) -> p t c", t=T)
        eneg = tmpT[:, 0, :].rearrange("p (d s) -> p d s", d=2)
        qe = blk[:, 0, :].rearrange("p (d s) -> p d s", d=2)
        ke = blk[:, 1, :].rearrange("p (d s) -> p d s", d=2)
        sc = blk2[:, 0, :].rearrange("p (d t s) -> p d t s", d=2, t=T)
        with ExitStack() as ph:
            with ExitStack() as sub:
                u_ffn = sb("u_ffn", [P, T, D], scope=sub)
            bhi = sb("bhi", [P, KT, S], F32R, scope=ph)
            blo = sb("blo", [P, KT, S], F32R, scope=ph)
            gates = sb("gates", [P, 2, D], scope=ph)
            fgain = sb("fgain", [P, D], scope=ph)

        acc = ctx.enter_context(nc.psum_tensor("acc", [P, 2 * T, NB], F32))
        tp = ctx.enter_context(nc.psum_tensor("tp", [P, 2, NB], F32))
        m0 = ctx.enter_context(nc.psum_tensor("m0", [P, NB], F32))
        m1 = ctx.enter_context(nc.psum_tensor("m1", [P, NB], F32))
        hspill = nc.dram_tensor("hspill", [T, P, D], F32).ap()

        group_landed = [sem(f"group_landed{i}") for i in range(WSLOTS)]
        hi_done = sem("hi_done")
        lo_done = sem("lo_done")
        group_multiplied = sem("group_multiplied")
        tp_ready = sem("tp_ready")
        tp_hi = sem("tp_hi")
        tp_tmp = sem("tp_tmp")
        tp_free = sem("tp_free")
        step_landed = [sem(f"step_landed{i}") for i in range(MSLOTS)]
        mod_acc = sem("mod_acc")
        mod_reduced = sem("mod_reduced")
        mod_set = sem("mod_set")
        start_in = sem("start_in")
        x_in = sem("x_in")
        misc_in = sem("misc_in")
        ctx_in_s = sem("ctx_in_s")
        wg_in = sem("wg_in")
        spill_s = sem("spill_s")
        reload_s = sem("reload_s")
        fg_in = sem("fg_in")
        mg_in = sem("mg_in")
        out_s = sem("out_s")
        pool_set = sem("pool_set")
        vec_turned = sem("vec_turned")
        vec_set = sem("vec_set")
        c_exp = sem("c_exp")
        c_sil = sem("c_sil")
        ssq_done = sem("ssq_done")
        squares_summed = sem("squares_summed")
        mean_done = sem("mean_done")
        root_done = sem("root_done")
        rstd_done = sem("rstd_done")
        u_done = sem("u_done")
        blk_ready = sem("blk_ready")
        blk_half = sem("blk_half")
        h_added = sem("h_added")
        h_scaled = sem("h_scaled")
        proj_set = sem("proj_set")
        f1_done, f1_copied, f2_done, f2_copied, f3_done, f3_hi, f3_lo = (
            sem(n) for n in ("f1_done", "f1_copied", "f2_done", "f2_copied", "f3_done", "f3_hi", "f3_lo"))
        qk_turned, qk_copied, scores_done, scores_biased, max_set, exps_done = (
            sem(n) for n in ("qk_turned", "qk_copied", "scores_done", "scores_biased", "max_set", "exps_done"))
        probs_summed, den_inverted, probs_ready, probs_turned, probsT_copied, pv_done, pv_hi, pv_lo = (
            sem(n) for n in ("probs_summed", "den_inverted", "probs_ready", "probs_turned",
                             "probsT_copied", "pv_done", "pv_hi", "pv_lo"))
        gain_set = sem("gain_set")
        in_set = sem("in_set")
        lr_turned, lr_copied, la_step, kdec_exp, cum_done, cum_exp, qe_done = (
            sem(n) for n in ("lr_turned", "lr_copied", "la_step", "kdec_exp", "cum_done", "cum_exp", "qe_done"))
        gsc_done, gsc_kept, state_step, o_copied = (
            sem(n) for n in ("gsc_done", "gsc_kept", "state_step", "o_copied"))
        sc_zeroed = sem("sc_zeroed")
        conv_step, conv_hi, conv_lo = sem("conv_step"), sem("conv_hi"), sem("conv_lo")
        o_mean, o_root, o_rstd, o_gated = sem("o_mean"), sem("o_root"), sem("o_rstd"), sem("o_gated")
        final_set = sem("final_set")

        C_IN = ("k", "l", "v0", "v1")
        X_IN = ("cc0", "cx0", "cb0", "cc1", "cx1", "cb1", "k", "l", "q", "v0", "v1", "g0", "g1")
        COLS = {"l": OFF_L, "k": OFF_K, "v0": OFF_V, "v1": OFF_V + NB, "q": OFF_Q,
                "cc0": OFF_CC, "cc1": OFF_CC + NB, "cx0": OFF_CX, "cx1": OFF_CX + NB,
                "cb0": OFF_CB, "cb1": OFF_CB + NB, "g0": OFF_G, "g1": OFF_G + NB}
        SPREAD = (2, 1, 1, 1, 1, 1, 1, 0)
        TILED = (2, 3, 0, 1)
        CHUNKS = (4, 4, 3)
        IN_SET, stored = ({}, {}), 0
        for names, values in zip((C_IN, X_IN), IN_SET):
            for name in names:
                if name[:2] != "cx":
                    stored += 1
                    values[name] = stored
        BESIDE = ({("l", 1): (("half_norm", 0, 0, 0),), ("v0", 0): (("mid_norm", 0, 0, 0),),
                   ("v0", 1): (("mid_norm", 0, 1, 0),),
                   ("v0", 2): (("x_squares", 0, 0, 0),), ("v0", 3): (("x_squares", 0, 2, 0),),
                   ("v1", 1): (("x_norm", 0, 0, 0),)}, {})
        BESIDE[1].update({
            ("cc0", 3): (("rank", 0, 0, 0),),
            ("cx0", 0): (("z", 0, 0, 0), ("z", 0, 0, 1)), ("cx0", 1): (("z", 0, 1, 0), ("z", 0, 1, 1)),
            ("cx0", 2): (("suffix", 0, 0, 0), ("suffix", 0, 0, 1)), ("cx0", 3): (("suffix", 0, 1, 0), ("suffix", 0, 1, 1)),
            ("cb0", 0): (("cum", 0, 0, 0),), ("cb0", 1): (("state", 0, 0, 0),),
            ("cb0", 2): (("state", 0, 0, 1), ("cum", 0, 1, 0)), ("cb0", 3): (("state", 0, 1, 0),),
            ("cc1", 0): (("conv", 1, 0, 0),), ("cc1", 1): (("conv", 1, 0, 1),),
            ("cc1", 2): (("state", 0, 1, 1), ("cum", 0, 2, 0)), ("cc1", 3): (("state", 0, 2, 0),),
            ("cx1", 0): (("state", 0, 2, 1), ("cum", 0, 3, 0)), ("cx1", 1): (("state", 0, 3, 0),),
            ("cx1", 2): (("state", 0, 3, 1),),
            ("k", 0): (("conv", 1, 1, 0),), ("k", 1): (("conv", 1, 1, 1),),
            ("q", 0): (("rank", 1, 0, 0),),
            ("q", 1): (("z", 1, 0, 0), ("z", 1, 0, 1)), ("q", 2): (("z", 1, 1, 0), ("z", 1, 1, 1)),
            ("q", 3): (("suffix", 1, 0, 0), ("suffix", 1, 0, 1)), ("v0", 0): (("suffix", 1, 1, 0), ("suffix", 1, 1, 1)),
            ("v0", 3): (("cum", 1, 0, 0), ("turn", 1, 0, 0)),
            ("v1", 0): (("scores", 1, 0, 0), ("state", 1, 0, 0)), ("v1", 1): (("state", 1, 0, 1),),
            ("v1", 2): (("out", 1, 0, 0), ("cum", 1, 1, 0), ("turn", 1, 1, 0)),
            ("v1", 3): (("scores", 1, 1, 0), ("state", 1, 1, 0)), ("g0", 0): (("state", 1, 1, 1),),
            ("g0", 1): (("out", 1, 1, 0), ("cum", 1, 2, 0), ("turn", 1, 2, 0)),
            ("g0", 2): (("scores", 1, 2, 0), ("state", 1, 2, 0)), ("g0", 3): (("state", 1, 2, 1),),
            ("g1", 0): (("out", 1, 2, 0), ("cum", 1, 3, 0), ("turn", 1, 3, 0)),
            ("g1", 1): (("scores", 1, 3, 0), ("state", 1, 3, 0)), ("g1", 2): (("state", 1, 3, 1),),
            ("g1", 3): (("out", 1, 3, 0),),
        })
        MOD_PAIRS = ({"v0": (0, 0), "v1": (0, 1)},
                     {"cx0": (1, 0), "cb0": (1, 1), "cc1": (2, 0), "cx1": (2, 1), "cb1": (3, 0), "k": (3, 1)})
        ORDER = ((0, 1, 2, 3), (3, 2, 1, 0))
        BANKS = {"z": 1, "suffix": 1, "state": 2, "turn": 1, "out": 1, "conv": 2}
        T_O = 8 + 8 + 8 * MLP_CHUNKS + 8 + 8 + 4 + sum(
            BANKS.get(step[0], 0) for steps in BESIDE[1].values() for step in steps)
        H_MLP = H0 + 4 + 4 * MLP_CHUNKS
        H_ALL = H_MLP + 4 + 4 * len(CHUNKS)
        block = ctx.enter_context(nc.Block())

        @block.sync
        def _(sp):
            c = Counts()

            def load(src, kts=KG, width=NB):
                sp.wait_ge(lo_done, c.at("g", 1))
                dst = wring[:, c.slot("g", WSLOTS), 0:kts * width].rearrange("p (k n) -> p k n", k=kts)
                sp.dma_start(dst, src).then_inc(group_landed[c.slot("g", WSLOTS)], 16)
                c.add("g")

            def block_of(w, col, kgroups=KT // KG, kg0=0, order=None):
                v = w.rearrange("(g k p) n -> g p k n", k=KG, p=P)
                for kg in order or range(kgroups):
                    if isinstance(kg0, int):
                        load(v[kg0 + kg, :, :, bass.ds(col, NB)])
                    else:
                        load(v[bass.ds(kg0 + kg, 1), :, :, bass.ds(col, NB)].rearrange("a p k n -> (a p) k n"))

            sp.dma_start(h[:, 0, :], x[0:P, :]).then_inc(x_in, 16)
            sp.dma_start(h[:, 1, :], x[P:2 * P, :]).then_inc(x_in, 16)
            with c.loop(sp, 4, g=8) as i:
                for j in range(2):
                    block_of(w_in, i * (2 * NB) + j * NB)
            with c.loop(sp, 2, g=8) as i:
                for j in range(2):
                    block_of(w_out, i * (2 * NB) + j * NB)
            with c.loop(sp, MLP_CHUNKS, g=32) as i:
                for j in range(4):
                    block_of(w_up, i * D + j * NB)
                for n in range(4):
                    block_of(w_down, n * NB, kg0=i * 4)
            for names in (C_IN, X_IN):
                for name in names:
                    if name == "l":
                        v = w_in2.rearrange("(g k p) n -> g p k n", k=8, p=P)
                        for half in range(2):
                            load(v[half, :, :, OFF_L:OFF_L + RANK2], 8, RANK2)
                    else:
                        block_of(w_in2, COLS[name])
            for n in range(4):
                block_of(w_out2, n * NB, order=TILED)

            def ffn(i, blocks):
                for j in range(blocks):
                    block_of(w_gate, i * D + j * NB)
                    block_of(w_up2, i * D + j * NB)
                for n in range(4):
                    block_of(w_down2, n * NB, kgroups=blocks, kg0=i * 4)

            with c.loop(sp, 2, g=48) as i:
                ffn(i, 4)
            ffn(2, 3)

        @block.gpsimd
        def _(pool):
            c = Counts()
            pool.memset(ones[:, :], 1.0).then_inc(pool_set, 1)
            pool.wait_ge(x_in, 32)
            pool.dma_start(tab_f[:, :, :], fourier_tables).then_inc(misc_in, 16)
            pool.dma_start(tab_a[:, :, :], attn_tables).then_inc(misc_in, 16)
            for g in range(FGROUPS):
                pool.dma_start(wf[:, g, :, :], w_fourier[g].rearrange("(c p) e -> p c e", p=P)).then_inc(misc_in, 16)
            w_mod_v = w_mod.rearrange("(s k p) n -> s p k n", k=2, p=P)

            def mod_block(kind, i, per_step, last_step):
                for s in range(MSTEPS):
                    pool.wait_ge(mod_acc, c.at("ma", 8 - (last_step if s == 0 else per_step)))
                    pool.dma_start(mring[:, c.slot("m", MSLOTS), :, :],
                                   w_mod_v[s, :, :, bass.ds(i * NB + kind * D, NB)])\
                        .then_inc(step_landed[c.slot("m", MSLOTS)], 16)
                    c.add("m")
                    c.add("ma", per_step)

            with c.loop(pool, 4, m=8, ma=32) as i:
                mod_block(SH1, i, 4, 4)
            pool.wait_ge(tp_free, 2 + 16)
            pool.dma_start(u_g[:, :, :], ctx_in.rearrange("(t p) d -> p t d", p=P)).then_inc(ctx_in_s, 16)
            pool.dma_start(mgain[:, :], mid_g.rearrange("(a n) -> a n", a=1).partition_broadcast(P)).then_inc(mg_in, 16)
            with c.loop(pool, MLP_CHUNKS, m=32, ma=80) as i:
                mod_block(SC2, i, 2, 2)
                mod_block(SC1, i, 4, 2)
                mod_block(GT1, i, 2, 4)
                mod_block(SH2, i, 2, 2)
            pool.wait_ge(h_added, H_MLP)
            pool.dma_start(wg[:, :, :], gates_w).then_inc(wg_in, 16)
            pool.memset(lrank[:, :, :], 0.0).then_inc(pool_set, 1)
            pool.wait_ge(pool_set, 2)
            pool.memset(lrank[:, :, RANK2:RANK2 + 1], 1.0).then_inc(pool_set, 1)
            with c.loop(pool, 4, m=8, ma=16) as i:
                mod_block(GT2, i, 2, 2)
            pool.wait_ge(tp_ready, T_O)
            pool.wait_ge(spill_s, 16)
            pool.dma_start(h[:, :, :], hspill.rearrange("t p d -> p t d")).then_inc(reload_s, 16)
            pool.dma_start(fgain[:, :], final_g.rearrange("(a n) -> a n", a=1).partition_broadcast(P))\
                .then_inc(fg_in, 16)

        @block.scalar
        def _(act):
            c = Counts()

            def round_groups(n, size=KG * NB):
                for _ in range(n):
                    g4, g2 = c.slot("g", WSLOTS), c.slot("g", HSLOTS)
                    act.wait_ge(group_landed[g4], c.landed("g", WSLOTS))
                    act.wait_ge(group_multiplied, c.at("g", 1))
                    act.activation(whi[:, g2, 0:size], wring[:, g4, 0:size], ACT.Copy).then_inc(hi_done, 1)
                    c.add("g")

            def wait_block(back):
                act.wait_ge(group_multiplied, c.at("g", HSLOTS - back))

            def round_banks(dst, tile, banks, gain=None):
                for b in range(banks):
                    src = tp[:, c.slot("q", 2), :].rearrange("p (j s) -> p j s", j=2)
                    act.wait_ge(tp_ready, c.at("q", 1))
                    t0 = tile + 2 * b
                    if gain is None:
                        act.activation(dst[:, t0:t0 + 2, :], src, ACT.Copy).then_inc(tp_hi, 1)
                    else:
                        act.activation(dst[:, t0, :], src[:, 0, :], ACT.Copy, scale=gain(t0)).then_inc(tp_hi, 1)
                        act.activation(dst[:, t0 + 1, :], src[:, 1, :], ACT.Copy, scale=gain(t0 + 1)).then_inc(tp_hi, 1)
                    c.add("q")

            def round_modulated(dst, b0, b1):
                for b in range(b0, b1):
                    act.wait_ge(tp_tmp, c.at("tmp", 1))
                    act.activation(dst[:, 2 * b:2 * b + 2, :],
                                   tmpT[:, b % 2, :].rearrange("p (j s) -> p j s", j=2), ACT.Copy).then_inc(tp_hi, 1)
                    c.add("tmp")
                    c.add("q")

            def opening(banks):
                banks(0, 6)
                round_groups(1)
                banks(6, 8)
                round_groups(1)

            def square(src, col, piece, junk=m0):
                for t in range(T):
                    if c.n.get("ssq", 0):
                        act.wait_ge(ssq_done, c.at("ssq"))
                    act.activation(junk[:, :], src[:, t, bass.ds(col, NB)], ACT.Square,
                                   accum_out=squares[:, t, bass.ds(piece, 1)]).then_inc(ssq_done, 1)
                    c.add("ssq")

            def square_added(col, piece):
                act.wait_ge(h_added, c.at("ha", 1))
                square(h, col, piece)
                c.add("ha")

            def root(n):
                act.wait_ge(mean_done, n + 1)
                act.activation(ssq[:, n, :], ssq[:, n, :], ACT.Sqrt).then_inc(root_done, 1)

            def root_and_scale(n, src, dst):
                root(n)
                act.wait_ge(rstd_done, n + 1)
                act.activation(dst[:, 1, :], src[:, 1, :], ACT.Copy, scale=rstd[:, n, 1:2]).then_inc(u_done, 1)

            def norm(n, src, dst, junk=m0):
                for piece in range(KG):
                    square(src, piece * NB, piece, junk)
                root_and_scale(n, src, dst)

            act.dma_start(vrows[:, :, :], vectors).then_inc(start_in, 16)
            act.dma_start(tabs[:, :, :], tables).then_inc(start_in, 16)
            act.sem_inc(proj_set, 2)
            act.wait_ge(x_in, 32)
            norm(0, h, u_mix, acc[:, 0, :])
            act.wait_ge(vec_set, 1)
            act.activation(csil[:, :, :].rearrange("p w k -> p (w k)"), vecs[:, 0, V_C:V_C + 2 * KT],
                           ACT.Exp, scale=-1.0).then_inc(c_exp, 1)
            round_groups(2)
            c.n["ha"] = H0

            def w_in_pair(i, first=False):
                for j in range(2):
                    if first and j == 0:
                        opening(lambda b0, b1: round_banks(xhi, 2 * b0, b1 - b0,
                                                           lambda k: vecs[:, 0, V_MIXG + k:V_MIXG + k + 1]))
                    else:
                        round_groups(2)
                    round_groups(2)
                    wait_block(2)
                    act.activation(proj[:, :, bass.ds(i * (2 * NB) + j * NB, NB)], acc[:, 2 * j:2 * j + 2, :],
                                   ACT.Copy).then_inc(proj_set, 1)

            w_in_pair(0, True)
            with c.loop(act, 4, 1, g=8) as i:
                w_in_pair(i)

            act.wait_ge(misc_in, 16 * 6)
            for s in range(HEADS + 1):
                g = s // 2
                if s < HEADS:
                    act.wait_ge(qk_turned, s + 1)
                    if s >= 2:
                        act.wait_ge(scores_done, s - 1)
                    act.activation(qkT[:, s % 2, 0, :], tp[:, 0, 0:S], ACT.Copy, scale=HD ** -0.5).then_inc(qk_copied, 1)
                    act.activation(qkT[:, s % 2, 1, :], tp[:, 0, S:2 * S], ACT.Copy).then_inc(qk_copied, 1)
                if s < HEADS and s % 2 == 0:
                    act.wait_ge(f1_done, g + 1)
                    if g:
                        act.wait_ge(f2_done, g)
                    act.activation(fpos[:, :, :], acc[:, 0:2, :], ACT.Copy).then_inc(f1_copied, 1)
                if s % 2:
                    act.wait_ge(f2_done, g + 1)
                    if g:
                        act.wait_ge(f3_done, g)
                    act.activation(fre, m0[:, :].rearrange("p (c s) -> p c s", c=2), ACT.Copy).then_inc(f2_copied, 1)
                if s:
                    act.wait_ge(probs_turned, s)
                    if s >= 2:
                        act.wait_ge(pv_done, s - 1)
                    act.activation(probsT, tp[:, 1, :].rearrange("p (c s) -> p c s", c=2), ACT.Copy).then_inc(probsT_copied, 1)
                if s < HEADS:
                    act.wait_ge(max_set, s + 1)
                    for t in range(T):
                        act.activation(probs[:, t * S:(t + 1) * S], sbias[:, t * S:(t + 1) * S], ACT.Exp,
                                       bias=nmax[:, s, t:t + 1]).then_inc(exps_done, 1)
                if s % 2:
                    act.wait_ge(f3_done, g + 1)
                    act.activation(xhi[:, 2 * g:2 * g + 2, :], m1[:, :].rearrange("p (c s) -> p c s", c=2),
                                   ACT.Copy).then_inc(f3_hi, 1)
                if s:
                    act.wait_ge(pv_done, s)
                    act.activation(xhi[:, 7 + s, :], acc[:, 3, 0:S], ACT.Copy).then_inc(pv_hi, 1)

            def added_pair(i):
                round_groups(5)
                square_added(i * (2 * NB), i * 2)
                round_groups(3)
                square_added(i * (2 * NB) + NB, i * 2 + 1)

            with c.loop(act, 2, g=8, ha=2, ssq=2 * T) as i:
                added_pair(i)
            root_and_scale(1, h, u_mlp)

            def relu_square(j):
                act.activation(blk2[:, :, :], acc[:, 2 * (j % 2):2 * (j % 2) + 2, :], ACT.Relu).then_inc(blk_half, 1)
                c.add("half")
                act.wait_ge(blk_half, c.at("half"))
                act.activation(blk[:, :, :], blk2[:, :, :], ACT.Square).then_inc(blk_ready, 1)
                c.add("blk")

            def mlp_chunk(first=False):
                for j in range(8):
                    if first and j == 0:
                        opening(lambda b0, b1: round_banks(xhi, 2 * b0, b1 - b0,
                                                           lambda k: vecs[:, 0, V_MLPG + k:V_MLPG + k + 1]))
                    else:
                        round_groups(1)
                        if j >= 5:
                            square_added((j - 5) * NB, j - 5)
                        round_groups(1)
                    if 1 <= j <= 4:
                        round_banks(ahi, 4 * (j - 1), 2)
                    round_groups(2)
                    if j < 4:
                        wait_block(2)
                        relu_square(j)
                square_added(3 * NB, 3)

            mlp_chunk(True)
            act.wait_ge(ctx_in_s, 16)
            norm(2, u_g, u_g)
            with c.loop(act, MLP_CHUNKS, 1, g=32, q=8, half=4, blk=4, ha=4, ssq=4 * T):
                mlp_chunk()

            def store_block(name, pair, x_pass):
                src = acc[:, 2 * pair:2 * pair + 2, :]
                if x_pass and name == "k":
                    act.wait_ge(state_step, STATE_STEPS[0] * GH)
                if name == "l":
                    act.wait_ge(pool_set, 3)
                    act.activation(lrank[:, :, 0:RANK2], src[:, :, 0:RANK2], ACT.Copy).then_inc(in_set, 1)
                elif name == "k":
                    act.activation(gk[:, :, :], src, ACT.Copy).then_inc(in_set, 1)
                elif name in ("v0", "v1"):
                    o = NB * int(name[1])
                    act.activation(gv[:, :, o:o + NB], src, ACT.Copy).then_inc(in_set, 1)
                elif name == "q":
                    act.activation(gq[:, :, :], src, ACT.Copy).then_inc(in_set, 1)
                elif name in ("cc0", "cc1"):
                    if name == "cc1":
                        act.wait_ge(tp_ready, c.at("q"))
                    act.activation(blk[:, :, :], src, ACT.Copy).then_inc(in_set, 1)
                elif name in ("cb0", "cb1"):
                    act.activation(blk2[:, :, :], src, ACT.Copy).then_inc(in_set, 1)
                elif name in ("g0", "g1"):
                    o = NB * int(name[1])
                    act.activation(silg[:, :, o:o + NB], src, ACT.Silu).then_inc(in_set, 1)

            def step(kind, p, a, b):
                if kind == "half_norm":
                    root(3)
                elif kind == "x_squares":
                    if a == 0:
                        act.wait_ge(u_done, 4 * T)
                        act.dma_start(hspill.rearrange("t p d -> p t d"), h[:, :, :]).then_inc(spill_s, 16)
                    for piece in (a, a + 1):
                        square(h, piece * NB, piece)
                elif kind == "x_norm":
                    act.wait_ge(spill_s, 16)
                    root_and_scale(4, h, h)
                elif kind == "rank":
                    act.wait_ge(lr_turned, p + 1)
                    act.activation(lrankT[:, :], m0[:, 0:S], ACT.Copy).then_inc(lr_copied, 1)
                elif kind == "z":
                    act.wait_ge(tp_ready, c.at("q", 1))
                    act.activation(la[:, a, b], tp[:, c.slot("q", 2), :], ACT.Abs).then_inc(la_step, 1)
                    act.wait_ge(la_step, c.at("la", 1))
                    act.activation(la[:, a, b], la[:, a, b], ACT.Exp, scale=-1.0).then_inc(la_step, 1)
                    act.wait_ge(la_step, c.at("la", 2))
                    act.activation(la[:, a, b], la[:, a, b], ACT.Ln, bias=1.0).then_inc(la_step, 1)
                    c.add("la", 3)
                elif kind == "suffix":
                    act.wait_ge(tp_ready, c.at("q", 1))
                    act.activation(kdec[:, a, b], tp[:, c.slot("q", 2), :], ACT.Exp).then_inc(kdec_exp, 1)
                elif kind == "cum":
                    hd = a
                    act.wait_ge(cum_done, GH * p + hd + 1)
                    if p or hd:
                        act.wait_ge(state_step, STATE_STEPS[p] * hd + STATE_STEPS[0] * GH * p)
                    if p and hd:
                        act.wait_ge(qe_done, 4 * hd)
                    act.activation(epos[:, :, :], m0[:, :].rearrange("p (d s) -> p d s", d=2), ACT.Exp).then_inc(cum_exp, 1)
                    if p:
                        act.activation(eneg, m0[:, :].rearrange("p (d s) -> p d s", d=2), ACT.Exp, scale=-1.0).then_inc(cum_exp, 1)
                elif kind == "out":
                    act.wait_ge(tp_ready, c.at("q", 1))
                    for t in range(T):
                        o = tp[:, c.slot("q", 2), t * DV:(t + 1) * DV]
                        act.activation(o_all[:, t, a * DV:(a + 1) * DV], o, ACT.Copy).then_inc(o_copied, 1)
                        act.activation(tmpT[:, 1, t * DV:(t + 1) * DV], o, ACT.Square,
                                       accum_out=oss[:, t, a:a + 1]).then_inc(o_copied, 1)
                c.add("q", BANKS.get(kind, 0))

            def in_blocks(names, b0, p):
                for n, name in enumerate(names):
                    following = (names + (("w_out",) if p else ("cc0",)))[n + 1]
                    if n == 0:
                        opening(lambda b0, b1: round_modulated(xhi, b0, b1))
                    for kg in range(2 if name == "l" else 4):
                        last = kg == (1 if name == "l" else 3)
                        if name == "l":
                            round_groups(1)
                        elif n == 0 and kg < 2:
                            continue
                        elif kg < 2:
                            round_groups(1)
                        else:
                            round_groups(1, 8 * RANK2 if following == "l" else KG * NB)
                        if last:
                            wait_block(2)
                            store_block(name, (b0 + n) % 2, p)
                        for st in BESIDE[p].get((name, kg), ()):
                            step(*st)

            in_blocks(C_IN, 44, 0)
            in_blocks(X_IN, 48, 1)
            act.wait_ge(conv_step, 8 * 4)
            act.activation(xhi[:, 8:16, :], convT[:, :, :], ACT.Copy).then_inc(conv_hi, 1)
            act.wait_ge(o_mean, 1)
            act.activation(oss[:, :, :], oss[:, :, :], ACT.Sqrt).then_inc(o_root, 1)
            round_banks(xhi, 0, 4, lambda k: vecs[:, 2, 24 + k % 2:25 + k % 2])

            c.add("q", 8)
            with c.loop(act, 2, g=8, ha=2, ssq=2 * T) as i:
                added_pair(i)
            root_and_scale(5, h, u_ffn)

            def silu_gate(pair):
                act.wait_ge(blk_ready, c.at("blk"))
                act.wait_ge(h_added, c.at("ha"))
                act.activation(blk2[:, :, :], acc[:, 2 * pair:2 * pair + 2, :], ACT.Silu).then_inc(blk_half, 1)
                c.add("half")

            def ffn(blocks, first=False):
                for j in range(blocks):
                    if first and j == 0:
                        opening(lambda b0, b1: round_modulated(xhi, b0, b1))
                    else:
                        round_groups(2)
                    if j:
                        round_banks(bhi, 4 * (j - 1), 2)
                    round_groups(2)
                    wait_block(2)
                    silu_gate(0)
                    round_groups(4)
                    c.add("blk")
                for n in range(4):
                    last = blocks < 4
                    round_groups(blocks - 2)
                    if n == 0:
                        round_banks(bhi, 4 * (blocks - 1), 2)
                    if last and n:
                        square_added((n - 1) * NB, n - 1)
                    if not (last and n == 3):
                        round_groups(2)
                if last:
                    square_added(3 * NB, 3)
                else:
                    c.add("ha", 4)

            c.n["blk"] = 4 * MLP_CHUNKS + 2
            ffn(4, True)
            with c.loop(act, 2, 1, g=48, q=8, half=4, blk=4, ha=4):
                ffn(4)
            ffn(3)
            root(6)
            act.wait_ge(fg_in, 16)
            for t in range(T):
                act.wait_ge(final_set, t + 1)
                act.dma_start(out[t * P:(t + 1) * P, :], u_ffn[:, t, :]).then_inc(out_s, 16)
            act.wait_ge(out_s, 32)

        @block.vector
        def _(dve):
            c = Counts()

            def remainders(n, size=KG * NB):
                for _ in range(n):
                    g4, g2 = c.slot("g", WSLOTS), c.slot("g", HSLOTS)
                    dve.wait_ge(hi_done, c.at("g", 1))
                    dve.tensor_tensor(wlo[:, g2, 0:size], wring[:, g4, 0:size], whi[:, g2, 0:size].bitcast(F32),
                                      ALU.subtract).then_inc(lo_done, 1)
                    c.add("g")

            def wait_block(back):
                dve.wait_ge(group_multiplied, c.at("g", HSLOTS - back))

            def mod_steps(n, s0, dual):
                for s in range(s0, s0 + n):
                    m2 = c.slot("m", MSLOTS)
                    dve.wait_ge(step_landed[m2], c.landed("m", MSLOTS))
                    for kt in range(2):
                        k = 2 * s + kt
                        for who in range(2 if dual else 1):
                            if k == 0:
                                dve.tensor_scalar(macc[:, who, :], mring[:, m2, kt, :], csil[:, who, k:k + 1], None,
                                                  ALU.mult).then_inc(mod_acc, 1)
                            else:
                                dve.wait_ge(mod_acc, c.at("ma", 8 - (1 if dual else 0)))
                                dve.scalar_tensor_tensor(macc[:, who, :], mring[:, m2, kt, :], csil[:, who, k:k + 1],
                                                         macc[:, who, :], ALU.mult, ALU.add).then_inc(mod_acc, 1)
                            c.add("ma")
                    c.add("m")

            def set_mod(kind, i, dual):
                dve.wait_ge(mod_reduced, c.at("mb", 1))
                for who in range(2 if dual else 1):
                    dve.tensor_tensor(modT[:, who, bass.ds(i * 4 + kind * KT, 4)], m1[:, 4 * who:4 * who + 4],
                                      vecs[:, 1, bass.ds(i * 4 + kind * KT, 4)], ALU.add).then_inc(mod_set, 1)
                c.add("mb")

            def remain_banks(hi, lo, tile, banks, gain=None):
                for b in range(banks):
                    src = tp[:, c.slot("q", 2), :].rearrange("p (j s) -> p j s", j=2)
                    t0 = tile + 2 * b
                    dve.wait_ge(tp_hi, c.at("hi", 1 if gain is None else 2))
                    c.add("hi", 1 if gain is None else 2)
                    if gain is None:
                        dve.tensor_tensor(lo[:, t0:t0 + 2, :], src, hi[:, t0:t0 + 2, :].bitcast(F32), ALU.subtract).then_inc(tp_free, 1)
                    else:
                        dve.scalar_tensor_tensor(lo[:, t0, :], src[:, 0, :], gain(t0), hi[:, t0, :].bitcast(F32),
                                                 ALU.mult, ALU.subtract)
                        dve.scalar_tensor_tensor(lo[:, t0 + 1, :], src[:, 1, :], gain(t0 + 1), hi[:, t0 + 1, :].bitcast(F32),
                                                 ALU.mult, ALU.subtract).then_inc(tp_free, 1)
                    c.add("q")

            def opening(banks):
                banks(0, 6)
                remainders(1)
                banks(6, 8)
                remainders(1)

            def modulate(hi, lo, b0, b1, gain, shift):
                def remainder(b):
                    dve.wait_ge(tp_hi, c.at("hi", 1))
                    dve.tensor_tensor(lo[:, 2 * b:2 * b + 2, :], tmpT[:, b % 2, :].rearrange("p (j s) -> p j s", j=2),
                                      hi[:, 2 * b:2 * b + 2, :].bitcast(F32), ALU.subtract).then_inc(tp_free, 1)
                    c.add("hi")

                for b in range(b0, b1):
                    q = c.slot("q", 2)
                    dve.wait_ge(tp_ready, c.at("q", 1))
                    dve.tensor_scalar(tmpT[:, b % 2, 0:S], tp[:, q, 0:S], gain(2 * b), shift(2 * b), ALU.mult, ALU.add)
                    dve.tensor_scalar(tmpT[:, b % 2, S:2 * S], tp[:, q, S:2 * S], gain(2 * b + 1), shift(2 * b + 1),
                                      ALU.mult, ALU.add).then_inc(tp_tmp, 1)
                    c.add("q")
                    if b > b0:
                        remainder(b - 1)
                remainder(b1 - 1)

            def norm_root(n):
                dve.wait_ge(ssq_done, c.at("ssq"))
                dve.reduce_sum(ssq[:, n, :], squares[:, :, :], AX_X).then_inc(squares_summed, 1)
                dve.wait_ge(squares_summed, n + 1)
                dve.tensor_scalar(ssq[:, n, :], ssq[:, n, :], 1.0 / D, EPS, ALU.mult, ALU.add).then_inc(mean_done, 1)
                dve.wait_ge(root_done, n + 1)
                dve.reciprocal(rstd[:, n, :], ssq[:, n, :]).then_inc(rstd_done, 1)
                dve.wait_ge(rstd_done, n + 1)

            def norm_scale(n, src, dst):
                norm_root(n)
                dve.tensor_scalar(dst[:, 0, :], src[:, 0, :], rstd[:, n, 0:1], None, ALU.mult).then_inc(u_done, 1)

            dve.sem_inc(mod_acc, 8)
            dve.sem_inc(lo_done, WSLOTS)
            dve.sem_inc(h_added, H0)
            dve.sem_inc(tp_free, 2)
            dve.wait_ge(x_in, 32)
            c.add("ssq", T * KG)
            norm_scale(0, h, u_mix)
            dve.wait_ge(vec_turned, 3)
            dve.tensor_copy(vecs[:, :, :], m0[:, 0:3 * P].rearrange("p (a b) -> p a b", a=3)).then_inc(vec_set, 1)
            dve.wait_ge(c_exp, 1)
            csil_flat = csil[:, :, :].rearrange("p w k -> p (w k)")
            dve.tensor_scalar(csil_flat, csil_flat, 1.0, None, ALU.add).then_inc(c_sil, 1)
            dve.wait_ge(c_sil, 1)
            dve.reciprocal(csil_flat, csil_flat).then_inc(c_sil, 1)
            dve.wait_ge(c_sil, 2)
            dve.tensor_tensor(csil_flat, csil_flat, vecs[:, 0, V_C:V_C + 2 * KT], ALU.mult).then_inc(c_sil, 1)
            dve.wait_ge(c_sil, 3)
            remainders(2)

            def w_in_pair(i, first=False):
                s = 0
                for g in range(8):
                    if first and g == 0:
                        opening(lambda b0, b1: remain_banks(xhi, xlo, 2 * b0, b1 - b0,
                                                            lambda k: vecs[:, 0, V_MIXG + k:V_MIXG + k + 1]))
                        mod_steps(2, 0, True)
                    elif not (first and g == 1):
                        remainders(1)
                        mod_steps(SPREAD[g], s, True)
                    s += SPREAD[g]
                    if first and g == 1:
                        mod_steps(1, 2, True)
                set_mod(SH1, i, True)

            w_in_pair(0, True)
            with c.loop(dve, 4, 1, g=8, m=8, ma=32, mb=1) as i:
                w_in_pair(i)

            dve.wait_ge(misc_in, 16 * 6)
            for s in range(HEADS + 1):
                g = s // 2
                if s < HEADS:
                    dve.wait_ge(scores_done, s + 1)
                    if s:
                        dve.wait_ge(exps_done, T * s)
                    dve.scalar_tensor_tensor(sbias, tab_a[:, 0, :], 2.0 ** (-8.0 * (s + 1) / HEADS), acc[:, 2, :],
                                             ALU.mult, ALU.add).then_inc(scores_biased, 1)
                    dve.wait_ge(scores_biased, s + 1)
                    dve.reduce_max(nmax[:, s, :], sbias.rearrange("p (t k) -> p t k", t=T), AX_X, negate=True).then_inc(max_set, 1)
                if s % 2:
                    dve.wait_ge(f3_hi, g + 1)
                    dve.tensor_tensor(xlo[:, 2 * g:2 * g + 2, :], m1[:, :].rearrange("p (c s) -> p c s", c=2),
                                      xhi[:, 2 * g:2 * g + 2, :].bitcast(F32), ALU.subtract).then_inc(f3_lo, 1)
                if s:
                    dve.wait_ge(pv_hi, s)
                    dve.tensor_tensor(xlo[:, 7 + s, :], acc[:, 3, 0:S], xhi[:, 7 + s, :].bitcast(F32),
                                      ALU.subtract).then_inc(pv_lo, 1)
                if s < HEADS:
                    for t in range(T):
                        dve.wait_ge(exps_done, T * s + t + 1)
                        dve.scalar_tensor_tensor(probs[:, t * S:(t + 1) * S], probs[:, t * S:(t + 1) * S], 1.0,
                                                 tab_a[:, 1, t * S:(t + 1) * S], ALU.mult, ALU.mult,
                                                 accum_out=aden[:, s, t:t + 1]).then_inc(probs_summed, 1)
                    dve.wait_ge(probs_summed, T * (s + 1))
                    dve.reciprocal(arden[:, s, :], aden[:, s, :]).then_inc(den_inverted, 1)
                    dve.wait_ge(den_inverted, s + 1)
                    for t in range(T):
                        dve.tensor_scalar(probs[:, t * S:(t + 1) * S], probs[:, t * S:(t + 1) * S],
                                          arden[:, s, t:t + 1], None, ALU.mult).then_inc(probs_ready, 1)

            def add_block(n, pair):
                dve.tensor_tensor(h[:, :, bass.ds(n, NB)], acc[:, 2 * pair:2 * pair + 2, :], h[:, :, bass.ds(n, NB)],
                                  ALU.add).then_inc(h_added, 1)

            with c.loop(dve, 2, g=8) as i:
                for pair in range(2):
                    remainders(3)
                    wait_block(1)
                    add_block(i * (2 * NB) + pair * NB, pair)
                    remainders(1)
            c.add("ssq", T * KG)
            norm_scale(1, h, u_mlp)

            def mlp_chunk(i, first=False):
                kinds = ((SC2, False), (SC1, True), (GT1, False), (SH2, False))
                for t in range(4):
                    s = 0
                    for g in range(8):
                        j = 2 * t + g // 4
                        if first and j == 0 and g < 2:
                            if g == 0:
                                opening(lambda b0, b1: remain_banks(xhi, xlo, 2 * b0, b1 - b0,
                                                                    lambda k: vecs[:, 0, V_MLPG + k:V_MLPG + k + 1]))
                        else:
                            remainders(1)
                        mod_steps(SPREAD[g], s, kinds[t][1])
                        s += SPREAD[g]
                        if g % 4 == 1 and 1 <= j <= 4:
                            remain_banks(ahi, alo, 4 * (j - 1), 2)
                        if g % 4 == 3 and j >= 4:
                            wait_block(2)
                            add_block((j - 4) * NB, j % 2)
                    set_mod(kinds[t][0], i, kinds[t][1])

            mlp_chunk(0, True)
            c.add("ssq", 2 * T * KG)
            dve.wait_ge(ctx_in_s, 16)
            norm_scale(2, u_g, u_g)
            with c.loop(dve, MLP_CHUNKS, 1, g=32, q=8, hi=8, m=32, ma=80, mb=4) as i:
                mlp_chunk(i)
            c.add("ssq", (MLP_CHUNKS - 1) * T * KG)

            def store_block(name, pair):
                src = acc[:, 2 * pair:2 * pair + 2, :]
                if name in ("cx0", "cx1"):
                    dve.wait_ge(in_set, IN_SET[1]["cc" + name[2]])
                    dve.tensor_tensor(blk[:, :, :], blk[:, :, :], src, ALU.mult).then_inc(blk_ready, 1)

            def conv(half, pr):
                qu, qb = c.slot("q", 2), (c.slot("q", 2) + 1) % 2
                dve.wait_ge(tp_ready, c.at("q", 2))
                for j in range(2):
                    ch = 4 * half + 2 * pr + j
                    n = 4 * ch
                    y = convT[:, ch, :]
                    yr = y.rearrange("p (r w) -> p r w", w=GRID)
                    u = tp[:, qu, j * S:(j + 1) * S]
                    ur = u.rearrange("p (r w) -> p r w", w=GRID)
                    tap = [vecs[:, 2, 8 * k + ch:8 * k + ch + 1] for k in range(3)]
                    dve.tensor_scalar(y, u, tap[1], None, ALU.mult).then_inc(conv_step, 1)
                    dve.wait_ge(conv_step, n + 1)
                    dve.scalar_tensor_tensor(yr[:, :, 1:GRID], ur[:, :, 0:GRID - 1], tap[0], yr[:, :, 1:GRID],
                                             ALU.mult, ALU.add).then_inc(conv_step, 1)
                    dve.wait_ge(conv_step, n + 2)
                    dve.scalar_tensor_tensor(yr[:, :, 0:GRID - 1], ur[:, :, 1:GRID], tap[2], yr[:, :, 0:GRID - 1],
                                             ALU.mult, ALU.add).then_inc(conv_step, 1)
                    dve.wait_ge(conv_step, n + 3)
                    dve.tensor_tensor(y, y, tp[:, qb, j * S:(j + 1) * S], ALU.mult).then_inc(conv_step, 1)
                dve.wait_ge(conv_step, n + 4)
                dve.sem_inc(tp_free, 2)
                c.add("q", 2)

            def step(kind, p, a, b):
                q = c.slot("q", 2)
                if kind == "half_norm":
                    norm_root(3)
                elif kind == "mid_norm":
                    dve.wait_ge(mg_in, 16)
                    dve.scalar_tensor_tensor(h[:, a, :], h[:, a, :], rstd[:, 3, a:a + 1], mgain[:, :],
                                             ALU.mult, ALU.mult).then_inc(u_done, 1)
                elif kind == "x_norm":
                    c.add("ssq", T * KG)
                    dve.wait_ge(spill_s, 16)
                    norm_scale(4, h, h)
                elif kind == "z":
                    dve.wait_ge(la_step, c.at("la", 3))
                    dve.scalar_tensor_tensor(la[:, a, b], tp[:, q, :], 0.0, la[:, a, b], ALU.min, ALU.subtract).then_inc(tp_free, 1)
                    c.add("la", 3)
                elif kind == "suffix":
                    dve.wait_ge(kdec_exp, c.at("kd", 1))
                    dve.tensor_tensor(kdec[:, a, b], kdec[:, a, b], gk[:, a, :], ALU.mult).then_inc(tp_free, 1)
                    c.add("kd")
                elif kind == "turn":
                    hd = a
                    dve.wait_ge(cum_exp, GH + 2 * (hd + 1))
                    dve.wait_ge(tp_ready, c.at("q", 1))
                    if hd == 0:
                        dve.memset(sc, 0.0).then_inc(sc_zeroed, 1)
                        dve.wait_ge(sc_zeroed, 1)
                    for d in range(2):
                        dve.scalar_tensor_tensor(qe[:, d, :], tp[:, q, 0:S], DK ** -0.5, epos[:, d, :],
                                                 ALU.mult, ALU.mult).then_inc(qe_done, 1)
                        dve.tensor_tensor(ke[:, d, :], tp[:, q, S:2 * S], eneg[:, d, :], ALU.mult).then_inc(qe_done, 1)
                    dve.wait_ge(qe_done, 4 * (hd + 1))
                    dve.sem_inc(tp_free, 1)
                elif kind == "scores":
                    dve.wait_ge(gsc_done, a + 1)
                    for d in range(2):
                        for t in range(T):
                            dve.copy_predicated(sc[:, d, t, :], keep[d], m1[:, (2 * d + t) * P:(2 * d + t + 1) * P]).then_inc(gsc_kept, 1)
                elif kind == "state":
                    hd, d = a, b
                    dve.wait_ge(cum_exp, hd + 1 if p == 0 else GH + 2 * (hd + 1))
                    dve.wait_ge(tp_ready, c.at("q", 2))
                    for n in range(NCH if p == 0 else NCH - 1):
                        ck = ORDER[d][n]
                        decay = epos[:, d, CH * ck + CH - 1:CH * ck + CH] if d == 0 else epos[:, d, CH * ck:CH * ck + 1]
                        ds = tp[:, (q + ck % 2) % 2, (ck // 2) * DV:(ck // 2 + 1) * DV]
                        if p == 0 and n == 0:
                            dve.tensor_copy(states[:, d, hd, :], ds).then_inc(state_step, 1)
                        else:
                            if n:
                                dve.wait_ge(state_step, c.at("st"))
                            src = gst[:, d, ck, :] if p and n else states[:, d, hd, :]
                            dst = gst[:, d, ORDER[d][n + 1], :] if p else states[:, d, hd, :]
                            dve.scalar_tensor_tensor(dst, src, decay, ds, ALU.mult, ALU.add).then_inc(state_step, 1)
                        c.add("st")
                    dve.wait_ge(state_step, c.at("st"))
                    dve.sem_inc(tp_free, 2)
                elif kind == "out":
                    dve.wait_ge(o_copied, 4 * (a + 1))
                    dve.sem_inc(tp_free, 1)
                if kind == "conv":
                    conv(a, b)
                else:
                    c.add("q", BANKS.get(kind, 0))

            def in_blocks(names, p, hi, lo, gain, shift):
                for n, name in enumerate(names):
                    following = (names + (("w_out",) if p else ("cc0",)))[n + 1]
                    if n == 0:
                        opening(lambda b0, b1: modulate(hi, lo, b0, b1, gain, shift))
                    which, part = MOD_PAIRS[p].get(name, (None, 0))
                    for kg in range(2 if name == "l" else 4):
                        last = kg == (1 if name == "l" else 3)
                        if n == 0 and kg < 2:
                            continue
                        remainders(1, 8 * RANK2 if name != "l" and kg >= 2 and following == "l" else KG * NB)
                        if last:
                            wait_block(2)
                            store_block(name, (48 + n) % 2)
                        for st in BESIDE[p].get((name, kg), ()):
                            step(*st)
                        if which is not None:
                            k = 4 * part + kg
                            mod_steps(SPREAD[k], sum(SPREAD[0:k]), False)
                            if k == 7:
                                set_mod(GT2, which, False)

            dve.wait_ge(mod_set, 8 + MLP_CHUNKS * 5)
            for who in range(2):
                dve.scalar_tensor_tensor(gain1[:, who, :], modT[:, who, SC1 * KT:(SC1 + 1) * KT], 1.0,
                                         vecs[:, 0, V_N1G:V_N1G + KT], ALU.add, ALU.mult).then_inc(gain_set, 1)
            dve.wait_ge(gain_set, 2)
            in_blocks(C_IN, 0, xhi, xlo, lambda k: gain1[:, 1, k:k + 1], lambda k: modT[:, 1, SH1 * KT + k:SH1 * KT + k + 1])
            in_blocks(X_IN, 1, xhi, xlo, lambda k: gain1[:, 0, k:k + 1], lambda k: modT[:, 0, SH1 * KT + k:SH1 * KT + k + 1])
            dve.wait_ge(conv_hi, 1)
            dve.tensor_tensor(xlo[:, 8:16, :], convT[:, :, :], xhi[:, 8:16, :].bitcast(F32), ALU.subtract).then_inc(conv_lo, 1)
            dve.wait_ge(o_copied, 4 * GH)
            dve.tensor_scalar(oss[:, :, :], oss[:, :, :], 1.0 / DV, EPS, ALU.mult, ALU.add).then_inc(o_mean, 1)
            dve.wait_ge(o_root, 1)
            dve.reciprocal(orstd[:, :, :], oss[:, :, :]).then_inc(o_rstd, 1)
            dve.wait_ge(o_rstd, 1)
            for hd in range(GH):
                for t in range(T):
                    o = o_all[:, t, hd * DV:(hd + 1) * DV]
                    dve.scalar_tensor_tensor(o, o, orstd[:, t, hd:hd + 1], silg[:, t, hd * DV:(hd + 1) * DV],
                                             ALU.mult, ALU.mult).then_inc(o_gated, 1)
            remain_banks(xhi, xlo, 0, 4, lambda k: vecs[:, 2, 24 + k % 2:25 + k % 2])

            for which in range(2):
                for b in range(4):
                    dve.wait_ge(tp_ready, c.at("q", 1))
                    dve.tensor_copy(gates[:, which, b * NB:(b + 1) * NB], tp[:, c.slot("q", 2), :]).then_inc(tp_free, 1)
                    c.add("q")
                remainders(1)
            dve.wait_ge(tp_free, c.at("q", 2))

            def gated_add(which, n, pair):
                gate = gates[:, which, bass.ds(n, NB)].unsqueeze(1).broadcast_to([P, T, NB])
                dve.tensor_tensor(blk2[:, :, :], acc[:, 2 * pair:2 * pair + 2, :], gate, ALU.mult).then_inc(h_scaled, 1)
                c.add("hs")
                dve.wait_ge(h_scaled, c.at("hs"))
                dve.tensor_tensor(h[:, :, bass.ds(n, NB)], blk2[:, :, :], h[:, :, bass.ds(n, NB)], ALU.add).then_inc(h_added, 1)
                c.add("ha")

            def w_out2_pair(i, first=False):
                for pair in range(2):
                    remainders(1 if first and pair == 0 else 3)
                    wait_block(1)
                    if first and pair == 0:
                        dve.wait_ge(reload_s, 16)
                    gated_add(0, i * (2 * NB) + pair * NB, pair)
                    remainders(1)

            w_out2_pair(0, True)
            with c.loop(dve, 2, 1, g=8, hs=2, ha=2) as i:
                w_out2_pair(i)
            dve.scalar_tensor_tensor(gain2[:, :], modT[:, 0, SC2 * KT:(SC2 + 1) * KT], 1.0,
                                     vecs[:, 0, V_N2G:V_N2G + KT], ALU.add, ALU.mult).then_inc(gain_set, 1)
            c.add("ssq", T * KG)
            norm_scale(5, h, u_ffn)
            dve.wait_ge(gain_set, 3)

            def gate_up():
                dve.wait_ge(blk_half, c.at("half", 1))
                dve.tensor_tensor(blk[:, :, :], blk2[:, :, :], acc[:, 2:4, :], ALU.mult).then_inc(blk_ready, 1)
                c.add("half")

            def ffn(blocks, first=False):
                for j in range(blocks):
                    if first and j == 0:
                        opening(lambda b0, b1: modulate(xhi, xlo, b0, b1, lambda k: gain2[:, k:k + 1],
                                                        lambda k: modT[:, 0, SH2 * KT + k:SH2 * KT + k + 1]))
                    else:
                        remainders(2)
                    if j:
                        remain_banks(bhi, blo, 4 * (j - 1), 2)
                    remainders(6)
                    wait_block(2)
                    gate_up()
                for n in range(4):
                    remainders(blocks - 2)
                    if n == 0:
                        remain_banks(bhi, blo, 4 * (blocks - 1), 2)
                    if blocks < 4 and n == 3:
                        wait_block(0)
                    else:
                        remainders(2)
                        wait_block(2)
                    gated_add(1, n * NB, n % 2)

            c.n["half"] = 4 * MLP_CHUNKS
            ffn(4, True)
            with c.loop(dve, 2, 1, g=48, q=8, hi=8, half=4, hs=4, ha=4):
                ffn(4)
            ffn(3)
            c.add("ssq", T * KG)
            norm_root(6)
            dve.wait_ge(fg_in, 16)
            for t in range(T):
                dve.scalar_tensor_tensor(u_ffn[:, t, :], h[:, t, :], rstd[:, 6, t:t + 1], fgain[:, :],
                                         ALU.mult, ALU.mult).then_inc(final_set, 1)

        @block.tensor
        def _(pe):
            c = Counts()

            def multiply(hi, lo, kgs, kgroups, pair, half=None, order=None):
                first, final = (order[0], order[-1]) if order else (0, kgroups - 1)
                kts, width = (KG, NB) if half is None else (8, RANK2)
                for kg in kgs:
                    g2 = c.slot("g", HSLOTS)
                    pe.wait_ge(lo_done, c.at("g", WSLOTS + 1))
                    for k in range(kts):
                        tile = kg * kts + k
                        w = slice(k * width, (k + 1) * width)
                        for t in range(T):
                            dst = acc[:, 2 * pair + t, 0:width]
                            rows = slice(t * P, (t + 1) * P)
                            pe.matmul(dst, hi[:, tile, rows], whi[:, g2, w], start=(kg == first and k == 0), stop=False)
                            pe.matmul(dst, hi[:, tile, rows], wlo[:, g2, w], start=False, stop=False)
                            last = pe.matmul(dst, lo[:, tile, rows], whi[:, g2, w], start=False,
                                             stop=(kg == final and k == kts - 1))
                    last.then_inc(group_multiplied, 1)
                    c.add("g")

            def turn_rows(src, banks, b0=0):
                for b in range(b0, b0 + banks):
                    q = c.slot("q", 2)
                    pe.wait_ge(tp_free, c.at("q", 1))
                    for j in range(2):
                        for t in range(T):
                            f = (2 * b + j) * P
                            last = pe.transpose(tp[:, q, j * S + t * P:j * S + (t + 1) * P], src[:, t, f:f + P], ident)
                    last.then_inc(tp_ready, 1)
                    c.add("q")

            def reduce_mod(per_nb, dual):
                c.add("ma", per_nb)
                pe.wait_ge(mod_acc, c.at("ma", 8))
                for who in range(2 if dual else 1):
                    for j in range(4):
                        last = pe.matmul(m1[:, 4 * who + j:4 * who + j + 1], macc[:, who, j * P:(j + 1) * P],
                                         ones[:, 0:1], start=True, stop=True)
                last.then_inc(mod_reduced, 1)

            def opening(src, pair):
                turn_rows(src, 4)
                multiply(xhi, xlo, (0,), 4, pair)
                turn_rows(src, 2, 4)
                multiply(xhi, xlo, (1,), 4, pair)
                turn_rows(src, 2, 6)
                multiply(xhi, xlo, (2,), 4, pair)
                pe.wait_ge(tp_free, c.at("q", 2))
                multiply(xhi, xlo, (3,), 4, pair)

            pe.sem_inc(group_multiplied, HSLOTS)
            pe.wait_ge(start_in, 32)
            for a in range(3):
                pe.transpose(m0[:, a * P:(a + 1) * P], vrows[:, a, :], ident).then_inc(vec_turned, 1)
            pe.wait_ge(u_done, T)
            pe.wait_ge(pool_set, 1)

            def w_in_pair(first=False):
                for pair in range(2):
                    pe.wait_ge(proj_set, c.at("ps", 1))
                    if first and pair == 0:
                        opening(u_mix, 0)
                    else:
                        multiply(xhi, xlo, range(4), 4, pair)
                    c.add("ps")
                reduce_mod(32, True)

            for i in range(4):
                w_in_pair(i == 0)

            pe.wait_ge(proj_set, 2 + 8)
            pe.wait_ge(misc_in, 16 * 6)
            for s in range(HEADS + 1):
                g = s // 2
                if s < HEADS:
                    if s:
                        pe.wait_ge(qk_copied, 2 * s)
                    for w, col in ((0, 2 * NB), (1, 4 * NB)):
                        for t in range(T):
                            last = pe.transpose(tp[:, 0, w * S + t * P:w * S + (t + 1) * P],
                                                proj[:, t, col + s * HD:col + (s + 1) * HD], ident)
                    last.then_inc(qk_turned, 1)
                if s < HEADS and s % 2 == 0:
                    if g:
                        pe.wait_ge(f1_copied, g)
                    for ct in range(2):
                        for t in range(T):
                            last = pe.matmul(acc[:, ct, :], proj[:, t, g * FDIM + ct * P:g * FDIM + (ct + 1) * P],
                                             tab_f[:, t, 0:2 * S], start=(t == 0), stop=(t == T - 1))
                    last.then_inc(f1_done, 1)
                if s % 2:
                    pe.wait_ge(f1_copied, g + 1)
                    if g:
                        pe.wait_ge(f2_copied, g)
                    for cc in range(2):
                        for n, (part, ct) in enumerate(((0, 0), (0, 1), (1, 0), (1, 1))):
                            last = pe.matmul(m0[:, cc * S:(cc + 1) * S],
                                             tab_f[:, ct, part * 2 * S + cc * P:part * 2 * S + (cc + 1) * P],
                                             fpos[:, ct, part * S:(part + 1) * S], start=(n == 0), stop=(n == 3))
                    last.then_inc(f2_done, 1)
                if s < HEADS:
                    pe.wait_ge(qk_copied, 2 * (s + 1))
                    if s:
                        pe.wait_ge(scores_biased, s)
                    for t in range(T):
                        last = pe.matmul(acc[:, 2, t * S:(t + 1) * S], qkT[:, s % 2, 0, t * P:(t + 1) * P],
                                         qkT[:, s % 2, 1, :], start=True, stop=True)
                    last.then_inc(scores_done, 1)
                if s:
                    pe.wait_ge(probs_ready, T * s)
                    if s >= 2:
                        pe.wait_ge(probsT_copied, s - 1)
                    for kt in range(2):
                        for t in range(T):
                            last = pe.transpose(tp[:, 1, kt * S + t * P:kt * S + (t + 1) * P],
                                                probs[:, t * S + kt * P:t * S + (kt + 1) * P], ident)
                    last.then_inc(probs_turned, 1)
                if s % 2:
                    pe.wait_ge(f2_copied, g + 1)
                    if g:
                        pe.wait_ge(f3_lo, g)
                    for e in range(2):
                        for cc in range(2):
                            last = pe.matmul(m1[:, e * S:(e + 1) * S], wf[:, g, cc, e * P:(e + 1) * P], fre[:, cc, :],
                                             start=(cc == 0), stop=(cc == 1))
                    last.then_inc(f3_done, 1)
                if s:
                    pe.wait_ge(probsT_copied, s)
                    if s >= 2:
                        pe.wait_ge(pv_lo, s - 1)
                    v = 6 * NB + (s - 1) * HD
                    for kt in range(2):
                        last = pe.matmul(acc[:, 3, 0:S], proj[:, kt, v:v + HD], probsT[:, kt, :],
                                         start=(kt == 0), stop=(kt == 1))
                    last.then_inc(pv_done, 1)
            pe.wait_ge(f3_lo, FGROUPS)
            pe.wait_ge(pv_lo, HEADS)

            for n in range(4):
                pe.wait_ge(h_added, c.at("ha", 1))
                multiply(xhi, xlo, range(4), 4, n % 2)
                c.add("ha")
            pe.wait_ge(u_done, 2 * T)

            def mlp_chunk(first=False):
                for j in range(8):
                    pair = j % 2
                    if j < 2:
                        pe.wait_ge(h_added, c.at("ha", 1 + j))
                    elif j < 6:
                        pe.wait_ge(blk_half, c.at("half", j - 1))
                    else:
                        pe.wait_ge(h_added, c.at("ha", 2 + j - 5))
                    if first and j == 0:
                        opening(u_mlp, 0)
                        continue
                    hi, lo = (xhi, xlo) if j < 4 else (ahi, alo)
                    multiply(hi, lo, range(2), 4, pair)
                    if 1 <= j <= 4:
                        pe.wait_ge(blk_ready, c.at("blk", j))
                        turn_rows(blk, 2)
                    multiply(hi, lo, (2,), 4, pair)
                    if j == 4:
                        pe.wait_ge(tp_free, c.at("q", 2))
                    multiply(hi, lo, (3,), 4, pair)
                    if j % 2:
                        reduce_mod(32 if j == 3 else 16, j == 3)
                c.add("ha", 4)
                c.add("half", 4)
                c.add("blk", 4)

            mlp_chunk(True)
            with c.loop(pe, MLP_CHUNKS, 1, g=32, q=8, ma=80, ha=4, half=4, blk=4):
                mlp_chunk()

            def evacuated(name, p):
                if p and name in ("cx0", "cx1"):
                    pe.wait_ge(blk_ready, 4 * MLP_CHUNKS + 1 + int(name[2]))
                else:
                    pe.wait_ge(in_set, IN_SET[p][name])

            def turn_conv(half, pr):
                pe.wait_ge(blk_ready, 4 * MLP_CHUNKS + 1 + half)
                pe.wait_ge(in_set, IN_SET[1]["cb1" if half else "cb0"])
                turn_rows(blk, 1, pr)
                turn_rows(blk2, 1, pr)

            def step(kind, p, a, b):
                q = c.slot("q", 2)
                if kind == "conv":
                    turn_conv(a, b)
                elif kind == "rank":
                    pe.wait_ge(in_set, IN_SET[p]["l"])
                    if p:
                        pe.wait_ge(cum_exp, GH)
                    for t in range(T):
                        last = pe.transpose(m0[:, t * P:(t + 1) * P], lrank[:, t, :], ident)
                    last.then_inc(lr_turned, 1)
                elif kind == "z":
                    pe.wait_ge(lr_copied, p + 1)
                    pe.wait_ge(wg_in, 16)
                    pe.wait_ge(tp_free, c.at("q", 1))
                    pe.matmul(tp[:, q, :], lrankT[:, a * P:(a + 1) * P], wg[:, b, :], start=True, stop=True).then_inc(tp_ready, 1)
                    c.add("q")
                elif kind == "suffix":
                    pe.wait_ge(tp_free, c.at("q", 2 if a == b == 0 else 1))
                    pe.matmul(tp[:, q, :], after[b], la[:, a, b], start=True, stop=True).then_inc(tp_ready, 1)
                    c.add("q")
                elif kind == "cum":
                    hd = a
                    if hd:
                        pe.wait_ge(cum_exp, hd if p == 0 else GH + 2 * hd)
                    else:
                        pe.wait_ge(lr_copied, p + 1)
                    for d in range(2):
                        for t in range(T):
                            last = pe.matmul(m0[:, d * S + t * P:d * S + (t + 1) * P], la[:, t, d, hd * DK:(hd + 1) * DK],
                                             tri[d], start=True, stop=True)
                    last.then_inc(cum_done, 1)
                elif kind == "turn":
                    hd = a
                    pe.wait_ge(in_set, IN_SET[p]["q"])
                    pe.wait_ge(tp_free, c.at("q", 1))
                    for w, src in ((0, gq), (1, gk)):
                        for t in range(T):
                            last = pe.transpose(tp[:, q, w * S + t * P:w * S + (t + 1) * P],
                                                src[:, t, hd * DK:(hd + 1) * DK], ident)
                    last.then_inc(tp_ready, 1)
                    c.add("q")
                elif kind == "scores":
                    pe.wait_ge(qe_done, 4 * (a + 1))
                    if a:
                        pe.wait_ge(gsc_kept, 4 * a)
                    else:
                        pe.wait_ge(mod_set, 32)
                    for d in range(2):
                        for t in range(T):
                            last = pe.matmul(m1[:, (2 * d + t) * P:(2 * d + t + 1) * P], ke[:, d, t * P:(t + 1) * P],
                                             qe[:, d, t * P:(t + 1) * P], start=True, stop=True)
                    last.then_inc(gsc_done, 1)
                elif kind == "state":
                    hd, d = a, b
                    pe.wait_ge(in_set, IN_SET[p]["v0" if hd < 2 else "v1"])
                    pe.wait_ge(tp_free, c.at("q", 2))
                    for bank in range(2):
                        for ck in (bank, bank + 2):
                            if p and ck == ORDER[d][-1]:
                                continue
                            rows = slice(bank * CH, (bank + 1) * CH)
                            last = pe.matmul(tp[:, (q + bank) % 2, (ck // 2) * DV:(ck // 2 + 1) * DV],
                                             kdec[rows, ck // 2, d, hd * DK:(hd + 1) * DK],
                                             gv[rows, ck // 2, hd * DV:(hd + 1) * DV], start=True, stop=True)
                        last.then_inc(tp_ready, 1)
                    c.add("q", 2)
                elif kind == "out":
                    hd = a
                    pe.wait_ge(gsc_kept, 4 * (hd + 1))
                    pe.wait_ge(state_step, STATE_STEPS[0] * GH + STATE_STEPS[1] * (hd + 1))
                    pe.wait_ge(tp_free, c.at("q", 1))
                    for t in range(T):
                        for d in range(2):
                            pe.matmul(tp[:, q, t * DV:(t + 1) * DV], sc[:, d, t, :], gv[:, t, hd * DV:(hd + 1) * DV],
                                      start=(d == 0), stop=False)
                        for d in range(2):
                            for half in range(2):
                                ck = 2 * t + half
                                state = states[:, d, hd, :] if ck == ORDER[d][0] else gst[:, d, ck, :]
                                last = pe.matmul(tp[half * CH:(half + 1) * CH, q, t * DV:(t + 1) * DV],
                                                 qe[:, d, ck * CH:(ck + 1) * CH], state, start=False, stop=(d == 1))
                    last.then_inc(tp_ready, 1)
                    c.add("q")

            def evacuated(name, p):
                if name in ("cx0", "cx1"):
                    pe.wait_ge(blk_ready, 4 * MLP_CHUNKS + 1 + int(name[2]))
                else:
                    pe.wait_ge(in_set, IN_SET[p][name])

            def in_blocks(names, b0, p, rows):
                for n, name in enumerate(names):
                    pair = (b0 + n) % 2
                    if n >= 2:
                        evacuated(names[n - 2], p)
                    elif p:
                        evacuated(C_IN[len(C_IN) - 2 + n], 0)
                    else:
                        pe.wait_ge(h_added, H_MLP - 1 + n)
                    which, part = MOD_PAIRS[p].get(name, (None, 0))
                    if n == 0:
                        opening(rows, pair)
                    for kg in range(2 if name == "l" else 4):
                        if name == "l":
                            multiply(xhi, xlo, (kg,), 2, pair, half=True)
                        elif n:
                            multiply(xhi, xlo, (kg,), 4, pair)
                        if n or kg == 3:
                            for st in BESIDE[p].get((name, kg), ()):
                                step(*st)
                    if part:
                        reduce_mod(16, False)

            pe.wait_ge(u_done, 3 * T)
            in_blocks(C_IN, 44, 0, u_g)
            pe.wait_ge(u_done, 5 * T)
            in_blocks(X_IN, 48, 1, h)

            def gate_columns(which):
                for b in range(4):
                    q = c.slot("q", 2)
                    pe.wait_ge(tp_free, c.at("q", 1))
                    for j in range(4):
                        col = (GT2 if which else GT1) * KT + 4 * b + j
                        last = pe.matmul(tp[:, q, j * P:(j + 1) * P], modT[:, 0, col:col + 1].broadcast_to([P, P]), ident,
                                         start=True, stop=True)
                    last.then_inc(tp_ready, 1)
                    c.add("q")

            def w_out2_pair(first=False):
                for pair in range(2):
                    if first and pair == 0:
                        pe.wait_ge(conv_lo, 1)
                        pe.wait_ge(in_set, IN_SET[1]["g1"])
                        multiply(xhi, xlo, (2, 3), 4, 0, order=TILED)
                        pe.wait_ge(o_gated, T * GH)
                        turn_rows(o_all, 4)
                        pe.wait_ge(mod_set, 32)
                        gate_columns(0)
                        multiply(xhi, xlo, (0,), 4, 0, order=TILED)
                        gate_columns(1)
                        multiply(xhi, xlo, (1,), 4, 0, order=TILED)
                        c.add("ha")
                        continue
                    pe.wait_ge(h_added, c.at("ha", 1))
                    multiply(xhi, xlo, TILED, 4, pair, order=TILED)
                    c.add("ha")

            for i in range(2):
                w_out2_pair(i == 0)
            pe.wait_ge(u_done, 6 * T)
            c.n["half"] = 4 * MLP_CHUNKS
            c.n["blk"] = 4 * MLP_CHUNKS + 2

            def ffn(blocks, first=False):
                for j in range(blocks):
                    if j:
                        pe.wait_ge(blk_half, c.at("half", j))
                    else:
                        pe.wait_ge(h_scaled, c.at("hs", -1))
                    if first and j == 0:
                        opening(u_ffn, 0)
                    else:
                        multiply(xhi, xlo, range(2), 4, 0)
                        if j:
                            pe.wait_ge(blk_ready, c.at("blk", j))
                            turn_rows(blk, 2)
                        multiply(xhi, xlo, (2, 3), 4, 0)
                    if not j:
                        pe.wait_ge(h_scaled, c.at("hs"))
                    multiply(xhi, xlo, range(4), 4, 1)
                for n in range(4):
                    if n == 0:
                        pe.wait_ge(blk_half, c.at("half", blocks))
                    elif n >= 2:
                        pe.wait_ge(h_scaled, c.at("hs", n - 1))
                    multiply(bhi, blo, range(2), blocks, n % 2)
                    if n == 0:
                        pe.wait_ge(blk_ready, c.at("blk", blocks))
                        turn_rows(blk, 2)
                    for kg in range(2, blocks):
                        if n == 0 and kg == blocks - 1:
                            pe.wait_ge(tp_free, c.at("q", 2))
                        multiply(bhi, blo, (kg,), blocks, n % 2)
                c.add("half", blocks)
                c.add("blk", blocks)
                c.add("hs", 4)

            c.n["hs"] = 4
            ffn(4, True)
            with c.loop(pe, 2, 1, g=48, q=8, half=4, blk=4, hs=4):
                ffn(4)
            ffn(3)


def kernel(**inputs):
    import concourse.bacc as bacc
    from concourse.bass_utils import run_bass_kernel_spmd

    nc = bacc.Bacc("TRN2", target_bir_lowering=False, num_devices=1)
    a = {k: np.asarray(v) for k, v in inputs.items()}

    vectors = np.zeros((P, 3, P), np.float32)
    rows = [a["norm_mix_g"], a["norm_mlp_g"], a["norm1_g_2"], a["norm2_g_2"], a["c_2"], a["c_ctx_2"]]
    vectors[0:96, 0] = np.concatenate([r.reshape(KT, P) for r in rows])
    vectors[0:96, 1] = a["b_mod_2"].reshape(6 * KT, P)
    vectors[0:24, 2] = a["conv_w_2"].reshape(24, P)
    vectors[24:26, 2] = a["gla_norm_g_2"].reshape(2, P)
    gates_w = np.zeros((P, 2, GH * DK), np.float32)
    for d, n in enumerate(("f", "b")):
        gates_w[16 * d:16 * d + 16, d] = a[f"w_gate_{n}_2"][0]
        gates_w[RANK2, d] = a[f"b_gate_{n}_2"][0]

    j, i = np.mgrid[0:P, 0:P]
    same = j // CH == i // CH
    tables = np.stack([np.eye(P), (same & (j <= i)) / 16.0, (same & (j >= i)) / 16.0,
                       (same & (j > i)) / 16.0, (same & (j < i)) / 16.0,
                       same & (j <= i), same & (j >= i)], axis=1).astype(np.float32)
    ang = 2 * np.pi * (np.outer(np.arange(S), np.arange(S)) % S) / S
    dft = np.concatenate([np.cos(ang), np.sin(ang), -np.sin(ang)], axis=1) / np.sqrt(S)
    fourier_tables = np.ascontiguousarray(dft.reshape(2, P, 3 * S).transpose(1, 0, 2)).astype(np.float32)
    dist = np.abs(np.arange(S)[:, None] - np.arange(S)[None, :])
    seen = sum(((dist % dil == 0) & (dist // dil <= (window // 2) // dil)).astype(int)
               for window, dil in ((128, 1), (512, 4), (2048, 16)))
    attn = np.stack([np.where(seen > 0, -dist, -1e30), seen])
    attn_tables = np.ascontiguousarray(attn.reshape(2, T, P, S).transpose(2, 0, 1, 3).reshape(P, 2, T * S)).astype(np.float32)

    arrays = {
        "x": a["x"][0], "ctx_in": a["ctx_2"][0], "w_in": a["w_in"][0], "w_fourier": a["w_fourier"][0],
        "w_out": a["w_out"][0], "w_up": a["w_up"][0], "w_down": a["w_down"][0], "w_mod": a["w_mod_2"][0],
        "w_in2": a["w_in_2"][0], "w_out2": a["w_out_2"][0], "w_gate": a["w_ffn_gate_2"][0],
        "w_up2": a["w_ffn_up_2"][0], "w_down2": a["w_ffn_down_2"][0], "vectors": vectors,
        "gates_w": gates_w, "mid_g": a["norm_final_g"], "final_g": a["final_g_2"], "tables": tables,
        "fourier_tables": fourier_tables, "attn_tables": attn_tables,
    }
    args = {}
    for name, v in arrays.items():
        arrays[name] = np.ascontiguousarray(v)
        args[name] = nc.dram_tensor(name, arrays[name].shape, mybir.dt.from_np(arrays[name].dtype), kind="ExternalInput").ap()
    args["out"] = nc.dram_tensor("out", [S, D], F32, kind="ExternalOutput").ap()
    two_blocks(nc, **args)
    r = run_bass_kernel_spmd(nc, [arrays], core_ids=[0])
    return r.results[0]["out"].reshape(1, S, D)
```

```python
from contextlib import ExitStack, contextmanager

import numpy as np

import concourse.bass as bass
from concourse import mybir

P = 128
F32 = mybir.dt.float32
F32R = mybir.dt.float32r
U32 = mybir.dt.uint32
ACT = mybir.ActivationFunctionType
ALU = mybir.AluOpType
AX_X = mybir.AxisListType.X

D = 2048
S = 256
T = S // P
KT = D // P
NB = 512
KG = 4
EPS = 1e-6

FGROUPS, FDIM = 4, 256
HEADS, HD = 8, 128
MLP_CHUNKS = 4

GH, DK, DV = 4, 128, 256
CH = 64
NCH = S // CH
RANK2 = 32
OFF_Q, OFF_K, OFF_V, OFF_G, OFF_L, OFF_CB, OFF_CC, OFF_CX = 0, 512, 1024, 2048, 3072, 3104, 4128, 5152
FFN_BLOCKS = 11
GRID = 64

WSLOTS = 4
HSLOTS = 2
MSLOTS = 2
MSTEPS = 8
STATE_STEPS = (8, 6)
H0 = 2
SH1, SC1, GT1, SH2, SC2, GT2 = range(6)

V_MIXG, V_MLPG, V_N1G, V_N2G, V_C = range(0, 80, 16)


class Counts:

    def __init__(self, **start):
        self.n = dict(start)
        self.i, self.start, self.per = None, 0, {}

    def at(self, name, off=0):
        v = self.n.get(name, 0) + off
        if self.i is not None and self.per.get(name, 0):
            return self.i * self.per[name] + (v - self.start * self.per[name])
        return v

    def landed(self, name, slots):
        v = 16 * (self.n.get(name, 0) // slots + 1)
        if self.i is not None and self.per.get(name, 0):
            per = self.per[name] // slots * 16
            return self.i * per + (v - self.start * per)
        return v

    def slot(self, name, slots):
        assert self.i is None or self.per.get(name, 0) % slots == 0, name
        return self.n.get(name, 0) % slots

    def add(self, name, k=1):
        self.n[name] = self.n.get(name, 0) + k

    @contextmanager
    def loop(self, eng, trips, start=0, **per):
        before = {k: self.n.get(k, 0) for k in per}
        with eng.Fori(start, trips) as i:
            self.i, self.start, self.per = i, start, per
            yield i
            self.i, self.per = None, {}
        for k, v in per.items():
            assert self.n.get(k, 0) - before[k] == v, (k, self.n.get(k, 0) - before[k], v)
            self.n[k] += v * (trips - start - 1)


def two_blocks(nc, x, ctx_in, w_in, w_fourier, w_out, w_up, w_down, w_mod, w_in2, w_out2, w_gate,
               w_up2, w_down2, vectors, gates_w, mid_g, final_g, tables, fourier_tables, attn_tables, out):
    ctx = ExitStack()
    with ctx:
        def sb(name, shape, dt=F32, scope=ctx):
            return scope.enter_context(nc.sbuf_tensor(name, shape, dt))

        def sem(name):
            return ctx.enter_context(nc.semaphore(name))

        wring = sb("wring", [P, WSLOTS, KG * NB])
        whi = sb("whi", [P, HSLOTS, KG * NB], F32R)
        wlo = sb("wlo", [P, HSLOTS, KG * NB], F32R)
        mring = sb("mring", [P, MSLOTS, 2, NB])
        macc = sb("macc", [P, 2, NB])
        h = sb("h", [P, T, D])
        xhi = sb("xhi", [P, KT, S], F32R)
        xlo = sb("xlo", [P, KT, S], F32R)
        tabs = sb("tabs", [P, 7, P])
        ident = tabs[:, 0, :]
        tri = [tabs[:, 1, :], tabs[:, 2, :]]
        after = [tabs[:, 3, :], tabs[:, 4, :]]
        keep = [tabs[:, 5, :].bitcast(U32), tabs[:, 6, :].bitcast(U32)]
        ones = sb("ones", [P, 1])
        vrows = sb("vrows", [P, 3, P])
        vecs = sb("vecs", [P, 3, P])
        csil = sb("csil", [P, 2, KT])
        modT = sb("modT", [P, 2, 6 * KT])
        gain1 = sb("gain1", [P, 2, KT])
        gain2 = sb("gain2", [P, KT])
        squares = sb("squares", [P, T, KG])
        ssq = sb("ssq", [P, 7, T])
        rstd = sb("rstd", [P, 7, T])
        blk = sb("blk", [P, T, NB])
        blk2 = sb("blk2", [P, T, NB])
        tmpT = sb("tmpT", [P, 2, NB])

        with ExitStack() as ph:
            tab_f = sb("tab_f", [P, 2, 3 * S], scope=ph)
            tab_a = sb("tab_a", [P, 2, T * S], scope=ph)
            proj = sb("proj", [P, T, 8 * NB], scope=ph)
            wf = sb("wf", [P, FGROUPS, 2, FDIM], scope=ph)
            qkT = sb("qkT", [P, 2, 2, S], scope=ph)
            nmax = sb("nmax", [P, HEADS, T], scope=ph)
            aden = sb("aden", [P, HEADS, T], scope=ph)
            arden = sb("arden", [P, HEADS, T], scope=ph)
        u_mix = proj[:, :, 0:D]
        fpos = blk
        fre = tmpT[:, 0, :].rearrange("p (c s) -> p c s", c=2)
        probsT = tmpT[:, 1, :].rearrange("p (c s) -> p c s", c=2)
        sbias = blk2[:, 0, :]
        probs = blk2[:, 1, :]
        with ExitStack() as ph:
            ahi = sb("ahi", [P, KT, S], F32R, scope=ph)
            alo = sb("alo", [P, KT, S], F32R, scope=ph)
            u_mlp = sb("u_mlp", [P, T, D], scope=ph)
            mgain = sb("mgain", [P, D], scope=ph)
        with ExitStack() as ph:
            states = sb("states", [P, 2, GH, DV], scope=ph)
            wg = sb("wg", [P, 2, GH * DK], scope=ph)
            gk = sb("gk", [P, T, GH * DK], scope=ph)
            gv = sb("gv", [P, T, GH * DV], scope=ph)
            gq = sb("gq", [P, T, GH * DK], scope=ph)
            lrankT = sb("lrankT", [P, S], scope=ph)
            epos = sb("epos", [P, 2, S], scope=ph)
            sb("spare", [P, 2 * P], scope=ph)
            gbig = sb("gbig", [P, 2 * D], scope=ph)
            silg = sb("silg", [P, T, GH * DV], scope=ph)
            convT = sb("convT", [P, 8, S], scope=ph)
            oss = sb("oss", [P, T, GH], scope=ph)
            orstd = sb("orstd", [P, T, GH], scope=ph)
        u_g = gbig[:, :].rearrange("p (t d) -> p t d", t=T)
        la = gbig[:, 0:D].rearrange("p (t d c) -> p t d c", t=T, d=2)
        kdec = gbig[:, D:2 * D].rearrange("p (t d c) -> p t d c", t=T, d=2)
        gst = h[:, 0, :].rearrange("p (d c v) -> p d c v", d=2, c=NCH)
        o_all = h[:, 1, :].rearrange("p (t c) -> p t c", t=T)
        eneg = tmpT[:, 0, :].rearrange("p (d s) -> p d s", d=2)
        qe = blk[:, 0, :].rearrange("p (d s) -> p d s", d=2)
        ke = blk[:, 1, :].rearrange("p (d s) -> p d s", d=2)
        sc = blk2[:, 0, :].rearrange("p (d t s) -> p d t s", d=2, t=T)
        with ExitStack() as ph:
            with ExitStack() as sub:
                u_ffn = sb("u_ffn", [P, T, D], scope=sub)
            bhi = sb("bhi", [P, KT, S], F32R, scope=ph)
            blo = sb("blo", [P, KT, S], F32R, scope=ph)
            gates = sb("gates", [P, 2, D], scope=ph)
            fgain = sb("fgain", [P, D], scope=ph)

        acc = ctx.enter_context(nc.psum_tensor("acc", [P, 2 * T, NB], F32))
        tp = ctx.enter_context(nc.psum_tensor("tp", [P, 2, NB], F32))
        m0 = ctx.enter_context(nc.psum_tensor("m0", [P, NB], F32))
        m1 = ctx.enter_context(nc.psum_tensor("m1", [P, NB], F32))
        hspill = nc.dram_tensor("hspill", [T, P, D], F32).ap()

        group_landed = [sem(f"group_landed{i}") for i in range(WSLOTS)]
        hi_done = sem("hi_done")
        lo_done = sem("lo_done")
        group_multiplied = sem("group_multiplied")
        tp_ready = sem("tp_ready")
        tp_hi = sem("tp_hi")
        tp_tmp = sem("tp_tmp")
        tp_free = sem("tp_free")
        step_landed = [sem(f"step_landed{i}") for i in range(MSLOTS)]
        mod_acc = sem("mod_acc")
        mod_reduced = sem("mod_reduced")
        mod_set = sem("mod_set")
        start_in = sem("start_in")
        x_in = [sem(f"x_in{piece}") for piece in range(KG)]
        misc_in = sem("misc_in")
        ctx_in_s = sem("ctx_in_s")
        wg_in = sem("wg_in")
        spill_s = sem("spill_s")
        reload_s = sem("reload_s")
        fg_in = sem("fg_in")
        mg_in = sem("mg_in")
        out_s = sem("out_s")
        pool_set = sem("pool_set")
        vec_turned = sem("vec_turned")
        vec_set = sem("vec_set")
        c_exp = sem("c_exp")
        c_sil = sem("c_sil")
        x_squares_a, x_squares_v = sem("x_squares_a"), sem("x_squares_v")
        ssq_done = sem("ssq_done")
        squares_summed = sem("squares_summed")
        mean_done = sem("mean_done")
        root_done = sem("root_done")
        rstd_done = sem("rstd_done")
        u_done = sem("u_done")
        blk_ready = sem("blk_ready")
        blk_half = sem("blk_half")
        h_added = sem("h_added")
        h_scaled = sem("h_scaled")
        proj_set = sem("proj_set")
        f1_done, f1_copied, f2_done, f2_copied, f3_done, f3_hi, f3_lo = (
            sem(n) for n in ("f1_done", "f1_copied", "f2_done", "f2_copied", "f3_done", "f3_hi", "f3_lo"))
        qk_turned, qk_copied, scores_done, scores_biased, max_set, exps_done = (
            sem(n) for n in ("qk_turned", "qk_copied", "scores_done", "scores_biased", "max_set", "exps_done"))
        probs_summed, den_inverted, probs_ready, probs_turned, probsT_copied, pv_done, pv_hi, pv_lo = (
            sem(n) for n in ("probs_summed", "den_inverted", "probs_ready", "probs_turned",
                             "probsT_copied", "pv_done", "pv_hi", "pv_lo"))
        gain_set = sem("gain_set")
        in_set = sem("in_set")
        la_step, kdec_exp, cum_done, cum_exp, qe_done = (
            sem(n) for n in ("la_step", "kdec_exp", "cum_done", "cum_exp", "qe_done"))
        gsc_done, gsc_kept, state_step, o_copied = (
            sem(n) for n in ("gsc_done", "gsc_kept", "state_step", "o_copied"))
        sc_zeroed = sem("sc_zeroed")
        conv_step, conv_hi, conv_lo = sem("conv_step"), sem("conv_hi"), sem("conv_lo")
        o_mean, o_root, o_rstd, o_gated = sem("o_mean"), sem("o_root"), sem("o_rstd"), sem("o_gated")
        final_set = sem("final_set")

        C_IN = ("k", "l", "v0", "v1")
        X_IN = ("cc0", "cx0", "cb0", "cc1", "cx1", "cb1", "k", "l", "q", "v0", "v1", "g0", "g1")
        COLS = {"l": OFF_L, "k": OFF_K, "v0": OFF_V, "v1": OFF_V + NB, "q": OFF_Q,
                "cc0": OFF_CC, "cc1": OFF_CC + NB, "cx0": OFF_CX, "cx1": OFF_CX + NB,
                "cb0": OFF_CB, "cb1": OFF_CB + NB, "g0": OFF_G, "g1": OFF_G + NB}
        SPREAD = (2, 1, 1, 1, 1, 1, 1, 0)
        MLP_MODS = {**{g: (SC2, n) for g, n in ((2, 2), (3, 2), (4, 2), (6, 2))},
                    **{g: (SC1, 1) for g in (7, 8, 10, 11, 12, 14, 15, 16)},
                    **{g: (GT1, n) for g, n in ((18, 2), (19, 1), (20, 2), (21, 1), (22, 1), (23, 1))},
                    **{g: (SH2, n) for g, n in ((24, 2), (25, 2), (26, 1), (28, 2), (29, 1))}}
        MLP_REDUCED = {7: SC2, 18: SC1, 24: GT1, 30: SH2}
        TILED = (2, 3, 0, 1)
        LAST_CHUNK = FFN_BLOCKS - 8
        IN_SET, stored = ({}, {}), 0
        for names, values in zip((C_IN, X_IN), IN_SET):
            for name in names:
                if name[:2] != "cx":
                    stored += 1
                    values[name] = stored
        BESIDE = ({("l", 1): (("half_norm", 0, 0, 0),), ("v0", 0): (("mid_norm", 0, 0, 0),),
                   ("v0", 1): (("mid_norm", 0, 1, 0),),
                   ("v0", 2): (("x_squares", 0, 0, 0),), ("v0", 3): (("x_squares", 0, 2, 0),),
                   ("v1", 1): (("x_norm", 0, 0, 0),)}, {})
        BESIDE[1].update({
            ("cc0", 3): (("z", 0, 0, 0),), ("cx0", 0): (("z", 0, 0, 1),),
            ("cx0", 1): (("z", 0, 1, 0),), ("cx0", 2): (("z", 0, 1, 1),),
            ("cx0", 3): (("suffix", 0, 0, 0), ("suffix", 0, 0, 1)), ("cb0", 0): (("suffix", 0, 1, 0), ("suffix", 0, 1, 1)),
            ("cb0", 1): (("cum", 0, 0, 0),), ("cb0", 2): (("state", 0, 0, 0),),
            ("cb0", 3): (("state", 0, 0, 1), ("cum", 0, 1, 0)),
            ("cc1", 0): (("conv", 1, 0, 0),), ("cc1", 1): (("conv", 1, 0, 1),),
            ("cc1", 2): (("state", 0, 1, 0),), ("cc1", 3): (("state", 0, 1, 1), ("cum", 0, 2, 0)),
            ("cx1", 0): (("state", 0, 2, 0),), ("cx1", 1): (("state", 0, 2, 1), ("cum", 0, 3, 0)),
            ("cx1", 2): (("state", 0, 3, 0),), ("cx1", 3): (("state", 0, 3, 1),),
            ("k", 0): (("conv", 1, 1, 0),), ("k", 1): (("conv", 1, 1, 1),),
            ("q", 0): (("z", 1, 0, 0),), ("q", 1): (("z", 1, 0, 1),),
            ("q", 2): (("z", 1, 1, 0),), ("q", 3): (("z", 1, 1, 1),),
            ("v0", 0): (("suffix", 1, 0, 0), ("suffix", 1, 0, 1)), ("v0", 1): (("suffix", 1, 1, 0), ("suffix", 1, 1, 1)),
            ("v0", 3): (("cum", 1, 0, 0), ("turn", 1, 0, 0)),
            ("v1", 0): (("scores", 1, 0, 0), ("state", 1, 0, 0)), ("v1", 1): (("state", 1, 0, 1),),
            ("v1", 2): (("out", 1, 0, 0), ("cum", 1, 1, 0), ("turn", 1, 1, 0)),
            ("v1", 3): (("scores", 1, 1, 0), ("state", 1, 1, 0)), ("g0", 0): (("state", 1, 1, 1),),
            ("g0", 1): (("out", 1, 1, 0), ("cum", 1, 2, 0), ("turn", 1, 2, 0)),
            ("g0", 2): (("scores", 1, 2, 0), ("state", 1, 2, 0)), ("g0", 3): (("state", 1, 2, 1),),
            ("g1", 0): (("out", 1, 2, 0), ("cum", 1, 3, 0), ("turn", 1, 3, 0)),
            ("g1", 1): (("scores", 1, 3, 0), ("state", 1, 3, 0)), ("g1", 2): (("state", 1, 3, 1),),
        })
        MOD_PAIRS = ({"v0": (0, 0), "v1": (0, 1)},
                     {"cx0": (1, 0), "cb0": (1, 1), "cc1": (2, 0), "cx1": (2, 1), "cb1": (3, 0), "k": (3, 1)})
        ORDER = ((0, 1, 2, 3), (3, 2, 1, 0))
        BANKS = {"z": 1, "suffix": 1, "state": 2, "turn": 1, "out": 1, "conv": 2}
        T_O = 8 + 8 + 8 * MLP_CHUNKS + 8 + 8 + 4 + BANKS["out"] + sum(
            BANKS.get(step[0], 0) for steps in BESIDE[1].values() for step in steps)
        H_MLP = H0 + 4 + 4 * MLP_CHUNKS
        block = ctx.enter_context(nc.Block())

        @block.sync
        def _(sp):
            c = Counts()

            def load(src, kts=KG, width=NB):
                sp.wait_ge(lo_done, c.at("g", 1))
                dst = wring[:, c.slot("g", WSLOTS), 0:kts * width].rearrange("p (k n) -> p k n", k=kts)
                sp.dma_start(dst, src).then_inc(group_landed[c.slot("g", WSLOTS)], 16)
                c.add("g")

            def block_of(w, col, kgroups=KT // KG, kg0=0, order=None):
                v = w.rearrange("(g k p) n -> g p k n", k=KG, p=P)
                for kg in order or range(kgroups):
                    if isinstance(kg0, int):
                        load(v[kg0 + kg, :, :, bass.ds(col, NB)])
                    else:
                        load(v[bass.ds(kg0 + kg, 1), :, :, bass.ds(col, NB)].rearrange("a p k n -> (a p) k n"))

            for piece in range(KG):
                cols = slice(piece * NB, (piece + 1) * NB)
                sp.dma_start(h[:, :, cols], x[:, cols].rearrange("(t p) n -> p t n", p=P)).then_inc(x_in[piece], 16)
            with c.loop(sp, 4, g=8) as i:
                for j in range(2):
                    block_of(w_in, i * (2 * NB) + j * NB)
            with c.loop(sp, 2, g=8) as i:
                for j in range(2):
                    block_of(w_out, i * (2 * NB) + j * NB)
            with c.loop(sp, MLP_CHUNKS, g=32) as i:
                for j in range(4):
                    block_of(w_up, i * D + j * NB)
                for n in range(4):
                    block_of(w_down, n * NB, kg0=i * 4)
            for names in (C_IN, X_IN):
                for name in names:
                    if name == "l":
                        v = w_in2.rearrange("(g k p) n -> g p k n", k=8, p=P)
                        for half in range(2):
                            load(v[half, :, :, OFF_L:OFF_L + RANK2], 8, RANK2)
                    else:
                        block_of(w_in2, COLS[name])
            for kgs in (TILED[0:2], TILED[2:4]):
                for n in range(2):
                    block_of(w_out2, n * NB, order=kgs)
            for n in range(2, 4):
                block_of(w_out2, n * NB, order=TILED)

            def ffn(i, blocks):
                for j in range(blocks):
                    block_of(w_gate, i * D + j * NB)
                    block_of(w_up2, i * D + j * NB)
                for n in range(4):
                    block_of(w_down2, n * NB, kgroups=blocks, kg0=i * 4)

            with c.loop(sp, 2, g=48) as i:
                ffn(i, 4)
            ffn(2, LAST_CHUNK)

        @block.gpsimd
        def _(pool):
            c = Counts()
            pool.memset(ones[:, :], 1.0).then_inc(pool_set, 1)
            pool.wait_ge(x_in[KG - 1], 16)
            pool.dma_start(tab_f[:, :, :], fourier_tables).then_inc(misc_in, 16)
            pool.dma_start(tab_a[:, :, :], attn_tables).then_inc(misc_in, 16)
            for g in range(FGROUPS):
                pool.dma_start(wf[:, g, :, :], w_fourier[g].rearrange("(c p) e -> p c e", p=P)).then_inc(misc_in, 16)
            w_mod_v = w_mod.rearrange("(s k p) n -> s p k n", k=2, p=P)

            def mod_block(kind, i, per_step, last_step):
                for s in range(MSTEPS):
                    pool.wait_ge(mod_acc, c.at("ma", 8 - (last_step if s == 0 else per_step)))
                    pool.dma_start(mring[:, c.slot("m", MSLOTS), :, :],
                                   w_mod_v[s, :, :, bass.ds(i * NB + kind * D, NB)])\
                        .then_inc(step_landed[c.slot("m", MSLOTS)], 16)
                    c.add("m")
                    c.add("ma", per_step)

            with c.loop(pool, 4, m=8, ma=32) as i:
                mod_block(SH1, i, 4, 4)
            mod_block(SC2, 0, 2, 4)
            pool.wait_ge(tp_free, 2 + 16)
            for t in range(T):
                pool.dma_start(u_g[:, t, :], ctx_in[t * P:(t + 1) * P, :]).then_inc(ctx_in_s, 16)
                if t == 0:
                    mod_block(SC1, 0, 4, 2)
            mod_block(GT1, 0, 2, 4)
            pool.dma_start(mgain[:, :], mid_g.rearrange("(a n) -> a n", a=1).partition_broadcast(P)).then_inc(mg_in, 16)
            mod_block(SH2, 0, 2, 2)
            with c.loop(pool, MLP_CHUNKS, 1, m=32, ma=80) as i:
                mod_block(SC2, i, 2, 2)
                mod_block(SC1, i, 4, 2)
                mod_block(GT1, i, 2, 4)
                mod_block(SH2, i, 2, 2)
            pool.wait_ge(h_added, H_MLP)
            pool.dma_start(wg[:, :, :], gates_w).then_inc(wg_in, 16)
            pool.memset(lrankT[RANK2:RANK2 + 1, :], 1.0).then_inc(pool_set, 1)
            with c.loop(pool, 4, m=8, ma=16) as i:
                mod_block(GT2, i, 2, 2)
            pool.wait_ge(tp_ready, T_O)
            pool.wait_ge(spill_s, 16)
            pool.dma_start(h[:, :, :], hspill.rearrange("t p d -> p t d")).then_inc(reload_s, 16)
            pool.wait_ge(h_added, H_MLP + 8)
            pool.dma_start(fgain[:, :], final_g.rearrange("(a n) -> a n", a=1).partition_broadcast(P))\
                .then_inc(fg_in, 16)

        @block.scalar
        def _(act):
            c = Counts()

            def round_groups(n, size=KG * NB):
                for _ in range(n):
                    g4, g2 = c.slot("g", WSLOTS), c.slot("g", HSLOTS)
                    act.wait_ge(group_landed[g4], c.landed("g", WSLOTS))
                    act.wait_ge(group_multiplied, c.at("g", 1))
                    act.activation(whi[:, g2, 0:size], wring[:, g4, 0:size], ACT.Copy).then_inc(hi_done, 1)
                    c.add("g")

            def wait_block(back):
                act.wait_ge(group_multiplied, c.at("g", HSLOTS - back))

            def round_banks(dst, tile, banks, gain=None):
                for b in range(banks):
                    src = tp[:, c.slot("q", 2), :].rearrange("p (j s) -> p j s", j=2)
                    act.wait_ge(tp_ready, c.at("q", 1))
                    t0 = tile + 2 * b
                    if gain is None:
                        act.activation(dst[:, t0:t0 + 2, :], src, ACT.Copy).then_inc(tp_hi, 1)
                    else:
                        act.activation(dst[:, t0, :], src[:, 0, :], ACT.Copy, scale=gain(t0)).then_inc(tp_hi, 1)
                        act.activation(dst[:, t0 + 1, :], src[:, 1, :], ACT.Copy, scale=gain(t0 + 1)).then_inc(tp_hi, 1)
                    c.add("q")

            def round_modulated(dst, b0, b1):
                for b in range(b0, b1):
                    act.wait_ge(tp_tmp, c.at("tmp", 1))
                    act.activation(dst[:, 2 * b:2 * b + 2, :],
                                   tmpT[:, b % 2, :].rearrange("p (j s) -> p j s", j=2), ACT.Copy).then_inc(tp_hi, 1)
                    c.add("tmp")
                    c.add("q")

            def opening(banks, late=0):
                banks(0, 4)
                round_groups(late)
                banks(4, 6)
                round_groups(1)
                banks(6, 8)
                round_groups(1)

            def square(src, col, piece, junk=m0):
                for t in range(T):
                    if c.n.get("ssq", 0):
                        act.wait_ge(ssq_done, c.at("ssq"))
                    act.activation(junk[:, :], src[:, t, bass.ds(col, NB)], ACT.Square,
                                   accum_out=squares[:, t, bass.ds(piece, 1)]).then_inc(ssq_done, 1)
                    c.add("ssq")

            def square_added(col, piece):
                act.wait_ge(h_added, c.at("ha", 1))
                square(h, col, piece)
                c.add("ha")

            def root(n):
                act.wait_ge(mean_done, n + 1)
                act.activation(ssq[:, n, :], ssq[:, n, :], ACT.Sqrt).then_inc(root_done, 1)

            def root_and_scale(n, src, dst):
                root(n)
                act.wait_ge(rstd_done, n + 1)
                act.activation(dst[:, 1, :], src[:, 1, :], ACT.Copy, scale=rstd[:, n, 1:2]).then_inc(u_done, 1)

            def norm(n, src, dst, junk=m0):
                for piece in range(KG):
                    square(src, piece * NB, piece, junk)
                root_and_scale(n, src, dst)

            act.dma_start(vrows[:, :, :], vectors).then_inc(start_in, 16)
            act.dma_start(tabs[:, :, :], tables).then_inc(start_in, 16)
            act.sem_inc(proj_set, 2)
            for piece in range(KG):
                act.wait_ge(x_in[piece], 16)
                if piece:
                    act.wait_ge(x_squares_a, piece)
                act.activation(acc[:, 0, :], h[:, 0, piece * NB:(piece + 1) * NB], ACT.Square,
                               accum_out=squares[:, 0, piece:piece + 1]).then_inc(x_squares_a, 1)
            root_and_scale(0, h, u_mix)
            act.wait_ge(vec_set, 1)

            round_groups(1)
            c.n["ha"] = H0

            def w_in_pair(i, first=False):
                for j in range(2):
                    if first and j == 0:
                        opening(lambda b0, b1: round_banks(xhi, 2 * b0, b1 - b0,
                                                           lambda k: vecs[:, 0, V_MIXG + k:V_MIXG + k + 1]), 1)
                        c_exponential()
                    else:
                        round_groups(2)
                    round_groups(2)
                    wait_block(2)
                    act.activation(proj[:, :, bass.ds(i * (2 * NB) + j * NB, NB)], acc[:, 2 * j:2 * j + 2, :],
                                   ACT.Copy).then_inc(proj_set, 1)

            def c_exponential():
                act.activation(csil[:, :, :].rearrange("p w k -> p (w k)"), vecs[:, 0, V_C:V_C + 2 * KT],
                               ACT.Exp, scale=-1.0).then_inc(c_exp, 1)

            w_in_pair(0, True)
            with c.loop(act, 4, 1, g=8) as i:
                w_in_pair(i)

            act.wait_ge(misc_in, 16 * 6)
            for s in range(HEADS + 1):
                g = s // 2
                if s < HEADS:
                    act.wait_ge(qk_turned, s + 1)
                    if s >= 2:
                        act.wait_ge(scores_done, s - 1)
                    act.activation(qkT[:, s % 2, 0, :], tp[:, 0, 0:S], ACT.Copy, scale=HD ** -0.5).then_inc(qk_copied, 1)
                    act.activation(qkT[:, s % 2, 1, :], tp[:, 0, S:2 * S], ACT.Copy).then_inc(qk_copied, 1)
                if s < HEADS and s % 2 == 0:
                    act.wait_ge(f1_done, g + 1)
                    if g:
                        act.wait_ge(f2_done, g)
                    act.activation(fpos[:, :, :], acc[:, 0:2, :], ACT.Copy).then_inc(f1_copied, 1)
                if s % 2:
                    act.wait_ge(f2_done, g + 1)
                    if g:
                        act.wait_ge(f3_done, g)
                    act.activation(fre, m0[:, :].rearrange("p (c s) -> p c s", c=2), ACT.Copy).then_inc(f2_copied, 1)
                if s:
                    act.wait_ge(probs_turned, s)
                    if s >= 2:
                        act.wait_ge(pv_done, s - 1)
                    act.activation(probsT, tp[:, 1, :].rearrange("p (c s) -> p c s", c=2), ACT.Copy).then_inc(probsT_copied, 1)
                if s < HEADS:
                    act.wait_ge(max_set, s + 1)
                    for t in range(T):
                        act.activation(probs[:, t * S:(t + 1) * S], sbias[:, t * S:(t + 1) * S], ACT.Exp,
                                       bias=nmax[:, s, t:t + 1]).then_inc(exps_done, 1)
                if s % 2:
                    act.wait_ge(f3_done, g + 1)
                    act.activation(xhi[:, 2 * g:2 * g + 2, :], m1[:, :].rearrange("p (c s) -> p c s", c=2),
                                   ACT.Copy).then_inc(f3_hi, 1)
                if s:
                    act.wait_ge(pv_done, s)
                    act.activation(xhi[:, 7 + s, :], acc[:, 3, 0:S], ACT.Copy).then_inc(pv_hi, 1)

            def added_pair(i):
                round_groups(5)
                square_added(i * (2 * NB), i * 2)
                round_groups(3)
                square_added(i * (2 * NB) + NB, i * 2 + 1)

            with c.loop(act, 2, g=8, ha=2, ssq=2 * T) as i:
                added_pair(i)
            root_and_scale(1, h, u_mlp)

            def relu_square(j):
                act.activation(blk2[:, :, :], acc[:, 2 * (j % 2):2 * (j % 2) + 2, :], ACT.Relu).then_inc(blk_half, 1)
                c.add("half")
                act.wait_ge(blk_half, c.at("half"))
                act.activation(blk[:, :, :], blk2[:, :, :], ACT.Square).then_inc(blk_ready, 1)
                c.add("blk")

            def square_block(n, first):
                if first:
                    act.wait_ge(ctx_in_s, 16 * T)
                    square(u_g, n * NB, n)
                    c.add("ha")
                else:
                    square_added(n * NB, n)

            def mlp_chunk(first=False):
                for j in range(8):
                    if first and j == 0:
                        opening(lambda b0, b1: round_banks(xhi, 2 * b0, b1 - b0,
                                                           lambda k: vecs[:, 0, V_MLPG + k:V_MLPG + k + 1]))
                    else:
                        round_groups(1)
                        if j >= 5:
                            square_block(j - 5, first)
                        round_groups(1)
                    if 1 <= j <= 4:
                        round_banks(ahi, 4 * (j - 1), 2)
                    round_groups(2)
                    if j < 4:
                        wait_block(2)
                        relu_square(j)
                square_block(3, first)

            mlp_chunk(True)
            root_and_scale(2, u_g, u_g)
            with c.loop(act, MLP_CHUNKS, 1, g=32, q=8, half=4, blk=4, ha=4, ssq=4 * T):
                mlp_chunk()

            def store_block(name, pair, x_pass):
                src = acc[:, 2 * pair:2 * pair + 2, :]
                if x_pass and name == "k":
                    act.wait_ge(state_step, STATE_STEPS[0] * GH)
                if name == "l":
                    act.wait_ge(pool_set, 2)
                    act.activation(lrankT[0:RANK2, :], acc[0:RANK2, 2 * pair, 0:S], ACT.Copy).then_inc(in_set, 1)
                elif name == "k":
                    act.activation(gk[:, :, :], src, ACT.Copy).then_inc(in_set, 1)
                elif name in ("v0", "v1"):
                    o = NB * int(name[1])
                    act.activation(gv[:, :, o:o + NB], src, ACT.Copy).then_inc(in_set, 1)
                elif name == "q":
                    act.activation(gq[:, :, :], src, ACT.Copy).then_inc(in_set, 1)
                elif name in ("cc0", "cc1"):
                    if name == "cc1":
                        act.wait_ge(tp_ready, c.at("q"))
                    act.activation(blk[:, :, :], src, ACT.Copy).then_inc(in_set, 1)
                elif name in ("cb0", "cb1"):
                    act.activation(blk2[:, :, :], src, ACT.Copy).then_inc(in_set, 1)
                elif name in ("g0", "g1"):
                    o = NB * int(name[1])
                    act.activation(silg[:, :, o:o + NB], src, ACT.Silu).then_inc(in_set, 1)

            def step(kind, p, a, b):
                if kind == "half_norm":
                    root(3)
                elif kind == "x_squares":
                    if a == 0:
                        act.wait_ge(u_done, 4 * T)
                        act.dma_start(hspill.rearrange("t p d -> p t d"), h[:, :, :]).then_inc(spill_s, 16)
                    for piece in (a, a + 1):
                        square(h, piece * NB, piece)
                elif kind == "x_norm":
                    act.wait_ge(spill_s, 16)
                    root_and_scale(4, h, h)
                elif kind == "z":
                    act.wait_ge(tp_ready, c.at("q", 1))
                    act.activation(la[:, a, b], tp[:, c.slot("q", 2), :], ACT.Abs).then_inc(la_step, 1)
                    act.wait_ge(la_step, c.at("la", 1))
                    act.activation(la[:, a, b], la[:, a, b], ACT.Exp, scale=-1.0).then_inc(la_step, 1)
                    act.wait_ge(la_step, c.at("la", 2))
                    act.activation(la[:, a, b], la[:, a, b], ACT.Ln, bias=1.0).then_inc(la_step, 1)
                    c.add("la", 3)
                elif kind == "suffix":
                    act.wait_ge(tp_ready, c.at("q", 1))
                    act.activation(kdec[:, a, b], tp[:, c.slot("q", 2), :], ACT.Exp).then_inc(kdec_exp, 1)
                elif kind == "cum":
                    hd = a
                    act.wait_ge(cum_done, GH * p + hd + 1)
                    if p or hd:
                        act.wait_ge(state_step, STATE_STEPS[p] * hd + STATE_STEPS[0] * GH * p)
                    if p and hd:
                        act.wait_ge(qe_done, 4 * hd)
                    act.activation(epos[:, :, :], m0[:, :].rearrange("p (d s) -> p d s", d=2), ACT.Exp).then_inc(cum_exp, 1)
                    if p:
                        act.activation(eneg, m0[:, :].rearrange("p (d s) -> p d s", d=2), ACT.Exp, scale=-1.0).then_inc(cum_exp, 1)
                elif kind == "out":
                    act.wait_ge(tp_ready, c.at("q", 1))
                    for t in range(T):
                        o = tp[:, c.slot("q", 2), t * DV:(t + 1) * DV]
                        act.activation(o_all[:, t, a * DV:(a + 1) * DV], o, ACT.Copy).then_inc(o_copied, 1)
                        act.activation(tmpT[:, 1, t * DV:(t + 1) * DV], o, ACT.Square,
                                       accum_out=oss[:, t, a:a + 1]).then_inc(o_copied, 1)
                c.add("q", BANKS.get(kind, 0))

            def in_blocks(names, b0, p):
                for n, name in enumerate(names):
                    following = (names + (("w_out",) if p else ("cc0",)))[n + 1]
                    if n == 0:
                        opening(lambda b0, b1: round_modulated(xhi, b0, b1))
                    for kg in range(2 if name == "l" else 4):
                        last = kg == (1 if name == "l" else 3)
                        if name == "l":
                            round_groups(1)
                        elif n == 0 and kg < 2:
                            continue
                        elif kg < 2:
                            round_groups(1)
                        else:
                            round_groups(1, 8 * RANK2 if following == "l" else KG * NB)
                        if last:
                            wait_block(2)
                            store_block(name, (b0 + n) % 2, p)
                        for st in BESIDE[p].get((name, kg), ()):
                            step(*st)

            in_blocks(C_IN, 44, 0)
            in_blocks(X_IN, 48, 1)
            act.wait_ge(conv_step, 8 * 4)
            for half in range(2):
                tiles = slice(4 * half, 4 * half + 4)
                act.activation(xhi[:, 8 + 4 * half:12 + 4 * half, :], convT[:, tiles, :], ACT.Copy).then_inc(conv_hi, 1)
            step("out", 1, GH - 1, 0)
            act.wait_ge(o_mean, 1)
            act.activation(oss[:, :, :], oss[:, :, :], ACT.Sqrt).then_inc(o_root, 1)
            round_groups(3)
            round_banks(xhi, 0, 4, lambda k: vecs[:, 2, 24 + k % 2:25 + k % 2])

            c.add("q", 8)
            round_groups(3)
            square_added(0, 0)
            round_groups(2)
            square_added(NB, 1)
            added_pair(1)
            root_and_scale(5, h, u_ffn)

            def silu_gate(pair):
                act.wait_ge(blk_ready, c.at("blk"))
                act.wait_ge(h_added, c.at("ha"))
                act.activation(blk2[:, :, :], acc[:, 2 * pair:2 * pair + 2, :], ACT.Silu).then_inc(blk_half, 1)
                c.add("half")

            def ffn(blocks, first=False):
                for j in range(blocks):
                    if first and j == 0:
                        opening(lambda b0, b1: round_modulated(xhi, b0, b1))
                    else:
                        round_groups(2)
                    if j:
                        round_banks(bhi, 4 * (j - 1), 2)
                    round_groups(2)
                    wait_block(2)
                    silu_gate(0)
                    round_groups(4)
                    c.add("blk")
                for n in range(4):
                    last = blocks < 4
                    round_groups(blocks - 2)
                    if n == 0:
                        round_banks(bhi, 4 * (blocks - 1), 2)
                    if last and n:
                        square_added((n - 1) * NB, n - 1)
                    if not (last and n == 3):
                        round_groups(2)
                if last:
                    square_added(3 * NB, 3)
                else:
                    c.add("ha", 4)

            c.n["blk"] = 4 * MLP_CHUNKS + 2
            ffn(4, True)
            with c.loop(act, 2, 1, g=48, q=8, half=4, blk=4, ha=4):
                ffn(4)
            ffn(LAST_CHUNK)
            root(6)
            act.wait_ge(fg_in, 16)
            for t in range(T):
                act.wait_ge(final_set, t + 1)
                act.dma_start(out[t * P:(t + 1) * P, :], u_ffn[:, t, :]).then_inc(out_s, 16)
            act.wait_ge(out_s, 32)

        @block.vector
        def _(dve):
            c = Counts()

            def remainders(n, size=KG * NB):
                for _ in range(n):
                    g4, g2 = c.slot("g", WSLOTS), c.slot("g", HSLOTS)
                    dve.wait_ge(hi_done, c.at("g", 1))
                    dve.tensor_tensor(wlo[:, g2, 0:size], wring[:, g4, 0:size], whi[:, g2, 0:size].bitcast(F32),
                                      ALU.subtract).then_inc(lo_done, 1)
                    c.add("g")

            def wait_block(back):
                dve.wait_ge(group_multiplied, c.at("g", HSLOTS - back))

            def mod_steps(n, s0, dual):
                for s in range(s0, s0 + n):
                    m2 = c.slot("m", MSLOTS)
                    dve.wait_ge(step_landed[m2], c.landed("m", MSLOTS))
                    for kt in range(2):
                        k = 2 * s + kt
                        for who in range(2 if dual else 1):
                            if k == 0:
                                dve.tensor_scalar(macc[:, who, :], mring[:, m2, kt, :], csil[:, who, k:k + 1], None,
                                                  ALU.mult).then_inc(mod_acc, 1)
                            else:
                                dve.wait_ge(mod_acc, c.at("ma", 8 - (1 if dual else 0)))
                                dve.scalar_tensor_tensor(macc[:, who, :], mring[:, m2, kt, :], csil[:, who, k:k + 1],
                                                         macc[:, who, :], ALU.mult, ALU.add).then_inc(mod_acc, 1)
                            c.add("ma")
                    c.add("m")

            def set_mod(kind, i, dual):
                dve.wait_ge(mod_reduced, c.at("mb", 1))
                for who in range(2 if dual else 1):
                    dve.tensor_tensor(modT[:, who, bass.ds(i * 4 + kind * KT, 4)], m1[:, 4 * who:4 * who + 4],
                                      vecs[:, 1, bass.ds(i * 4 + kind * KT, 4)], ALU.add).then_inc(mod_set, 1)
                c.add("mb")

            def remain_banks(hi, lo, tile, banks, gain=None):
                for b in range(banks):
                    src = tp[:, c.slot("q", 2), :].rearrange("p (j s) -> p j s", j=2)
                    t0 = tile + 2 * b
                    dve.wait_ge(tp_hi, c.at("hi", 1 if gain is None else 2))
                    c.add("hi", 1 if gain is None else 2)
                    if gain is None:
                        dve.tensor_tensor(lo[:, t0:t0 + 2, :], src, hi[:, t0:t0 + 2, :].bitcast(F32), ALU.subtract).then_inc(tp_free, 1)
                    else:
                        dve.scalar_tensor_tensor(lo[:, t0, :], src[:, 0, :], gain(t0), hi[:, t0, :].bitcast(F32),
                                                 ALU.mult, ALU.subtract)
                        dve.scalar_tensor_tensor(lo[:, t0 + 1, :], src[:, 1, :], gain(t0 + 1), hi[:, t0 + 1, :].bitcast(F32),
                                                 ALU.mult, ALU.subtract).then_inc(tp_free, 1)
                    c.add("q")

            def opening(banks, late=0):
                banks(0, 4)
                remainders(late)
                banks(4, 6)
                remainders(1)
                banks(6, 8)
                remainders(1)

            def modulate(hi, lo, b0, b1, gain, shift):
                def remainder(b):
                    dve.wait_ge(tp_hi, c.at("hi", 1))
                    dve.tensor_tensor(lo[:, 2 * b:2 * b + 2, :], tmpT[:, b % 2, :].rearrange("p (j s) -> p j s", j=2),
                                      hi[:, 2 * b:2 * b + 2, :].bitcast(F32), ALU.subtract).then_inc(tp_free, 1)
                    c.add("hi")

                for b in range(b0, b1):
                    q = c.slot("q", 2)
                    dve.wait_ge(tp_ready, c.at("q", 1))
                    dve.tensor_scalar(tmpT[:, b % 2, 0:S], tp[:, q, 0:S], gain(2 * b), shift(2 * b), ALU.mult, ALU.add)
                    dve.tensor_scalar(tmpT[:, b % 2, S:2 * S], tp[:, q, S:2 * S], gain(2 * b + 1), shift(2 * b + 1),
                                      ALU.mult, ALU.add).then_inc(tp_tmp, 1)
                    c.add("q")
                    if b > b0:
                        remainder(b - 1)
                remainder(b1 - 1)

            def norm_root(n):
                if n:
                    dve.wait_ge(ssq_done, c.at("ssq"))
                dve.reduce_sum(ssq[:, n, :], squares[:, :, :], AX_X).then_inc(squares_summed, 1)
                dve.wait_ge(squares_summed, n + 1)
                dve.tensor_scalar(ssq[:, n, :], ssq[:, n, :], 1.0 / D, EPS, ALU.mult, ALU.add).then_inc(mean_done, 1)
                dve.wait_ge(root_done, n + 1)
                dve.reciprocal(rstd[:, n, :], ssq[:, n, :]).then_inc(rstd_done, 1)
                dve.wait_ge(rstd_done, n + 1)

            def norm_scale(n, src, dst):
                norm_root(n)
                dve.tensor_scalar(dst[:, 0, :], src[:, 0, :], rstd[:, n, 0:1], None, ALU.mult).then_inc(u_done, 1)

            dve.sem_inc(mod_acc, 8)
            dve.sem_inc(lo_done, WSLOTS)
            dve.sem_inc(h_added, H0)
            dve.sem_inc(tp_free, 2)
            for piece in range(KG):
                dve.wait_ge(x_in[piece], 16)
                if piece:
                    dve.wait_ge(x_squares_v, piece)
                xs = h[:, 1, piece * NB:(piece + 1) * NB]
                dve.scalar_tensor_tensor(acc[:, 1, :], xs, 1.0, xs, ALU.mult, ALU.mult,
                                         accum_out=squares[:, 1, piece:piece + 1]).then_inc(x_squares_v, 1)
            dve.wait_ge(x_squares_a, KG)
            dve.wait_ge(x_squares_v, KG)
            norm_scale(0, h, u_mix)
            dve.wait_ge(vec_turned, 3)
            dve.tensor_copy(vecs[:, :, :], m0[:, 0:3 * P].rearrange("p (a b) -> p a b", a=3)).then_inc(vec_set, 1)
            remainders(1)

            def w_in_pair(i, first=False):
                for g in range(8):
                    if first and g == 0:
                        opening(lambda b0, b1: remain_banks(xhi, xlo, 2 * b0, b1 - b0,
                                                            lambda k: vecs[:, 0, V_MIXG + k:V_MIXG + k + 1]), 1)
                        c_silu()
                    elif not first and g == 1:
                        mod_steps(1, 7, True)
                        remainders(1)
                        set_mod(SH1, i - 1, True)
                    elif g != 1:
                        remainders(1)
                    if g >= 2:
                        mod_steps(1, g - 2, True)
                    elif not first and g == 0:
                        mod_steps(1, 6, True)

            def c_silu():
                dve.wait_ge(c_exp, 1)
                csil_flat = csil[:, :, :].rearrange("p w k -> p (w k)")
                dve.tensor_scalar(csil_flat, csil_flat, 1.0, None, ALU.add).then_inc(c_sil, 1)
                dve.wait_ge(c_sil, 1)
                dve.reciprocal(csil_flat, csil_flat).then_inc(c_sil, 1)
                dve.wait_ge(c_sil, 2)
                dve.tensor_tensor(csil_flat, csil_flat, vecs[:, 0, V_C:V_C + 2 * KT], ALU.mult).then_inc(c_sil, 1)
                dve.wait_ge(c_sil, 3)

            w_in_pair(0, True)
            with c.loop(dve, 4, 1, g=8, m=8, ma=32, mb=1) as i:
                w_in_pair(i)

            dve.wait_ge(misc_in, 16 * 6)
            for s in range(HEADS + 1):
                g = s // 2
                if s < HEADS:
                    dve.wait_ge(scores_done, s + 1)
                    if s:
                        dve.wait_ge(exps_done, T * s)
                    dve.scalar_tensor_tensor(sbias, tab_a[:, 0, :], 2.0 ** (-8.0 * (s + 1) / HEADS), acc[:, 2, :],
                                             ALU.mult, ALU.add).then_inc(scores_biased, 1)
                    dve.wait_ge(scores_biased, s + 1)
                    dve.reduce_max(nmax[:, s, :], sbias.rearrange("p (t k) -> p t k", t=T), AX_X, negate=True).then_inc(max_set, 1)
                if s % 2:
                    dve.wait_ge(f3_hi, g + 1)
                    dve.tensor_tensor(xlo[:, 2 * g:2 * g + 2, :], m1[:, :].rearrange("p (c s) -> p c s", c=2),
                                      xhi[:, 2 * g:2 * g + 2, :].bitcast(F32), ALU.subtract).then_inc(f3_lo, 1)
                if s:
                    dve.wait_ge(pv_hi, s)
                    dve.tensor_tensor(xlo[:, 7 + s, :], acc[:, 3, 0:S], xhi[:, 7 + s, :].bitcast(F32),
                                      ALU.subtract).then_inc(pv_lo, 1)
                if s < HEADS:
                    for t in range(T):
                        dve.wait_ge(exps_done, T * s + t + 1)
                        dve.scalar_tensor_tensor(probs[:, t * S:(t + 1) * S], probs[:, t * S:(t + 1) * S], 1.0,
                                                 tab_a[:, 1, t * S:(t + 1) * S], ALU.mult, ALU.mult,
                                                 accum_out=aden[:, s, t:t + 1]).then_inc(probs_summed, 1)
                    dve.wait_ge(probs_summed, T * (s + 1))
                    dve.reciprocal(arden[:, s, :], aden[:, s, :]).then_inc(den_inverted, 1)
                    dve.wait_ge(den_inverted, s + 1)
                    for t in range(T):
                        dve.tensor_scalar(probs[:, t * S:(t + 1) * S], probs[:, t * S:(t + 1) * S],
                                          arden[:, s, t:t + 1], None, ALU.mult).then_inc(probs_ready, 1)
                if s == HEADS - 2:
                    mod_steps(2, 6, True)
            set_mod(SH1, 3, True)

            def add_block(n, pair):
                dve.tensor_tensor(h[:, :, bass.ds(n, NB)], acc[:, 2 * pair:2 * pair + 2, :], h[:, :, bass.ds(n, NB)],
                                  ALU.add).then_inc(h_added, 1)

            with c.loop(dve, 2, g=8) as i:
                for pair in range(2):
                    remainders(3)
                    wait_block(1)
                    add_block(i * (2 * NB) + pair * NB, pair)
                    remainders(1)
            c.add("ssq", T * KG)
            norm_scale(1, h, u_mlp)

            def mlp_chunk(i, first=False):
                done = 0
                for g in range(32):
                    j = g // 4
                    if first and g < 2:
                        if g == 0:
                            opening(lambda b0, b1: remain_banks(xhi, xlo, 2 * b0, b1 - b0,
                                                                lambda k: vecs[:, 0, V_MLPG + k:V_MLPG + k + 1]))
                    elif g < 31:
                        remainders(1)
                    if g % 4 == 1 and 1 <= j <= 4:
                        remain_banks(ahi, alo, 4 * (j - 1), 2)
                    if g in MLP_REDUCED:
                        set_mod(MLP_REDUCED[g], i, MLP_REDUCED[g] == SC1)
                    if g in MLP_MODS:
                        kind, n = MLP_MODS[g]
                        mod_steps(n, done % MSTEPS, kind == SC1)
                        done += n
                    if g % 4 == 3 and j >= 4:
                        wait_block(2 if g < 31 else 1)
                        add_block((j - 4) * NB, j % 2)
                    if g == 31:
                        remainders(1)

            mlp_chunk(0, True)
            c.add("ssq", T * KG)
            norm_scale(2, u_g, u_g)
            with c.loop(dve, MLP_CHUNKS, 1, g=32, q=8, hi=8, m=32, ma=80, mb=4) as i:
                mlp_chunk(i)
            c.add("ssq", (MLP_CHUNKS - 1) * T * KG)

            def store_block(name, pair):
                src = acc[:, 2 * pair:2 * pair + 2, :]
                if name in ("cx0", "cx1"):
                    dve.wait_ge(in_set, IN_SET[1]["cc" + name[2]])
                    dve.tensor_tensor(blk[:, :, :], blk[:, :, :], src, ALU.mult).then_inc(blk_ready, 1)

            def conv(half, pr):
                qu, qb = c.slot("q", 2), (c.slot("q", 2) + 1) % 2
                dve.wait_ge(tp_ready, c.at("q", 2))
                for j in range(2):
                    ch = 4 * half + 2 * pr + j
                    n = 4 * ch
                    y = convT[:, ch, :]
                    yr = y.rearrange("p (r w) -> p r w", w=GRID)
                    u = tp[:, qu, j * S:(j + 1) * S]
                    ur = u.rearrange("p (r w) -> p r w", w=GRID)
                    tap = [vecs[:, 2, 8 * k + ch:8 * k + ch + 1] for k in range(3)]
                    dve.tensor_scalar(y, u, tap[1], None, ALU.mult).then_inc(conv_step, 1)
                    dve.wait_ge(conv_step, n + 1)
                    dve.scalar_tensor_tensor(yr[:, :, 1:GRID], ur[:, :, 0:GRID - 1], tap[0], yr[:, :, 1:GRID],
                                             ALU.mult, ALU.add).then_inc(conv_step, 1)
                    dve.wait_ge(conv_step, n + 2)
                    dve.scalar_tensor_tensor(yr[:, :, 0:GRID - 1], ur[:, :, 1:GRID], tap[2], yr[:, :, 0:GRID - 1],
                                             ALU.mult, ALU.add).then_inc(conv_step, 1)
                    dve.wait_ge(conv_step, n + 3)
                    dve.tensor_tensor(y, y, tp[:, qb, j * S:(j + 1) * S], ALU.mult).then_inc(conv_step, 1)
                dve.wait_ge(conv_step, n + 4)
                dve.sem_inc(tp_free, 2)
                c.add("q", 2)

            def step(kind, p, a, b):
                q = c.slot("q", 2)
                if kind == "half_norm":
                    norm_root(3)
                elif kind == "mid_norm":
                    dve.wait_ge(mg_in, 16)
                    dve.scalar_tensor_tensor(h[:, a, :], h[:, a, :], rstd[:, 3, a:a + 1], mgain[:, :],
                                             ALU.mult, ALU.mult).then_inc(u_done, 1)
                elif kind == "x_norm":
                    c.add("ssq", T * KG)
                    dve.wait_ge(spill_s, 16)
                    norm_scale(4, h, h)
                elif kind == "z":
                    dve.wait_ge(la_step, c.at("la", 3))
                    dve.scalar_tensor_tensor(la[:, a, b], tp[:, q, :], 0.0, la[:, a, b], ALU.min, ALU.subtract).then_inc(tp_free, 1)
                    c.add("la", 3)
                elif kind == "suffix":
                    dve.wait_ge(kdec_exp, c.at("kd", 1))
                    dve.tensor_tensor(kdec[:, a, b], kdec[:, a, b], gk[:, a, :], ALU.mult).then_inc(tp_free, 1)
                    c.add("kd")
                elif kind == "turn":
                    hd = a
                    dve.wait_ge(cum_exp, GH + 2 * (hd + 1))
                    dve.wait_ge(tp_ready, c.at("q", 1))
                    if hd == 0:
                        dve.memset(sc, 0.0).then_inc(sc_zeroed, 1)
                        dve.wait_ge(sc_zeroed, 1)
                    for d in range(2):
                        dve.scalar_tensor_tensor(qe[:, d, :], tp[:, q, 0:S], DK ** -0.5, epos[:, d, :],
                                                 ALU.mult, ALU.mult).then_inc(qe_done, 1)
                        dve.tensor_tensor(ke[:, d, :], tp[:, q, S:2 * S], eneg[:, d, :], ALU.mult).then_inc(qe_done, 1)
                    dve.wait_ge(qe_done, 4 * (hd + 1))
                    dve.sem_inc(tp_free, 1)
                elif kind == "scores":
                    dve.wait_ge(gsc_done, a + 1)
                    for d in range(2):
                        for t in range(T):
                            dve.copy_predicated(sc[:, d, t, :], keep[d], m1[:, (2 * d + t) * P:(2 * d + t + 1) * P]).then_inc(gsc_kept, 1)
                elif kind == "state":
                    hd, d = a, b
                    dve.wait_ge(cum_exp, hd + 1 if p == 0 else GH + 2 * (hd + 1))
                    dve.wait_ge(tp_ready, c.at("q", 2))
                    for n in range(NCH if p == 0 else NCH - 1):
                        ck = ORDER[d][n]
                        decay = epos[:, d, CH * ck + CH - 1:CH * ck + CH] if d == 0 else epos[:, d, CH * ck:CH * ck + 1]
                        ds = tp[:, (q + ck % 2) % 2, (ck // 2) * DV:(ck // 2 + 1) * DV]
                        if p == 0 and n == 0:
                            dve.tensor_copy(states[:, d, hd, :], ds).then_inc(state_step, 1)
                        else:
                            if n:
                                dve.wait_ge(state_step, c.at("st"))
                            src = gst[:, d, ck, :] if p and n else states[:, d, hd, :]
                            dst = gst[:, d, ORDER[d][n + 1], :] if p else states[:, d, hd, :]
                            dve.scalar_tensor_tensor(dst, src, decay, ds, ALU.mult, ALU.add).then_inc(state_step, 1)
                        c.add("st")
                    dve.wait_ge(state_step, c.at("st"))
                    dve.sem_inc(tp_free, 2)
                elif kind == "out":
                    dve.wait_ge(o_copied, 4 * (a + 1))
                    dve.sem_inc(tp_free, 1)
                if kind == "conv":
                    conv(a, b)
                else:
                    c.add("q", BANKS.get(kind, 0))

            def in_blocks(names, p, hi, lo, gain, shift):
                for n, name in enumerate(names):
                    following = (names + (("w_out",) if p else ("cc0",)))[n + 1]
                    if n == 0:
                        opening(lambda b0, b1: modulate(hi, lo, b0, b1, gain, shift))
                    which, part = MOD_PAIRS[p].get(name, (None, 0))
                    for kg in range(2 if name == "l" else 4):
                        last = kg == (1 if name == "l" else 3)
                        if n == 0 and kg < 2:
                            continue
                        remainders(1, 8 * RANK2 if name != "l" and kg >= 2 and following == "l" else KG * NB)
                        if last:
                            wait_block(2)
                            store_block(name, (48 + n) % 2)
                        for st in BESIDE[p].get((name, kg), ()):
                            step(*st)
                        if which is not None:
                            k = 4 * part + kg
                            mod_steps(SPREAD[k], sum(SPREAD[0:k]), False)
                            if k == 7:
                                set_mod(GT2, which, False)

            dve.wait_ge(mod_set, 8 + MLP_CHUNKS * 5)
            for who in range(2):
                dve.scalar_tensor_tensor(gain1[:, who, :], modT[:, who, SC1 * KT:(SC1 + 1) * KT], 1.0,
                                         vecs[:, 0, V_N1G:V_N1G + KT], ALU.add, ALU.mult).then_inc(gain_set, 1)
            dve.wait_ge(gain_set, 2)
            in_blocks(C_IN, 0, xhi, xlo, lambda k: gain1[:, 1, k:k + 1], lambda k: modT[:, 1, SH1 * KT + k:SH1 * KT + k + 1])
            in_blocks(X_IN, 1, xhi, xlo, lambda k: gain1[:, 0, k:k + 1], lambda k: modT[:, 0, SH1 * KT + k:SH1 * KT + k + 1])
            for half in range(2):
                tiles = slice(8 + 4 * half, 12 + 4 * half)
                dve.wait_ge(conv_hi, half + 1)
                dve.tensor_tensor(xlo[:, tiles, :], convT[:, 4 * half:4 * half + 4, :], xhi[:, tiles, :].bitcast(F32),
                                  ALU.subtract).then_inc(conv_lo, 1)
            step("out", 1, GH - 1, 0)
            dve.wait_ge(o_copied, 4 * GH)
            dve.tensor_scalar(oss[:, :, :], oss[:, :, :], 1.0 / DV, EPS, ALU.mult, ALU.add).then_inc(o_mean, 1)
            dve.wait_ge(o_root, 1)
            dve.reciprocal(orstd[:, :, :], oss[:, :, :]).then_inc(o_rstd, 1)
            dve.wait_ge(o_rstd, 1)
            for hd in range(GH):
                for t in range(T):
                    o = o_all[:, t, hd * DV:(hd + 1) * DV]
                    dve.scalar_tensor_tensor(o, o, orstd[:, t, hd:hd + 1], silg[:, t, hd * DV:(hd + 1) * DV],
                                             ALU.mult, ALU.mult).then_inc(o_gated, 1)
            remainders(3)
            remain_banks(xhi, xlo, 0, 4, lambda k: vecs[:, 2, 24 + k % 2:25 + k % 2])

            for which in range(2):
                for b in range(4):
                    dve.wait_ge(tp_ready, c.at("q", 1))
                    dve.tensor_copy(gates[:, which, b * NB:(b + 1) * NB], tp[:, c.slot("q", 2), :]).then_inc(tp_free, 1)
                    c.add("q")
                remainders(1)
            dve.wait_ge(tp_free, c.at("q", 2))

            def gated_add(which, n, pair):
                gate = gates[:, which, bass.ds(n, NB)].unsqueeze(1).broadcast_to([P, T, NB])
                dve.tensor_tensor(blk2[:, :, :], acc[:, 2 * pair:2 * pair + 2, :], gate, ALU.mult).then_inc(h_scaled, 1)
                c.add("hs")
                dve.wait_ge(h_scaled, c.at("hs"))
                dve.tensor_tensor(h[:, :, bass.ds(n, NB)], blk2[:, :, :], h[:, :, bass.ds(n, NB)], ALU.add).then_inc(h_added, 1)
                c.add("ha")

            wait_block(1)
            dve.wait_ge(reload_s, 16)
            gated_add(0, 0, 0)
            remainders(2)
            wait_block(1)
            gated_add(0, NB, 1)
            remainders(1)
            for n in range(2, 4):
                remainders(3)
                wait_block(1)
                gated_add(0, n * NB, n % 2)
                remainders(1)
            dve.scalar_tensor_tensor(gain2[:, :], modT[:, 0, SC2 * KT:(SC2 + 1) * KT], 1.0,
                                     vecs[:, 0, V_N2G:V_N2G + KT], ALU.add, ALU.mult).then_inc(gain_set, 1)
            c.add("ssq", T * KG)
            norm_scale(5, h, u_ffn)
            dve.wait_ge(gain_set, 3)

            def gate_up():
                dve.wait_ge(blk_half, c.at("half", 1))
                dve.tensor_tensor(blk[:, :, :], blk2[:, :, :], acc[:, 2:4, :], ALU.mult).then_inc(blk_ready, 1)
                c.add("half")

            def ffn(blocks, first=False):
                for j in range(blocks):
                    if first and j == 0:
                        opening(lambda b0, b1: modulate(xhi, xlo, b0, b1, lambda k: gain2[:, k:k + 1],
                                                        lambda k: modT[:, 0, SH2 * KT + k:SH2 * KT + k + 1]))
                    else:
                        remainders(2)
                    if j:
                        remain_banks(bhi, blo, 4 * (j - 1), 2)
                    remainders(6)
                    wait_block(2)
                    gate_up()
                for n in range(4):
                    remainders(blocks - 2)
                    if n == 0:
                        remain_banks(bhi, blo, 4 * (blocks - 1), 2)
                    if blocks < 4 and n == 3:
                        wait_block(0)
                    else:
                        remainders(2)
                        wait_block(2)
                    gated_add(1, n * NB, n % 2)

            c.n["half"] = 4 * MLP_CHUNKS
            ffn(4, True)
            with c.loop(dve, 2, 1, g=48, q=8, hi=8, half=4, hs=4, ha=4):
                ffn(4)
            ffn(LAST_CHUNK)
            c.add("ssq", T * KG)
            norm_root(6)
            dve.wait_ge(fg_in, 16)
            for t in range(T):
                dve.scalar_tensor_tensor(u_ffn[:, t, :], h[:, t, :], rstd[:, 6, t:t + 1], fgain[:, :],
                                         ALU.mult, ALU.mult).then_inc(final_set, 1)

        @block.tensor
        def _(pe):
            c = Counts()

            def multiply_rank(half, pair):
                g2 = c.slot("g", HSLOTS)
                pe.wait_ge(lo_done, c.at("g", WSLOTS + 1))
                dst = acc[0:RANK2, 2 * pair, 0:S]
                for k in range(8):
                    tile = half * 8 + k
                    w = slice(k * RANK2, (k + 1) * RANK2)
                    pe.matmul(dst, whi[:, g2, w], xhi[:, tile, :], start=(tile == 0), stop=False)
                    pe.matmul(dst, wlo[:, g2, w], xhi[:, tile, :], start=False, stop=False)
                    last = pe.matmul(dst, whi[:, g2, w], xlo[:, tile, :], start=False, stop=(tile == KT - 1))
                last.then_inc(group_multiplied, 1)
                c.add("g")

            def multiply(hi, lo, kgs, kgroups, pair, order=None):
                first, final = (order[0], order[-1]) if order else (0, kgroups - 1)
                kts, width = KG, NB
                for kg in kgs:
                    g2 = c.slot("g", HSLOTS)
                    pe.wait_ge(lo_done, c.at("g", WSLOTS + 1))
                    for k in range(kts):
                        tile = kg * kts + k
                        w = slice(k * width, (k + 1) * width)
                        for t in range(T):
                            dst = acc[:, 2 * pair + t, 0:width]
                            rows = slice(t * P, (t + 1) * P)
                            pe.matmul(dst, hi[:, tile, rows], whi[:, g2, w], start=(kg == first and k == 0), stop=False)
                            pe.matmul(dst, hi[:, tile, rows], wlo[:, g2, w], start=False, stop=False)
                            last = pe.matmul(dst, lo[:, tile, rows], whi[:, g2, w], start=False,
                                             stop=(kg == final and k == kts - 1))
                    last.then_inc(group_multiplied, 1)
                    c.add("g")

            def turn_rows(src, banks, b0=0):
                for b in range(b0, b0 + banks):
                    q = c.slot("q", 2)
                    pe.wait_ge(tp_free, c.at("q", 1))
                    for j in range(2):
                        for t in range(T):
                            f = (2 * b + j) * P
                            last = pe.transpose(tp[:, q, j * S + t * P:j * S + (t + 1) * P], src[:, t, f:f + P], ident)
                    last.then_inc(tp_ready, 1)
                    c.add("q")

            def reduce_mod(per_nb, dual):
                c.add("ma", per_nb)
                pe.wait_ge(mod_acc, c.at("ma", 8))
                for who in range(2 if dual else 1):
                    for j in range(4):
                        last = pe.matmul(m1[:, 4 * who + j:4 * who + j + 1], macc[:, who, j * P:(j + 1) * P],
                                         ones[:, 0:1], start=True, stop=True)
                last.then_inc(mod_reduced, 1)

            def opening(src, pair):
                turn_rows(src, 4)
                multiply(xhi, xlo, (0,), 4, pair)
                turn_rows(src, 2, 4)
                multiply(xhi, xlo, (1,), 4, pair)
                turn_rows(src, 2, 6)
                multiply(xhi, xlo, (2,), 4, pair)
                pe.wait_ge(tp_free, c.at("q", 2))
                multiply(xhi, xlo, (3,), 4, pair)

            pe.sem_inc(group_multiplied, HSLOTS)
            pe.wait_ge(start_in, 32)
            for a in range(3):
                pe.transpose(m0[:, a * P:(a + 1) * P], vrows[:, a, :], ident).then_inc(vec_turned, 1)
            pe.wait_ge(u_done, T)
            pe.wait_ge(pool_set, 1)

            for n in range(8):
                pe.wait_ge(proj_set, c.at("ps", 1))
                if n == 0:
                    opening(u_mix, 0)
                else:
                    multiply(xhi, xlo, range(3), 4, n % 2)
                    if n % 2 == 0:
                        reduce_mod(32, True)
                    multiply(xhi, xlo, (3,), 4, n % 2)
                c.add("ps")

            pe.wait_ge(proj_set, 2 + 8)
            pe.wait_ge(misc_in, 16 * 6)
            for s in range(HEADS + 1):
                g = s // 2
                if s < HEADS:
                    if s:
                        pe.wait_ge(qk_copied, 2 * s)
                    for w, col in ((0, 2 * NB), (1, 4 * NB)):
                        for t in range(T):
                            last = pe.transpose(tp[:, 0, w * S + t * P:w * S + (t + 1) * P],
                                                proj[:, t, col + s * HD:col + (s + 1) * HD], ident)
                    last.then_inc(qk_turned, 1)
                if s < HEADS and s % 2 == 0:
                    if g:
                        pe.wait_ge(f1_copied, g)
                    for ct in range(2):
                        for t in range(T):
                            last = pe.matmul(acc[:, ct, :], proj[:, t, g * FDIM + ct * P:g * FDIM + (ct + 1) * P],
                                             tab_f[:, t, 0:2 * S], start=(t == 0), stop=(t == T - 1))
                    last.then_inc(f1_done, 1)
                if s % 2:
                    pe.wait_ge(f1_copied, g + 1)
                    if g:
                        pe.wait_ge(f2_copied, g)
                    for cc in range(2):
                        for n, (part, ct) in enumerate(((0, 0), (0, 1), (1, 0), (1, 1))):
                            last = pe.matmul(m0[:, cc * S:(cc + 1) * S],
                                             tab_f[:, ct, part * 2 * S + cc * P:part * 2 * S + (cc + 1) * P],
                                             fpos[:, ct, part * S:(part + 1) * S], start=(n == 0), stop=(n == 3))
                    last.then_inc(f2_done, 1)
                if s < HEADS:
                    pe.wait_ge(qk_copied, 2 * (s + 1))
                    if s:
                        pe.wait_ge(scores_biased, s)
                    for t in range(T):
                        last = pe.matmul(acc[:, 2, t * S:(t + 1) * S], qkT[:, s % 2, 0, t * P:(t + 1) * P],
                                         qkT[:, s % 2, 1, :], start=True, stop=True)
                    last.then_inc(scores_done, 1)
                if s == HEADS:
                    pe.wait_ge(f3_lo, FGROUPS)
                    pe.wait_ge(h_added, c.at("ha", 1))
                    multiply(xhi, xlo, (0, 1), 4, 0)
                if s:
                    pe.wait_ge(probs_ready, T * s)
                    if s >= 2:
                        pe.wait_ge(probsT_copied, s - 1)
                    for kt in range(2):
                        for t in range(T):
                            last = pe.transpose(tp[:, 1, kt * S + t * P:kt * S + (t + 1) * P],
                                                probs[:, t * S + kt * P:t * S + (kt + 1) * P], ident)
                    last.then_inc(probs_turned, 1)
                if s % 2:
                    pe.wait_ge(f2_copied, g + 1)
                    if g:
                        pe.wait_ge(f3_lo, g)
                    for e in range(2):
                        for cc in range(2):
                            last = pe.matmul(m1[:, e * S:(e + 1) * S], wf[:, g, cc, e * P:(e + 1) * P], fre[:, cc, :],
                                             start=(cc == 0), stop=(cc == 1))
                    last.then_inc(f3_done, 1)
                if s:
                    pe.wait_ge(probsT_copied, s)
                    if s >= 2:
                        pe.wait_ge(pv_lo, s - 1)
                    v = 6 * NB + (s - 1) * HD
                    for kt in range(2):
                        last = pe.matmul(acc[:, 3, 0:S], proj[:, kt, v:v + HD], probsT[:, kt, :],
                                         start=(kt == 0), stop=(kt == 1))
                    last.then_inc(pv_done, 1)
            pe.wait_ge(pv_lo, HEADS)

            for n in range(4):
                if n == 0:
                    reduce_mod(32, True)
                    multiply(xhi, xlo, (2, 3), 4, 0)
                else:
                    pe.wait_ge(h_added, c.at("ha", 1))
                    multiply(xhi, xlo, range(4), 4, n % 2)
                c.add("ha")
            pe.wait_ge(u_done, 2 * T)

            def reduce_kind(kind):
                reduce_mod(32 if kind == SC1 else 16, kind == SC1)

            def mlp_chunk(first=False):
                for j in range(8):
                    pair = j % 2
                    if j < 2:
                        pe.wait_ge(h_added, c.at("ha", 1 + j))
                    elif j < 6:
                        pe.wait_ge(blk_half, c.at("half", j - 1))
                    else:
                        pe.wait_ge(h_added, c.at("ha", 2 + j - 5))
                    if first and j == 0:
                        opening(u_mlp, 0)
                        continue
                    hi, lo = (xhi, xlo) if j < 4 else (ahi, alo)
                    for kg in range(3):
                        multiply(hi, lo, (kg,), 4, pair)
                        if kg == 1 and 1 <= j <= 4:
                            pe.wait_ge(blk_ready, c.at("blk", j))
                            turn_rows(blk, 2)
                        if 4 * j + kg in MLP_REDUCED:
                            reduce_kind(MLP_REDUCED[4 * j + kg])
                    if j == 4:
                        pe.wait_ge(tp_free, c.at("q", 2))
                    multiply(hi, lo, (3,), 4, pair)
                    if 4 * j + 3 in MLP_REDUCED:
                        reduce_kind(MLP_REDUCED[4 * j + 3])
                c.add("ha", 4)
                c.add("half", 4)
                c.add("blk", 4)

            mlp_chunk(True)
            with c.loop(pe, MLP_CHUNKS, 1, g=32, q=8, ma=80, ha=4, half=4, blk=4):
                mlp_chunk()

            def evacuated(name, p):
                if p and name in ("cx0", "cx1"):
                    pe.wait_ge(blk_ready, 4 * MLP_CHUNKS + 1 + int(name[2]))
                else:
                    pe.wait_ge(in_set, IN_SET[p][name])

            def turn_conv(half, pr):
                pe.wait_ge(blk_ready, 4 * MLP_CHUNKS + 1 + half)
                pe.wait_ge(in_set, IN_SET[1]["cb1" if half else "cb0"])
                turn_rows(blk, 1, pr)
                turn_rows(blk2, 1, pr)

            def step(kind, p, a, b):
                q = c.slot("q", 2)
                if kind == "conv":
                    turn_conv(a, b)
                elif kind == "z":
                    pe.wait_ge(in_set, IN_SET[p]["l"])
                    pe.wait_ge(pool_set, 2)
                    pe.wait_ge(wg_in, 16)
                    pe.wait_ge(tp_free, c.at("q", 1))
                    pe.matmul(tp[:, q, :], lrankT[0:RANK2 + 1, a * P:(a + 1) * P], wg[0:RANK2 + 1, b, :], start=True, stop=True).then_inc(tp_ready, 1)
                    c.add("q")
                elif kind == "suffix":
                    pe.wait_ge(tp_free, c.at("q", 2 if a == b == 0 else 1))
                    pe.matmul(tp[:, q, :], after[b], la[:, a, b], start=True, stop=True).then_inc(tp_ready, 1)
                    c.add("q")
                elif kind == "cum":
                    hd = a
                    if hd == 0:
                        pe.wait_ge(tp_free, c.at("q", 2))
                    if p or hd:
                        pe.wait_ge(cum_exp, hd if p == 0 else GH + 2 * hd)
                    for d in range(2):
                        for t in range(T):
                            last = pe.matmul(m0[:, d * S + t * P:d * S + (t + 1) * P], la[:, t, d, hd * DK:(hd + 1) * DK],
                                             tri[d], start=True, stop=True)
                    last.then_inc(cum_done, 1)
                elif kind == "turn":
                    hd = a
                    pe.wait_ge(in_set, IN_SET[p]["q"])
                    pe.wait_ge(tp_free, c.at("q", 1))
                    for w, src in ((0, gq), (1, gk)):
                        for t in range(T):
                            last = pe.transpose(tp[:, q, w * S + t * P:w * S + (t + 1) * P],
                                                src[:, t, hd * DK:(hd + 1) * DK], ident)
                    last.then_inc(tp_ready, 1)
                    c.add("q")
                elif kind == "scores":
                    pe.wait_ge(qe_done, 4 * (a + 1))
                    if a:
                        pe.wait_ge(gsc_kept, 4 * a)
                    else:
                        pe.wait_ge(mod_set, 32)
                    for d in range(2):
                        for t in range(T):
                            last = pe.matmul(m1[:, (2 * d + t) * P:(2 * d + t + 1) * P], ke[:, d, t * P:(t + 1) * P],
                                             qe[:, d, t * P:(t + 1) * P], start=True, stop=True)
                    last.then_inc(gsc_done, 1)
                elif kind == "state":
                    hd, d = a, b
                    pe.wait_ge(in_set, IN_SET[p]["v0" if hd < 2 else "v1"])
                    pe.wait_ge(tp_free, c.at("q", 2))
                    for bank in range(2):
                        for ck in (bank, bank + 2):
                            if p and ck == ORDER[d][-1]:
                                continue
                            rows = slice(bank * CH, (bank + 1) * CH)
                            last = pe.matmul(tp[:, (q + bank) % 2, (ck // 2) * DV:(ck // 2 + 1) * DV],
                                             kdec[rows, ck // 2, d, hd * DK:(hd + 1) * DK],
                                             gv[rows, ck // 2, hd * DV:(hd + 1) * DV], start=True, stop=True)
                        last.then_inc(tp_ready, 1)
                    c.add("q", 2)
                elif kind == "out":
                    hd = a
                    pe.wait_ge(gsc_kept, 4 * (hd + 1))
                    pe.wait_ge(state_step, STATE_STEPS[0] * GH + STATE_STEPS[1] * (hd + 1))
                    pe.wait_ge(tp_free, c.at("q", 1))
                    for t in range(T):
                        for d in range(2):
                            pe.matmul(tp[:, q, t * DV:(t + 1) * DV], sc[:, d, t, :], gv[:, t, hd * DV:(hd + 1) * DV],
                                      start=(d == 0), stop=False)
                        for d in range(2):
                            for half in range(2):
                                ck = 2 * t + half
                                state = states[:, d, hd, :] if ck == ORDER[d][0] else gst[:, d, ck, :]
                                last = pe.matmul(tp[half * CH:(half + 1) * CH, q, t * DV:(t + 1) * DV],
                                                 qe[:, d, ck * CH:(ck + 1) * CH], state, start=False, stop=(d == 1))
                    last.then_inc(tp_ready, 1)
                    c.add("q")

            def evacuated(name, p):
                if name in ("cx0", "cx1"):
                    pe.wait_ge(blk_ready, 4 * MLP_CHUNKS + 1 + int(name[2]))
                else:
                    pe.wait_ge(in_set, IN_SET[p][name])

            def in_blocks(names, b0, p, rows):
                for n, name in enumerate(names):
                    pair = (b0 + n) % 2
                    if n >= 2:
                        evacuated(names[n - 2], p)
                    elif p:
                        evacuated(C_IN[len(C_IN) - 2 + n], 0)
                    else:
                        pe.wait_ge(h_added, H_MLP - 1 + n)
                    which, part = MOD_PAIRS[p].get(name, (None, 0))
                    if n == 0:
                        opening(rows, pair)
                    for kg in range(2 if name == "l" else 4):
                        if name == "l":
                            multiply_rank(kg, pair)
                        elif n:
                            multiply(xhi, xlo, (kg,), 4, pair)
                        if n or kg == 3:
                            for st in BESIDE[p].get((name, kg), ()):
                                step(*st)
                    if part:
                        reduce_mod(16, False)

            pe.wait_ge(u_done, 3 * T)
            in_blocks(C_IN, 44, 0, u_g)
            pe.wait_ge(u_done, 5 * T)
            in_blocks(X_IN, 48, 1, h)

            def gate_columns(which):
                for b in range(4):
                    q = c.slot("q", 2)
                    pe.wait_ge(tp_free, c.at("q", 1))
                    for j in range(4):
                        col = (GT2 if which else GT1) * KT + 4 * b + j
                        last = pe.matmul(tp[:, q, j * P:(j + 1) * P], modT[:, 0, col:col + 1].broadcast_to([P, P]), ident,
                                         start=True, stop=True)
                    last.then_inc(tp_ready, 1)
                    c.add("q")

            step("out", 1, GH - 1, 0)
            for n in range(2):
                pe.wait_ge(in_set, IN_SET[1]["g0" if n else "g1"])
                for half in range(2):
                    if n == 0:
                        pe.wait_ge(conv_lo, half + 1)
                    multiply(xhi, xlo, (TILED[half],), 4, n, order=TILED)
            pe.wait_ge(o_gated, T * GH)
            turn_rows(o_all, 4)
            pe.wait_ge(mod_set, 32)
            for n in range(2):
                for kg in TILED[2:4]:
                    if n == 0:
                        gate_columns(kg)
                    multiply(xhi, xlo, (kg,), 4, n, order=TILED)
                c.add("ha")
            for n in range(2, 4):
                pe.wait_ge(h_added, c.at("ha", 1))
                multiply(xhi, xlo, TILED, 4, n % 2, order=TILED)
                c.add("ha")
            pe.wait_ge(u_done, 6 * T)
            c.n["half"] = 4 * MLP_CHUNKS
            c.n["blk"] = 4 * MLP_CHUNKS + 2

            def ffn(blocks, first=False):
                for j in range(blocks):
                    if j:
                        pe.wait_ge(blk_half, c.at("half", j))
                    else:
                        pe.wait_ge(h_scaled, c.at("hs", -1))
                    if first and j == 0:
                        opening(u_ffn, 0)
                    else:
                        multiply(xhi, xlo, range(2), 4, 0)
                        if j:
                            pe.wait_ge(blk_ready, c.at("blk", j))
                            turn_rows(blk, 2)
                        multiply(xhi, xlo, (2, 3), 4, 0)
                    if not j:
                        pe.wait_ge(h_scaled, c.at("hs"))
                    multiply(xhi, xlo, range(4), 4, 1)
                for n in range(4):
                    if n == 0:
                        pe.wait_ge(blk_half, c.at("half", blocks))
                    elif n >= 2:
                        pe.wait_ge(h_scaled, c.at("hs", n - 1))
                    multiply(bhi, blo, range(2), blocks, n % 2)
                    if n == 0:
                        pe.wait_ge(blk_ready, c.at("blk", blocks))
                        turn_rows(blk, 2)
                    for kg in range(2, blocks):
                        if n == 0 and kg == blocks - 1:
                            pe.wait_ge(tp_free, c.at("q", 2))
                        multiply(bhi, blo, (kg,), blocks, n % 2)
                c.add("half", blocks)
                c.add("blk", blocks)
                c.add("hs", 4)

            c.n["hs"] = 4
            ffn(4, True)
            with c.loop(pe, 2, 1, g=48, q=8, half=4, blk=4, hs=4):
                ffn(4)
            ffn(LAST_CHUNK)


def kernel(**inputs):
    import concourse.bacc as bacc
    from concourse.bass_utils import run_bass_kernel_spmd

    nc = bacc.Bacc("TRN2", target_bir_lowering=False, num_devices=1)
    a = {k: np.asarray(v) for k, v in inputs.items()}

    vectors = np.zeros((P, 3, P), np.float32)
    rows = [a["norm_mix_g"], a["norm_mlp_g"], a["norm1_g_2"], a["norm2_g_2"], a["c_2"], a["c_ctx_2"]]
    vectors[0:96, 0] = np.concatenate([r.reshape(KT, P) for r in rows])
    vectors[0:96, 1] = a["b_mod_2"].reshape(6 * KT, P)
    vectors[0:24, 2] = a["conv_w_2"].reshape(24, P)
    vectors[24:26, 2] = a["gla_norm_g_2"].reshape(2, P)
    gates_w = np.zeros((P, 2, GH * DK), np.float32)
    for d, n in enumerate(("f", "b")):
        gates_w[16 * d:16 * d + 16, d] = a[f"w_gate_{n}_2"][0]
        gates_w[RANK2, d] = a[f"b_gate_{n}_2"][0]

    j, i = np.mgrid[0:P, 0:P]
    same = j // CH == i // CH
    tables = np.stack([np.eye(P), (same & (j <= i)) / 16.0, (same & (j >= i)) / 16.0,
                       (same & (j > i)) / 16.0, (same & (j < i)) / 16.0,
                       same & (j <= i), same & (j >= i)], axis=1).astype(np.float32)
    ang = 2 * np.pi * (np.outer(np.arange(S), np.arange(S)) % S) / S
    dft = np.concatenate([np.cos(ang), np.sin(ang), -np.sin(ang)], axis=1) / np.sqrt(S)
    fourier_tables = np.ascontiguousarray(dft.reshape(2, P, 3 * S).transpose(1, 0, 2)).astype(np.float32)
    dist = np.abs(np.arange(S)[:, None] - np.arange(S)[None, :])
    seen = sum(((dist % dil == 0) & (dist // dil <= (window // 2) // dil)).astype(int)
               for window, dil in ((128, 1), (512, 4), (2048, 16)))
    attn = np.stack([np.where(seen > 0, -dist, -1e30), seen])
    attn_tables = np.ascontiguousarray(attn.reshape(2, T, P, S).transpose(2, 0, 1, 3).reshape(P, 2, T * S)).astype(np.float32)

    arrays = {
        "x": a["x"][0], "ctx_in": a["ctx_2"][0], "w_in": a["w_in"][0], "w_fourier": a["w_fourier"][0],
        "w_out": a["w_out"][0], "w_up": a["w_up"][0], "w_down": a["w_down"][0], "w_mod": a["w_mod_2"][0],
        "w_in2": a["w_in_2"][0], "w_out2": a["w_out_2"][0], "w_gate": a["w_ffn_gate_2"][0],
        "w_up2": a["w_ffn_up_2"][0], "w_down2": a["w_ffn_down_2"][0], "vectors": vectors,
        "gates_w": gates_w, "mid_g": a["norm_final_g"], "final_g": a["final_g_2"], "tables": tables,
        "fourier_tables": fourier_tables, "attn_tables": attn_tables,
    }
    args = {}
    for name, v in arrays.items():
        arrays[name] = np.ascontiguousarray(v)
        args[name] = nc.dram_tensor(name, arrays[name].shape, mybir.dt.from_np(arrays[name].dtype), kind="ExternalInput").ap()
    args["out"] = nc.dram_tensor("out", [S, D], F32, kind="ExternalOutput").ap()
    two_blocks(nc, **args)
    r = run_bass_kernel_spmd(nc, [arrays], core_ids=[0])
    return r.results[0]["out"].reshape(1, S, D)
```
